# Optimizing a Trainium2 kernel written in Bass

```python
import math
import jax, jax.numpy as jnp
from jax import lax
import numpy as np

D_MODEL = 4096
BATCH = 1
SEQ = 256
DEPTH = 1

MIX_WIDTH = D_MODEL
BRANCH_WIDTH = MIX_WIDTH // 4
HEAD_DIM = 128
N_FOX_HEADS = BRANCH_WIDTH // HEAD_DIM
N_SB_HEADS = BRANCH_WIDTH // HEAD_DIM
SSM_GROUP = 16
N_SSM_GROUPS = BRANCH_WIDTH // SSM_GROUP
SSM_STATE = 64
LRU_BLOCKS = 16
LRU_BLOCK = BRANCH_WIDTH // LRU_BLOCKS
CONV_WIDTH = 4
LRU_C = 8.0
Q_BLOCK = 128
RMS_EPS = 1e-6
N_IN = 12 * BRANCH_WIDTH + N_FOX_HEADS

kernel_name = "hybrid_fox_sb_s5_rglru_parallel"

def rmsnorm(x, g):
    xf = x.astype(jnp.float32)
    y = xf * lax.rsqrt(jnp.mean(xf * xf, axis=-1, keepdims=True) + RMS_EPS)
    return (y * g.astype(jnp.float32)).astype(x.dtype)

def _split_heads(t, n_heads):
    b, l, _ = t.shape
    return t.reshape(b, l, n_heads, HEAD_DIM).transpose(0, 2, 1, 3)

def _merge_heads(t):
    b, h, l, d = t.shape
    return t.transpose(0, 2, 1, 3).reshape(b, l, h * d)

def _to_blocks(t):
    b, h, l = t.shape[:3]
    t = t.reshape((b, h, l // Q_BLOCK, Q_BLOCK) + t.shape[3:])
    return jnp.moveaxis(t, 2, 0)

def forgetting_attention(q, k, v, log_f):
    b, h, l, d = q.shape
    nb = l // Q_BLOCK
    cum_f = jnp.cumsum(log_f, axis=-1)
    k_pos = jnp.arange(l)
    scale = d ** -0.5

    def one_block(args):
        q_blk, f_blk, bi = args
        q_pos = bi * Q_BLOCK + jnp.arange(Q_BLOCK)
        s = jnp.einsum('bhqd,bhkd->bhqk', q_blk, k).astype(jnp.float32) * scale
        s = s + f_blk[..., :, None] - cum_f[..., None, :]
        mask = k_pos[None, :] <= q_pos[:, None]
        p = jax.nn.softmax(jnp.where(mask, s, -jnp.inf), axis=-1)
        return jnp.einsum('bhqk,bhkd->bhqd', p.astype(v.dtype), v)

    out = lax.map(one_block, (_to_blocks(q), _to_blocks(cum_f), jnp.arange(nb)))
    return jnp.moveaxis(out, 0, 2).reshape(b, h, l, d)

def stick_breaking_attention(q, k, v):
    b, h, l, d = q.shape
    nb = l // Q_BLOCK
    k_pos = jnp.arange(l)
    scale = d ** -0.5

    def one_block(args):
        q_blk, bi = args
        q_pos = bi * Q_BLOCK + jnp.arange(Q_BLOCK)
        z = jnp.einsum('bhqd,bhkd->bhqk', q_blk, k).astype(jnp.float32) * scale
        mask = k_pos[None, :] < q_pos[:, None]
        log_keep = jnp.where(mask, jax.nn.log_sigmoid(-z), 0.0)
        after = lax.cumsum(log_keep, axis=3, reverse=True) - log_keep
        w = jnp.where(mask, jnp.exp(jax.nn.log_sigmoid(z) + after), 0.0)
        return jnp.einsum('bhqk,bhkd->bhqd', w.astype(v.dtype), v)

    out = lax.map(one_block, (_to_blocks(q), jnp.arange(nb)))
    return jnp.moveaxis(out, 0, 2).reshape(b, h, l, d)

def _linear_scan(a, bx):
    def combine(left, right):
        a_l, b_l = left
        a_r, b_r = right
        return a_r * a_l, a_r * b_l + b_r
    _, hs = lax.associative_scan(combine, (a, bx), axis=1)
    return hs

def s5_mixer(u, a_re, a_im, log_dt, b_re, b_im, c_re, c_im, d_skip, w_glu, b_glu):
    bsz, l, w = u.shape
    uf = u.astype(jnp.float32).reshape(bsz, l, N_SSM_GROUPS, SSM_GROUP)
    dt = jnp.exp(log_dt.astype(jnp.float32))[:, None]
    lam = lax.complex(a_re.astype(jnp.float32), a_im.astype(jnp.float32))
    lam_bar = jnp.exp(lam * dt)
    b_c = lax.complex(b_re.astype(jnp.float32), b_im.astype(jnp.float32))
    b_bar = ((lam_bar - 1.0) / lam)[..., None] * b_c
    bu = jnp.einsum('gph,blgh->blgp', b_bar, uf.astype(jnp.complex64))
    states = _linear_scan(jnp.broadcast_to(lam_bar, bu.shape), bu)
    c_c = lax.complex(c_re.astype(jnp.float32), c_im.astype(jnp.float32))
    y = jnp.einsum('ghp,blgp->blgh', c_c, states).real
    y = y + d_skip.astype(jnp.float32).reshape(N_SSM_GROUPS, SSM_GROUP) * uf
    y = jax.nn.gelu(y.reshape(bsz, l, w))
    y = y * jax.nn.sigmoid(y @ w_glu.astype(jnp.float32) + b_glu.astype(jnp.float32))
    return y.astype(u.dtype)

def rglru_mixer(xb, conv_w, conv_b, w_r, b_r, w_i, b_i, lam):
    bsz, l, w = xb.shape
    xc = lax.conv_general_dilated(
        xb, conv_w[:, None, :], window_strides=(1,), padding=[(CONV_WIDTH - 1, 0)],
        dimension_numbers=('NWC', 'WIO', 'NWC'), feature_group_count=w) + conv_b
    xf = xc.astype(jnp.float32)
    xblk = xf.reshape(bsz, l, LRU_BLOCKS, LRU_BLOCK)
    r = jax.nn.sigmoid(jnp.einsum('blni,nio->blno', xblk, w_r.astype(jnp.float32)).reshape(bsz, l, w)
                       + b_r.astype(jnp.float32))
    i = jax.nn.sigmoid(jnp.einsum('blni,nio->blno', xblk, w_i.astype(jnp.float32)).reshape(bsz, l, w)
                       + b_i.astype(jnp.float32))
    log_a = LRU_C * r * jax.nn.log_sigmoid(lam.astype(jnp.float32))
    a = jnp.exp(log_a)
    bx = jnp.sqrt(-jnp.expm1(2.0 * log_a)) * (i * xf)
    return _linear_scan(a, bx).astype(xb.dtype)

def hybrid_layer(h, g_pre, w_in, b_forget, ssm_a_re, ssm_a_im, ssm_log_dt, ssm_b_re, ssm_b_im,
                 ssm_c_re, ssm_c_im, ssm_d, w_glu, b_glu, conv_w, conv_b, w_rgate, b_rgate,
                 w_igate, b_igate, lru_lambda, w_out, g_post):
    bw = BRANCH_WIDTH
    u = rmsnorm(h, g_pre)
    p = u @ w_in
    sizes = [bw] * 4 + [N_FOX_HEADS] + [bw] * 4 + [bw] * 2 + [bw] * 2
    (fq, fk, fv, fgate, f_logit, sq, sk, sv, sgate,
     su, ssm_gate, lx, lru_gate) = jnp.split(p, np.cumsum(sizes)[:-1].tolist(), axis=-1)

    log_f = jax.nn.log_sigmoid(f_logit.astype(jnp.float32) + b_forget.astype(jnp.float32))
    o_fox = forgetting_attention(_split_heads(fq, N_FOX_HEADS), _split_heads(fk, N_FOX_HEADS),
                                 _split_heads(fv, N_FOX_HEADS), log_f.transpose(0, 2, 1))
    o_fox = _merge_heads(o_fox) * jax.nn.silu(fgate)

    o_sb = stick_breaking_attention(_split_heads(sq, N_SB_HEADS), _split_heads(sk, N_SB_HEADS),
                                    _split_heads(sv, N_SB_HEADS))
    o_sb = _merge_heads(o_sb) * jax.nn.silu(sgate)

    o_ssm = s5_mixer(su, ssm_a_re, ssm_a_im, ssm_log_dt, ssm_b_re, ssm_b_im, ssm_c_re, ssm_c_im,
                     ssm_d, w_glu, b_glu) * jax.nn.silu(ssm_gate)

    o_lru = rglru_mixer(lx, conv_w, conv_b, w_rgate, b_rgate, w_igate, b_igate,
                        lru_lambda) * jax.nn.silu(lru_gate)

    mixed = jnp.concatenate([o_fox, o_sb, o_ssm, o_lru], axis=-1) @ w_out
    return h + rmsnorm(mixed, g_post)

def setup_inputs(seed: int = 0) -> dict:
    key = jax.random.key(seed)
    ks = jax.random.split(key, 24)
    f32 = jnp.float32
    bw, g, pst, hg = BRANCH_WIDTH, N_SSM_GROUPS, SSM_STATE, SSM_GROUP
    nrm = lambda k, shape, s: jax.random.normal(k, shape, f32) * s
    x = jax.random.normal(ks[0], (BATCH, SEQ, D_MODEL), f32)
    g_pre = 1.0 + nrm(ks[1], (DEPTH, D_MODEL), 0.02)
    w_in = nrm(ks[2], (DEPTH, D_MODEL, N_IN), D_MODEL ** -0.5)
    b_forget = jax.random.uniform(ks[3], (DEPTH, N_FOX_HEADS), f32, 1.0, 6.0)
    ssm_a_re = -0.5 + nrm(ks[4], (DEPTH, g, pst), 0.01)
    ssm_a_im = math.pi * jnp.arange(pst, dtype=f32) + nrm(ks[5], (DEPTH, g, pst), 0.01)
    ssm_log_dt = jax.random.uniform(ks[6], (DEPTH, g), f32, math.log(1e-3), math.log(1e-1))
    ssm_b_re = nrm(ks[7], (DEPTH, g, pst, hg), (2 * hg) ** -0.5)
    ssm_b_im = nrm(ks[8], (DEPTH, g, pst, hg), (2 * hg) ** -0.5)
    ssm_c_re = nrm(ks[9], (DEPTH, g, hg, pst), (2 * pst) ** -0.5)
    ssm_c_im = nrm(ks[10], (DEPTH, g, hg, pst), (2 * pst) ** -0.5)
    ssm_d = nrm(ks[11], (DEPTH, bw), 1.0)
    w_glu = nrm(ks[12], (DEPTH, bw, bw), bw ** -0.5)
    b_glu = nrm(ks[13], (DEPTH, bw), 0.02)
    conv_w = nrm(ks[14], (DEPTH, CONV_WIDTH, bw), CONV_WIDTH ** -0.5)
    conv_b = nrm(ks[15], (DEPTH, bw), 0.02)
    w_rgate = nrm(ks[16], (DEPTH, LRU_BLOCKS, LRU_BLOCK, LRU_BLOCK), LRU_BLOCK ** -0.5)
    b_rgate = nrm(ks[17], (DEPTH, bw), 0.1)
    w_igate = nrm(ks[18], (DEPTH, LRU_BLOCKS, LRU_BLOCK, LRU_BLOCK), LRU_BLOCK ** -0.5)
    b_igate = nrm(ks[19], (DEPTH, bw), 0.1)
    a_c = jax.random.uniform(ks[20], (DEPTH, bw), f32, 0.9, 0.999)
    s = a_c ** (1.0 / LRU_C)
    lru_lambda = jnp.log(s) - jnp.log1p(-s)
    w_out = nrm(ks[21], (DEPTH, MIX_WIDTH, D_MODEL), MIX_WIDTH ** -0.5)
    g_post = 1.0 + nrm(ks[22], (DEPTH, D_MODEL), 0.02)
    return {"x": x, "g_pre": g_pre, "w_in": w_in, "b_forget": b_forget,
            "ssm_a_re": ssm_a_re, "ssm_a_im": ssm_a_im, "ssm_log_dt": ssm_log_dt,
            "ssm_b_re": ssm_b_re, "ssm_b_im": ssm_b_im, "ssm_c_re": ssm_c_re, "ssm_c_im": ssm_c_im,
            "ssm_d": ssm_d, "w_glu": w_glu, "b_glu": b_glu, "conv_w": conv_w, "conv_b": conv_b,
            "w_rgate": w_rgate, "b_rgate": b_rgate, "w_igate": w_igate, "b_igate": b_igate,
            "lru_lambda": lru_lambda, "w_out": w_out, "g_post": g_post}

def reference(x, g_pre, w_in, b_forget, ssm_a_re, ssm_a_im, ssm_log_dt, ssm_b_re, ssm_b_im,
              ssm_c_re, ssm_c_im, ssm_d, w_glu, b_glu, conv_w, conv_b, w_rgate, b_rgate,
              w_igate, b_igate, lru_lambda, w_out, g_post):
    h = x
    for layer in range(DEPTH):
        h = hybrid_layer(h, g_pre[layer], w_in[layer], b_forget[layer], ssm_a_re[layer],
                         ssm_a_im[layer], ssm_log_dt[layer], ssm_b_re[layer], ssm_b_im[layer],
                         ssm_c_re[layer], ssm_c_im[layer], ssm_d[layer], w_glu[layer], b_glu[layer],
                         conv_w[layer], conv_b[layer], w_rgate[layer], b_rgate[layer],
                         w_igate[layer], b_igate[layer], lru_lambda[layer], w_out[layer],
                         g_post[layer])
    return h


_drawn_inputs = setup_inputs


def setup_inputs(seed=0):
    import zlib

    import numpy as np

    out = dict(_drawn_inputs(seed))
    spreads = {}
    factors = {'ssm_a_re': 64.0,
     'ssm_a_im': 31.504,
     'ssm_log_dt': 32.024,
     'ssm_b_re': 44.536,
     'ssm_b_im': 44.48,
     'ssm_c_re': 44.76,
     'ssm_c_im': 45.24,
     'b_glu': 8.0,
     'b_rgate': 6.531,
     'b_igate': 3.875,
     'g_post': 11.743}
    for name, (base, spread) in spreads.items():
        noise = np.random.default_rng([zlib.crc32(name.encode()), seed]).standard_normal(out[name].shape)
        drawn = base * np.exp(spread * noise) if base else spread * noise
        out[name] = __import__('jax').numpy.asarray(drawn.astype(out[name].dtype))
    for name, factor in factors.items():
        out[name] = (out[name] * factor).astype(out[name].dtype)
    return out
```

```python
import math
from contextlib import ExitStack

import concourse.bass as bass
from concourse import mybir

F32 = mybir.dt.float32
F32R = mybir.dt.float32r
BF16 = mybir.dt.bfloat16
ACT = mybir.ActivationFunctionType
ALU = mybir.AluOpType
AX = mybir.AxisListType

P = 128
D = 4096
T = 256
TT = T // P
NK = D // P
BW = D // 4
FT = BW // P
BLK = 512
JB = BLK // P
KC = 2
CH = NK // KC
CW = KC * BLK
RING = 4
LEAD = RING - 1
STATE, HG = 64, 16
SJ = 4
N_IN_BLOCKS = 24
N_OUT_BLOCKS = D // BLK
N_BLOCKS = N_IN_BLOCKS + N_OUT_BLOCKS
B_SRC, B_QK, B_V, B_G1, B_G2, B_OUT = 0, 4, 12, 16, 20, 24
EPS = 1e-6
QK_SCALE = float(P) ** -0.25
LRU_C = 8.0
ROUND = 1.5 * 2.0 ** 23
TWO_PI = 6.283185
PI_1 = 6.28125
PI_2 = 0.0019350051879882812
PI_3 = 2.0 * math.pi - 6.28125 - 0.0019350051879882812
NEG = -1.0e30
SSM0, LRU0, FOX0, SB0, KEY0 = 0, FT, 2 * FT, 3 * FT, 4 * FT
PC = {}
_at = 0
for _name, _n in (("g_pre", NK), ("a_re", 32), ("a_im", 32), ("log_dt", 32), ("b_forget", TT * FT),
                  ("ssm_d", FT), ("lam", FT), ("lru", FT * 9)):
    PC[_name] = (_at, _at + _n)
    _at += _n
NPAR = _at
TAP0, CONV_B, B_R, B_I, LOG_A, B_GLU = 0, 4, 5, 6, 7, 8


def hybrid_trunk(nc, x, par, bt, ct, wfg, wglu, wri, gpost, wall, out):
    ctx = ExitStack()
    with ctx:
        def sb(name, shape, dt=F32):
            return ctx.enter_context(nc.sbuf_tensor(name, shape, dt))

        def sem(name):
            return ctx.enter_context(nc.semaphore(name))

        acts = sb("acts", [P, NK, 2 * T], F32R)
        w_raw = sb("w_raw", [P, RING, CW])
        w_hi = sb("w_hi", [P, RING, CW], F32R)
        w_lo = sb("w_lo", [P, RING, CW], F32R)
        br = sb("br", [P, 6 * FT, T])
        vals = sb("vals", [P, TT, 2 * BW])
        cross = sb("cross", [P, JB, T])
        scr = sb("scr", [P, 5120])
        pars = sb("pars", [P, NPAR])
        s5par = sb("s5par", [P, FT, 5 * SJ])
        small = sb("small", [P, 178])
        wf = sb("wf", [P, NK, 2 * FT], F32R)
        logf = sb("logf", [P, FT, TT])
        later = sb("later", [P, 2 * P])
        upto = sb("upto", [P, P])
        ident = sb("ident", [P, P])
        ident_b = sb("ident_b", [P, P], BF16)
        causal_b = sb("causal_b", [P, P], BF16)
        strict_b = sb("strict_b", [P, P], BF16)

        main = ctx.enter_context(nc.psum_tensor("main", [P, 4, BLK], F32))
        side = ctx.enter_context(nc.psum_tensor("side", [P, 4, BLK], F32))

        x_rows = br[:, 0:32, :].rearrange("p (a k) t -> p a (k t)", a=TT)
        mixed = br[:, 0:32, :].rearrange("p (a k) t -> p a (k t)", a=TT)
        g_rows = br[:, 32:48, :].rearrange("p k t -> p (k t)")
        x_late = [vals[:, :, :].rearrange("p a n -> p (a n)"), scr[:, 0:D]]
        wf_raw = scr[:, 0:256].rearrange("p (k n) -> p k n", k=NK)
        s5tmp = scr[:, 256:800].rearrange("p (n f) -> p n f", n=17)
        vflat = vals[:, :, :].rearrange("p a n -> p (a n)")
        s5_m1, s5_m2, s5_g = vflat[:, 0:512], vflat[:, 512:1024], vflat[:, 1024:1536]
        s5_h = [vflat[:, 1536:2048], vflat[:, 2048:2560]]
        s5_sin = [vflat[:, 2560:3072], vflat[:, 3072:3584]]
        s5_cos = [vflat[:, 3584:3840], vflat[:, 3840:4096]]
        steps_t = scr[:, 3328:3328 + T]
        s5_bt = scr[:, 0:1024].rearrange("p (j r s) -> p j r s", j=SJ, r=2)
        s5_ct = scr[:, 1024:1280].rearrange("p (j r h) -> p j r h", j=SJ, r=2)
        s5_cp = scr[:, 1280:1536].rearrange("p (j r h) -> p j r h", j=SJ, r=2)
        s5_u = scr[:, 1536:1792]
        s5_a, s5_k, s5_f, s5_q = (scr[:, 1792 + T * n:1792 + T * (n + 1)] for n in range(4))
        s5_c = [scr[:, 2816 + 128 * n:2816 + 128 * (n + 1)].rearrange("p (j h) -> p j h", j=SJ)
                for n in range(4)]
        glu_w = scr[:, 0:1024].rearrange("p (k n) -> p k n", k=FT)
        lru_w = scr[:, 1024:1280].rearrange("p (r n) -> p r n", r=2)
        lru_x, lru_xc = scr[:, 1280:1536], scr[:, 1536:1792]
        lru_ri = scr[:, 1792:2304]
        lru_a, lru_th, lru_s = scr[:, 2304:2560], scr[:, 2560:2816], scr[:, 2816:3072]
        glu_z = scr[:, 3072:5120].rearrange("p (n t) -> p n t", n=FT)
        at_q = scr[:, 0:256]
        at_v = scr[:, 256:512].rearrange("p (a d) -> p a d", a=TT)
        at_dec = scr[:, 512:896].rearrange("p (n t) -> p n t", n=3)
        at_p, at_pt = scr[:, 896:1280], scr[:, 1280:1664]
        at_e, at_sp, at_r = scr[:, 1664:2048], scr[:, 2048:2432], scr[:, 2432:2816]
        sumsq, ms, rs_a, rs_b, rstd = (small[:, 4 * n:4 * n + 4] for n in range(5))
        s5_now = small[:, 20:40]
        lru_now = small[:, 40:49]
        lf_now = small[:, 50:54]
        ones = later[:, 0:1].to_broadcast([P, T])
        row_max, row_sum, row_inv = small[:, 54:56], small[:, 56:58], small[:, 58:60]
        ss_new, ss_all = small[:, 60:62], small[:, 62:64]
        fl = small[:, 64:112].rearrange("p (a n) -> p a n", a=TT)
        fl_z, fl_e = (small[:, 112 + 16 * n:128 + 16 * n].rearrange("p (a n) -> p a n", a=TT)
                      for n in range(2))
        log_a = [small[:, 144 + 8 * n:152 + 8 * n] for n in range(4)]

        def col(name, n=None):
            a, b = PC[name]
            return pars[:, a:b] if n is None else pars[:, a + n:a + n + 1]

        def xt_bank(k):
            return (side if k % 8 < 4 else main)[:, k % 4, 0:T]

        lru_par = col("lru").rearrange("p (f n) -> p f n", f=FT)
        halves = [(a, h) for a in range(TT) for h in range(2)]
        HW = D // 2

        x_in = [sem(f"x_in{n}") for n in range(4)]
        par_in, wf_in = sem("par_in"), sem("wf_in")
        raw_in = [sem(f"raw_in{n}") for n in range(RING)]
        hi_ready, lo_ready = sem("hi_ready"), sem("lo_ready")
        w_used = sem("w_used")
        fm_done, tm_done = sem("fm_done"), sem("tm_done")
        bank_cross = sem("bank_cross")
        bank_free = sem("bank_free")
        v_free = sem("v_free")
        squared, rms_act, rms_dve = sem("squared"), sem("rms_act"), sem("rms_dve")
        xt_done, u_hi, u_lo = sem("xt_done"), sem("u_hi"), sem("u_lo")
        consts, const_steps = sem("consts"), sem("const_steps")
        pa, pd = sem("pa"), sem("pd")
        wf_hi, wf_lo = sem("wf_hi"), sem("wf_lo")
        fl_mm, fl_act, fl_dve = sem("fl_mm"), sem("fl_act"), sem("fl_dve")
        bt_in, ct_in, p5_ready, su_ready = sem("bt_in"), sem("ct_in"), sem("p5_ready"), sem("su_ready")
        s5_tab, s5_frac, s5_trig, s5_cosd = sem("s5_tab"), sem("s5_frac"), sem("s5_trig"), sem("s5_cosd")
        s5_cq, s5_cprime = sem("s5_cq"), sem("s5_cprime")
        s5_bmm, s5_cmm, s5_dve, s5_done, s5_y = (sem(n) for n in
                                                 ("s5_bmm", "s5_cmm", "s5_dve", "s5_done", "s5_y"))
        gelu_done, wg_in, wr_in = sem("gelu_done"), sem("wg_in"), sem("wr_in")
        lru_v, lru_mm, lru_act, lru_done = sem("lru_v"), sem("lru_mm"), sem("lru_act"), sem("lru_done")
        glu_mm, glu_sig, glu_applied = sem("glu_mm"), sem("glu_sig"), sem("glu_applied")
        lf_ready, dec_ready, qs_ready, vs_ready = (sem(n) for n in
                                                   ("lf_ready", "dec_ready", "qs_ready", "vs_ready"))
        at_scores, at_max, at_exp, at_inv, at_norm = (sem(n) for n in
                                                      ("at_scores", "at_max", "at_exp", "at_inv", "at_norm"))
        at_tr, at_ptd, at_out, at_o = sem("at_tr"), sem("at_ptd"), sem("at_out"), sem("at_o")
        sb_act, sb_dve = sem("sb_act"), sem("sb_dve")
        gate_silu, gate_used = sem("gate_silu"), sem("gate_used")
        mix_hi, mix_lo = sem("mix_hi"), sem("mix_lo")
        g_in, xl_in = sem("g_in"), [sem("xl_in0"), sem("xl_in1")]
        o_sq, o_mg, o_ss = sem("o_sq"), sem("o_mg"), sem("o_ss")
        fin_act, fin_dve, fin_sum, stored = (sem(n) for n in ("fin_act", "fin_dve", "fin_sum", "stored"))

        N_CONST = 8
        N_PD_S5, N_PD = 28, 28 + 16
        block = ctx.enter_context(nc.Block())

        @block.sync
        def _(sp):
            for n, (a, h) in enumerate(halves):
                sp.dma_start(x_rows[:, a, h * HW:(h + 1) * HW],
                             x[a * P:(a + 1) * P, h * HW:(h + 1) * HW]).then_inc(x_in[n], 16)

            def load(b, c):
                sp.dma_start(w_raw[:, c % RING, :],
                             wall[bass.ds(b, 1), :, c * CW:(c + 1) * CW].rearrange("b p n -> (b p) n")
                             ).then_inc(raw_in[c % RING], 16)

            for c in range(RING):
                load(0, c)
            with sp.Fori(0, N_BLOCKS - 1) as b:
                for c in range(CH):
                    sp.wait_ge(lo_ready, b * CH + c + 1)
                    load(b + (c + RING) // CH, (c + RING) % CH)
            for c in range(CH - RING):
                sp.wait_ge(lo_ready, (N_BLOCKS - 1) * CH + c + 1)
                load(N_BLOCKS - 1, c + RING)
            for n, (a, h) in enumerate(halves):
                sp.wait_ge(fin_sum, n + 1)
                sp.dma_start(out[a * P:(a + 1) * P, h * HW:(h + 1) * HW],
                             mixed[:, a, h * HW:(h + 1) * HW]).then_inc(stored, 16)
            sp.wait_ge(stored, 16 * len(halves))

        @block.tensor
        def _(pe):
            def chunk_fm(b, m, c):
                pe.wait_ge(lo_ready, b * CH + c + 1)
                s = c % RING
                for j in range(JB):
                    if c == 0:
                        pe.wait_ge(bank_free, m * JB + j + 1)
                    for kk in range(KC):
                        k, at = KC * c + kk, kk * BLK + j * P
                        pe.matmul(main[:, j, :], w_hi[:, s, at:at + P], acts[:, k, :],
                                  start=(k == 0), stop=False)
                        mm = pe.matmul(main[:, j, T:2 * T], w_lo[:, s, at:at + P], acts[:, k, 0:T],
                                       start=False, stop=(k == NK - 1))
                    if c == CH - 1 and j < JB - 1:
                        mm.then_inc(fm_done, 1)
                mm.then_inc(w_used, 1)

            def chunk_tm(b, c, free, mixed_parts=False):
                pe.wait_ge(lo_ready, b * CH + c + 1)
                if mixed_parts:
                    pe.wait_ge(mix_lo, KC * (c + 1))
                s = c % RING
                for a in range(TT):
                    if c == 0:
                        free(a)
                    for kk in range(KC):
                        k = KC * c + kk
                        u_h, u_l = acts[:, k, a * P:(a + 1) * P], acts[:, k, T + a * P:T + (a + 1) * P]
                        wh, wl = w_hi[:, s, kk * BLK:(kk + 1) * BLK], w_lo[:, s, kk * BLK:(kk + 1) * BLK]
                        pe.matmul(main[:, a, :], u_h, wh, start=(k == 0), stop=False)
                        pe.matmul(main[:, a, :], u_h, wl, start=False, stop=False)
                        mm = pe.matmul(main[:, a, :], u_l, wh, start=False, stop=(k == NK - 1))
                    if c == CH - 1 and a < TT - 1:
                        mm.then_inc(tm_done, 1)
                mm.then_inc(w_used, 1)

            pe.wait_ge(consts, N_CONST)
            pe.wait_ge(bank_free, 4)
            for k in range(NK):
                if k >= 8:
                    pe.wait_ge(u_lo, k - 7)
                for a in range(TT):
                    tr = pe.transpose(xt_bank(k)[:, a * P:(a + 1) * P], x_rows[:, a, k * P:(k + 1) * P],
                                      ident[:, :])
                tr.then_inc(xt_done, 1)
            pe.wait_ge(u_lo, NK)

            with pe.Fori(0, B_QK - B_SRC) as i:
                for c in range(CH):
                    chunk_fm(i, i, c)

            pe.wait_ge(wf_lo, 1)
            for a in range(TT):
                for k in range(NK):
                    pe.matmul(side[:, a, 0:2 * FT], acts[:, k, a * P:(a + 1) * P], wf[:, k, :],
                              start=(k == 0), stop=(k == NK - 1))
                    mm = pe.matmul(side[:, 2 + a, 0:FT], acts[:, k, T + a * P:T + (a + 1) * P],
                                   wf[:, k, 0:FT], start=(k == 0), stop=(k == NK - 1))
            mm.then_inc(fl_mm, 1)
            pe.wait_ge(fl_act, 2)

            with pe.Fori(0, B_V - B_QK) as i:
                for c in range(CH):
                    if c % 3 == 1 and c // 3 < SJ:
                        j = c // 3
                        if j == 0:
                            pe.wait_ge(su_ready, i + 1)
                            pe.wait_ge(bt_in, i * 16 + 16)
                        pe.wait_ge(s5_done, i * SJ + max(j - 1, 0))
                        for r in range(2):
                            mm = pe.matmul(side[:, j % 2, r * T:(r + 1) * T], s5_bt[:, j, r, :], s5_u[:, :],
                                           start=True, stop=True)
                        mm.then_inc(s5_bmm, 1)
                    if c % 3 == 0 and 2 <= c // 3:
                        j = c // 3 - 2
                        if j == 0:
                            pe.wait_ge(s5_cprime, i + 1)
                            pe.wait_ge(s5_y, i)
                        pe.wait_ge(s5_done, i * SJ + j + 1)
                        for r in range(2):
                            mm = pe.matmul(side[32 * j:32 * j + 32, 2, 0:T], s5_cp[:, j, r, :],
                                           s5_h[j % 2][:, r * T:(r + 1) * T], start=(r == 0), stop=(r == 1))
                        mm.then_inc(s5_cmm, 1)
                    chunk_fm(i + B_QK, i + B_QK, c)

            with pe.Fori(0, B_G1 - B_V) as i:
                def v_bank(a):
                    pe.wait_ge(bank_free, B_V * JB + 4)
                    pe.wait_ge(v_free, i * TT)

                for c in range(CH):
                    for a, at in ((0, 0), (1, 7)):
                        if c == at + 2:
                            pe.wait_ge(wr_in, i * 32 + 16 * (a + 1))
                            pe.wait_ge(lru_v, i * 18 + 9 * a + 6)
                            pe.wait_ge(lru_act, i * 12 + 6 * a)
                            for r in range(2):
                                mm = pe.matmul(side[:, 0, r * T:(r + 1) * T], lru_w[:, r, :], lru_xc[:, :],
                                               start=True, stop=True)
                            mm.then_inc(lru_mm, 1)
                        if c == at + 3:
                            pe.wait_ge(wg_in, i * 32 + 16 * (a + 1))
                            pe.wait_ge(gelu_done, FT)
                            pe.wait_ge(glu_sig, i * 2 + a)
                            for k in range(FT):
                                mm = pe.matmul(side[:, 1, 0:T], glu_w[:, k, :], br[:, SSM0 + k, :],
                                               start=(k == 0), stop=(k == FT - 1))
                            mm.then_inc(glu_mm, 1)
                    chunk_tm(i + B_V, c, v_bank)

            def transposes(h):
                pe.wait_ge(at_ptd, h)
                pe.transpose(side[:, 1, 0:P], at_p[:, 0:P], ident[:, :])
                pe.transpose(side[:, 1, P:2 * P], at_p[:, P:2 * P], ident[:, :])
                pe.transpose(side[:, 1, 2 * P:3 * P], at_p[:, 2 * P:3 * P], ident[:, :]).then_inc(at_tr, 1)

            def weighted_values(h):
                pe.wait_ge(at_ptd, h + 1)
                pe.wait_ge(vs_ready, h + 1)
                pe.wait_ge(at_o, h)
                pe.matmul(side[:, 2, 0:T], at_v[:, 0, :], at_pt[:, 0:T], start=True, stop=False)
                pe.matmul(side[:, 2, P:T], at_v[:, 1, :], at_pt[:, T:3 * P], start=False,
                          stop=True).then_inc(at_out, 1)

            pe.wait_ge(v_free, (B_G1 - B_V) * TT)
            with pe.Fori(0, B_G2 - B_G1) as i:
                for c in range(CH):
                    for a in range(2):
                        h = i * 2 + a
                        if c == 1 + 7 * a:
                            pe.wait_ge(qs_ready, h + 1)
                            pe.wait_ge(dec_ready, h + 1)
                            pe.wait_ge(at_exp, i * 4 + 2 * a)
                            key = br[:, KEY0 + h, :]
                            q0, q1 = side[:, 0, 0:P], side[:, 0, P:3 * P]
                            pe.matmul(q0, at_q[:, 0:P], key[:, 0:P], start=True, stop=False)
                            pe.matmul(q0, at_dec[:, 0, :], later[:, P:2 * P], start=False, stop=False)
                            pe.matmul(q0, ident_b[:, :], causal_b[:, :], start=False, stop=True)
                            pe.matmul(q1, at_q[:, P:T], key[:, :], start=True, stop=False)
                            pe.matmul(side[:, 0, P:2 * P], at_dec[:, 1, :], later[:, P:2 * P],
                                      start=False, stop=False)
                            pe.matmul(q1, at_dec[:, 2, :], later[:, :], start=False, stop=False)
                            pe.matmul(side[:, 0, 2 * P:3 * P], ident_b[:, :], causal_b[:, :],
                                      start=False, stop=True).then_inc(at_scores, 1)
                        if c == 4 + 7 * a:
                            pe.wait_ge(at_norm, i * 4 + 2 * a + 2)
                            transposes(h)
                        if c == 6 + 7 * a:
                            weighted_values(h)
                    chunk_fm(i + B_G1, i + B_V, c)

            with pe.Fori(0, B_OUT - B_G2) as i:
                for c in range(CH):
                    for a in range(2):
                        h = i * 2 + (FT + a)
                        if c == 1 + 7 * a:
                            pe.wait_ge(qs_ready, h + 1)
                            pe.wait_ge(sb_dve, i * 8 + 4 * a)
                            pe.wait_ge(at_exp, i * 2 + (2 * FT + a))
                            key = br[:, KEY0 + h, :]
                            q0, q1 = side[:, 0, 0:P], side[:, 0, P:3 * P]
                            pe.matmul(q0, at_q[:, 0:P], key[:, 0:P], start=True, stop=False)
                            pe.matmul(q0, ident_b[:, :], strict_b[:, :], start=False, stop=True)
                            pe.matmul(q1, at_q[:, P:T], key[:, :], start=True, stop=False)
                            pe.matmul(side[:, 0, 2 * P:3 * P], ident_b[:, :], strict_b[:, :],
                                      start=False, stop=True).then_inc(at_scores, 1)
                        if c == 5 + 7 * a:
                            pe.wait_ge(at_exp, i * 2 + (2 * FT + a + 1))
                            transposes(h)
                        if c == 7 + 7 * a:
                            weighted_values(h)
                    chunk_fm(i + B_G2, i + (B_V + B_G2 - B_G1), c)

            for c in range(CH):
                chunk_tm(B_OUT, c, lambda a: pe.wait_ge(bank_free, 20 * JB + 4), mixed_parts=True)
            with pe.Fori(1, N_OUT_BLOCKS) as i:
                def o_bank(a):
                    pe.wait_ge(o_mg, i * TT - TT + a + 1)

                for c in range(CH):
                    chunk_tm(i + B_OUT, c, o_bank)

        @block.scalar
        def _(act):
            def high(b, c):
                act.wait_ge(raw_in[c % RING], b * (16 * CH // RING) + 16 * (c // RING + 1))
                if not (isinstance(b, int) and b * CH + c < RING):
                    act.wait_ge(w_used, b * CH + (c - RING + 1))
                act.activation(w_hi[:, c % RING, :], w_raw[:, c % RING, :], ACT.Copy).then_inc(hi_ready, 1)

            def fm_wait(b, m, j):
                if j < JB - 1:
                    act.wait_ge(fm_done, m * (JB - 1) + j + 1)
                else:
                    act.wait_ge(w_used, b * CH + CH)

            def copy_cross(b, m, scale):
                for j in range(JB):
                    fm_wait(b, m, j)
                    act.activation(cross[:, j, :], main[:, j, T:2 * T], ACT.Copy,
                                   scale=scale).then_inc(bank_cross, 1)

            act.dma_start(pars[:, :], par).then_inc(par_in, 16)
            act.dma_start(wf_raw, wfg).then_inc(wf_in, 16)
            tmp = lambda n: s5tmp[:, n, :]
            act.wait_ge(par_in, 16)
            act.activation(tmp(0), col("log_dt"), ACT.Exp).then_inc(pa, 1)
            act.activation(log_a[0], col("lam"), ACT.Abs).then_inc(pa, 1)
            act.wait_ge(pa, 2)
            act.activation(log_a[0], log_a[0], ACT.Exp, scale=-1.0).then_inc(pa, 1)
            act.wait_ge(pd, 9)
            act.activation(tmp(4), tmp(1), ACT.Exp).then_inc(pa, 1)
            act.activation(tmp(5), tmp(1), ACT.Tanh, scale=0.5).then_inc(pa, 1)
            act.activation(tmp(6), tmp(3), ACT.Sin, scale=TWO_PI).then_inc(pa, 1)
            act.activation(tmp(7), tmp(3), ACT.Sin, scale=TWO_PI / 2).then_inc(pa, 1)
            act.wait_ge(wf_in, 16)
            act.activation(wf[:, :, 0:FT], wf_raw, ACT.Copy).then_inc(wf_hi, 1)
            for n, (a, h) in enumerate(halves):
                act.wait_ge(x_in[n], 16)
                if n:
                    act.wait_ge(squared, n)
                act.activation(main[:, :, :].rearrange("p j n -> p (j n)"), x_rows[:, a, h * HW:(h + 1) * HW],
                               ACT.Square, accum_out=sumsq[:, n:n + 1]).then_inc(squared, 1)
            act.wait_ge(rms_dve, 2)
            act.activation(rs_a[:, 0:TT], ms[:, 0:TT], ACT.Sqrt).then_inc(rms_act, 1)
            for c in range(LEAD):
                high(0, c)
            for k in range(NK):
                act.wait_ge(xt_done, k + 1)
                act.activation(acts[:, k, 0:T], xt_bank(k)[:, :], ACT.Copy,
                               scale=col("g_pre", k)).then_inc(u_hi, 1)

            with act.Fori(0, B_QK - B_SRC) as i:
                for c in range(CH):
                    if c == CH - 1:
                        copy_cross(i, i, 1.0)
                    high(i, c + LEAD)

            act.wait_ge(fl_mm, 1)
            act.activation(fl[:, :, 0:2 * FT], side[:, 0:2, 0:2 * FT], ACT.Copy).then_inc(fl_act, 1)
            act.activation(fl[:, :, 2 * FT:3 * FT], side[:, 2:4, 0:FT], ACT.Copy).then_inc(fl_act, 1)
            act.wait_ge(fl_dve, 3)
            act.activation(fl_e, fl_z, ACT.Abs).then_inc(fl_act, 1)
            act.wait_ge(fl_act, 3)
            act.activation(fl_e, fl_e, ACT.Exp, scale=-1.0).then_inc(fl_act, 1)
            act.wait_ge(fl_act, 4)
            act.activation(fl_e, fl_e, ACT.Ln, bias=1.0).then_inc(fl_act, 1)

            with act.Fori(0, B_V - B_QK) as i:
                for c in range(CH):
                    if c == 0:
                        act.wait_ge(s5_bmm, i * SJ)
                        act.dma_start(s5_bt, bt[bass.ds(i, 1), :, :].rearrange("f p n -> (f p) n")
                                      .rearrange("p (j r s) -> p j r s", j=SJ, r=2)).then_inc(bt_in, 16)
                        act.wait_ge(s5_cprime, i)
                        act.dma_start(s5_ct, ct[bass.ds(i, 1), :, :].rearrange("f p n -> (f p) n")
                                      .rearrange("p (j r h) -> p j r h", j=SJ, r=2)).then_inc(ct_in, 16)
                    if c % 3 == 0 and c // 3 < SJ:
                        j = c // 3
                        act.wait_ge(s5_frac, i * SJ + j + 1)
                        act.wait_ge(s5_done, i * SJ + max(j - 1, 0))
                        act.activation(s5_sin[j % 2][:, 0:T], s5_f, ACT.Sin, scale=TWO_PI).then_inc(s5_trig, 1)
                        act.activation(s5_sin[j % 2][:, T:2 * T], s5_f, ACT.Sin, scale=-TWO_PI
                                       ).then_inc(s5_trig, 1)
                        act.wait_ge(s5_cosd, i * SJ + j)
                        act.activation(s5_q, s5_f, ACT.Sin, scale=TWO_PI / 2).then_inc(s5_trig, 1)
                        act.wait_ge(s5_trig, i * 4 * SJ + 4 * j + 3)
                        act.activation(s5_q, s5_q, ACT.Square, scale=math.sqrt(2.0)).then_inc(s5_trig, 1)
                    if c == CH - 1:
                        copy_cross(i + B_QK, i + B_QK, QK_SCALE)
                    high(i + B_QK, c + LEAD)

            act.wait_ge(s5_y, FT)
            for f in range(FT):
                act.activation(br[:, SSM0 + f, :], br[:, SSM0 + f, :], ACT.Gelu_apprx_tanh).then_inc(gelu_done, 1)

            with act.Fori(0, B_G1 - B_V) as i:
                for c in range(CH):
                    for a, at in ((0, 0), (1, 7)):
                        f = i * 2 + a
                        if c == at:
                            act.wait_ge(glu_mm, f)
                            act.dma_start(glu_w, wglu[bass.ds(f, 1), :, :].rearrange("f p n -> (f p) n")
                                          .rearrange("p (k n) -> p k n", k=FT)).then_inc(wg_in, 16)
                            act.wait_ge(lru_mm, f)
                            act.dma_start(lru_w, wri[bass.ds(f, 1), :, :].rearrange("f p n -> (f p) n")
                                          .rearrange("p (r n) -> p r n", r=2)).then_inc(wr_in, 16)
                        if c == at + 3:
                            act.wait_ge(lru_mm, f + 1)
                            act.wait_ge(lru_done, f)
                            act.activation(lru_ri[:, 0:T], side[:, 0, 0:T], ACT.Sigmoid,
                                           bias=lru_now[:, B_R:B_R + 1]).then_inc(lru_act, 1)
                            act.activation(lru_ri[:, T:2 * T], side[:, 0, T:2 * T], ACT.Sigmoid,
                                           bias=lru_now[:, B_I:B_I + 1]).then_inc(lru_act, 1)
                            act.wait_ge(lru_act, i * 12 + 6 * a + 1)
                            act.activation(lru_a, lru_ri[:, 0:T], ACT.Exp,
                                           scale=lru_now[:, LOG_A:LOG_A + 1]).then_inc(lru_act, 1)
                            act.activation(lru_th, lru_ri[:, 0:T], ACT.Tanh,
                                           scale=lru_now[:, LOG_A:LOG_A + 1]).then_inc(lru_act, 1)
                            act.wait_ge(lru_act, i * 12 + 6 * a + 3)
                            act.activation(lru_s, lru_a, ACT.Square).then_inc(lru_act, 1)
                        if c == at + 5:
                            act.wait_ge(lru_v, i * 18 + 9 * a + 7)
                            act.activation(lru_s, lru_s, ACT.Sqrt, scale=-1.0).then_inc(lru_act, 1)
                            act.wait_ge(glu_mm, f + 1)
                            act.wait_ge(par_in, 16)
                            act.activation(glu_z[:, f, :], side[:, 1, 0:T], ACT.Sigmoid,
                                           bias=lru_now[:, B_GLU:B_GLU + 1]).then_inc(glu_sig, 1)
                    if c == CH - 1:
                        for a in range(TT):
                            if a < TT - 1:
                                act.wait_ge(tm_done, i * (TT - 1) + a + 1)
                            else:
                                act.wait_ge(w_used, (i + B_V) * CH + CH)
                            act.wait_ge(gelu_done, FT)
                            act.activation(vals[:, a, bass.ds(i * BLK, BLK)], main[:, a, :],
                                           ACT.Copy).then_inc(v_free, 1)
                    high(i + B_V, c + LEAD)

            def silus(m):
                for j in range(JB):
                    act.wait_ge(bank_free, m * JB + (JB + j + 1))
                    act.activation(cross[:, j, :], cross[:, j, :], ACT.Silu).then_inc(gate_silu, 1)

            def copy_weights(h):
                act.wait_ge(at_tr, h + 1)
                act.wait_ge(at_out, h)
                act.activation(at_pt, side[:, 1, 0:3 * P], ACT.Copy).then_inc(at_ptd, 1)

            with act.Fori(0, B_G2 - B_G1) as i:
                for c in range(CH):
                    for a in range(2):
                        h = i * 2 + a
                        if c == 2 + 7 * a:
                            act.wait_ge(at_max, h + 1)
                            act.wait_ge(at_tr, h)
                            act.activation(at_p[:, 0:P], side[:, 0, 0:P], ACT.Exp, bias=row_max[:, 0:1],
                                           accum_out=row_sum[:, 0:1]).then_inc(at_exp, 1)
                            act.activation(at_p[:, P:3 * P], side[:, 0, P:3 * P], ACT.Exp, bias=row_max[:, 1:2],
                                           accum_out=row_sum[:, 1:2]).then_inc(at_exp, 1)
                        if c == 5 + 7 * a:
                            copy_weights(h)
                    if c == CH - 1:
                        act.wait_ge(gate_used, i * JB)
                        copy_cross(i + B_G1, i + B_V, 1.0)
                        silus(i + B_V)
                    high(i + B_G1, c + LEAD)

            with act.Fori(0, B_OUT - B_G2) as i:
                for c in range(CH):
                    for a in range(2):
                        h = i * 2 + (FT + a)
                        if c == 2 + 7 * a:
                            act.wait_ge(at_scores, h + 1)
                            act.wait_ge(at_exp, i * 2 + (2 * FT + a))
                            act.activation(at_e, side[:, 0, 0:3 * P], ACT.Abs).then_inc(sb_act, 1)
                            act.wait_ge(sb_act, i * 6 + 3 * a + 1)
                            act.activation(at_e, at_e, ACT.Exp, scale=-1.0).then_inc(sb_act, 1)
                            act.wait_ge(sb_act, i * 6 + 3 * a + 2)
                            act.activation(at_e, at_e, ACT.Ln, bias=1.0).then_inc(sb_act, 1)
                        if c == 4 + 7 * a:
                            act.wait_ge(sb_dve, i * 8 + 4 * a + 4)
                            act.wait_ge(at_tr, h)
                            act.activation(at_p, at_e, ACT.Exp).then_inc(at_exp, 1)
                        if c == 6 + 7 * a:
                            copy_weights(h)
                    if c == CH - 1:
                        act.wait_ge(gate_used, i * JB + (B_G2 - B_G1) * JB)
                        copy_cross(i + B_G2, i + (B_V + B_G2 - B_G1), 1.0)
                        silus(i + (B_V + B_G2 - B_G1))
                    high(i + B_G2, c + LEAD)

            def squares(n, last):
                for a in range(TT):
                    if a < TT - 1:
                        act.wait_ge(tm_done, n * (TT - 1) + (B_G1 - B_V) * (TT - 1) + a + 1)
                    else:
                        act.wait_ge(w_used, (n + B_OUT) * CH + CH)
                    act.wait_ge(o_ss, n)
                    act.activation(side[:, a, :], main[:, a, :], ACT.Square,
                                   accum_out=ss_new[:, a:a + 1]).then_inc(o_sq, 1)

            act.wait_ge(at_o, 2 * FT)
            act.wait_ge(w_used, B_OUT * CH)
            act.dma_start(g_rows, gpost.partition_broadcast(P)).then_inc(g_in, 16)
            for a in range(TT):
                act.dma_start(x_late[a], x[a * P:(a + 1) * P, :]).then_inc(xl_in[a], 16)
            for c in range(CH):
                for k in range(KC * c, KC * (c + 1)):
                    act.wait_ge(gate_used, min(k + 1, NK))
                    act.activation(acts[:, k, 0:T], br[:, k, :], ACT.Copy).then_inc(mix_hi, 1)
                if c == CH - 1:
                    squares(0, False)
                high(B_OUT, c + LEAD)
            with act.Fori(1, N_OUT_BLOCKS - 1) as i:
                for c in range(CH):
                    if c == CH - 1:
                        squares(i, False)
                    high(i + B_OUT, c + LEAD)
            for c in range(CH - LEAD):
                high(N_BLOCKS - 1, c + LEAD)
            squares(N_OUT_BLOCKS - 1, True)
            act.wait_ge(fin_dve, 1)
            act.activation(rs_a[:, 0:TT], ms[:, 0:TT], ACT.Sqrt).then_inc(fin_act, 1)

        @block.vector
        def _(dve):
            def low(b, c):
                dve.wait_ge(hi_ready, b * CH + c + 1)
                if not (isinstance(b, int) and b * CH + c < RING):
                    dve.wait_ge(w_used, b * CH + (c - RING + 1))
                dve.tensor_tensor(w_lo[:, c % RING, :], w_raw[:, c % RING, :],
                                  w_hi[:, c % RING, :].bitcast(F32), ALU.subtract).then_inc(lo_ready, 1)

            tmp = lambda n: s5tmp[:, n, :]
            kind = lambda n: s5par[:, :, n * SJ:(n + 1) * SJ]
            by_tile = lambda ap: ap.rearrange("p (f j) -> p f j", f=FT)
            are, aim = col("a_re"), col("a_im")
            n_pd = 0

            def stepped(instruction):
                nonlocal n_pd
                instruction.then_inc(pd, 1)
                n_pd += 1
                return n_pd

            dve.wait_ge(pa, 1)
            dve.wait_ge(par_in, 16)
            stepped(dve.tensor_tensor(tmp(1), are, tmp(0), ALU.mult))
            y = stepped(dve.tensor_tensor(tmp(2), aim, tmp(0), ALU.mult))
            dve.wait_ge(pd, y)
            y = stepped(dve.tensor_scalar(tmp(8), tmp(2), 1.0 / (2 * math.pi), ROUND, ALU.mult, ALU.add))
            dve.wait_ge(pd, y)
            y = stepped(dve.tensor_scalar(tmp(9), tmp(8), -ROUND, None, ALU.add))
            dve.wait_ge(pd, y)
            y = stepped(dve.scalar_tensor_tensor(tmp(10), tmp(9), -PI_1, tmp(2), ALU.mult, ALU.add))
            dve.wait_ge(pd, y)
            y = stepped(dve.scalar_tensor_tensor(tmp(11), tmp(9), -PI_2, tmp(10), ALU.mult, ALU.add))
            dve.wait_ge(pd, y)
            y = stepped(dve.scalar_tensor_tensor(tmp(12), tmp(9), -PI_3, tmp(11), ALU.mult, ALU.add))
            dve.wait_ge(pd, y)
            y = stepped(dve.tensor_scalar(tmp(13), tmp(12), 1.0 / (2 * math.pi), 0.5, ALU.mult, ALU.min))
            dve.wait_ge(pd, y)
            y = stepped(dve.tensor_scalar(tmp(3), tmp(13), -0.5, None, ALU.max))
            dve.wait_ge(pd, y)
            stepped(dve.tensor_scalar(kind(0), by_tile(tmp(3)), 1.0, None, ALU.mult))
            dve.wait_ge(pa, 7)
            stepped(dve.tensor_scalar(kind(1), by_tile(tmp(4)), 1.0, None, ALU.mult))
            em = stepped(dve.scalar_tensor_tensor(tmp(8), tmp(4), 1.0, tmp(5), ALU.add, ALU.mult))
            sh = stepped(dve.tensor_tensor(tmp(9), tmp(7), tmp(7), ALU.mult))
            stepped(dve.tensor_tensor(tmp(10), tmp(4), tmp(6), ALU.mult))
            stepped(dve.tensor_tensor(tmp(11), are, are, ALU.mult))
            a2 = stepped(dve.tensor_tensor(tmp(12), aim, aim, ALU.mult))
            dve.wait_ge(pd, a2)
            y = stepped(dve.tensor_scalar(tmp(9), tmp(9), -2.0, None, ALU.mult))
            stepped(dve.tensor_tensor(tmp(13), tmp(11), tmp(12), ALU.add))
            dve.wait_ge(pd, y)
            y = stepped(dve.tensor_tensor(tmp(14), tmp(8), tmp(9), ALU.mult))
            dve.wait_ge(pd, y)
            y = stepped(dve.tensor_tensor(tmp(15), tmp(14), tmp(8), ALU.add))
            stepped(dve.reciprocal(tmp(16), tmp(13)))
            dve.wait_ge(pd, y)
            y = stepped(dve.tensor_tensor(tmp(14), tmp(15), tmp(9), ALU.add))
            dve.wait_ge(pd, y)
            stepped(dve.tensor_tensor(tmp(11), tmp(14), are, ALU.mult))
            stepped(dve.tensor_tensor(tmp(12), tmp(10), aim, ALU.mult))
            stepped(dve.tensor_tensor(tmp(13), tmp(10), are, ALU.mult))
            y = stepped(dve.tensor_tensor(tmp(15), tmp(14), aim, ALU.mult))
            dve.wait_ge(pd, y)
            stepped(dve.tensor_tensor(tmp(11), tmp(11), tmp(12), ALU.add))
            y = stepped(dve.tensor_tensor(tmp(13), tmp(15), tmp(13), ALU.subtract))
            dve.wait_ge(pd, y)
            y = stepped(dve.tensor_tensor(kind(2), by_tile(tmp(11)), by_tile(tmp(16)), ALU.mult))
            stepped(dve.tensor_tensor(kind(4), by_tile(tmp(13)), by_tile(tmp(16)), ALU.mult))
            dve.wait_ge(pd, y)
            stepped(dve.tensor_scalar(kind(3), kind(2), -1.0, None, ALU.mult))
            e, s, s2, q = log_a
            dve.wait_ge(pa, 3)
            y = stepped(dve.tensor_scalar(s, e, 2.0, None, ALU.add))
            dve.wait_ge(pd, y)
            y = stepped(dve.reciprocal(s2, s))
            dve.wait_ge(pd, y)
            y = stepped(dve.tensor_tensor(s, e, s2, ALU.mult))
            dve.wait_ge(pd, y)
            y = stepped(dve.tensor_tensor(s2, s, s, ALU.mult))
            dve.wait_ge(pd, y)
            y = stepped(dve.tensor_scalar(q, s2, 1.0 / 17, None, ALU.mult))
            for n in range(15, 1, -2):
                dve.wait_ge(pd, y)
                y = stepped(dve.scalar_tensor_tensor(q, q, 1.0 / n, s2, ALU.add, ALU.mult))
            dve.wait_ge(pd, y)
            y = stepped(dve.scalar_tensor_tensor(q, q, 1.0, s, ALU.add, ALU.mult))
            y = stepped(dve.tensor_scalar(e, col("lam"), 0.0, LRU_C, ALU.min, ALU.mult))
            dve.wait_ge(pd, y)
            y = stepped(dve.scalar_tensor_tensor(lru_par[:, :, LOG_A:LOG_A + 1].rearrange("p f n -> p (f n)"),
                                                 q, -2.0 * LRU_C, e, ALU.mult, ALU.add))
            dve.wait_ge(wf_hi, 1)
            dve.tensor_tensor(wf[:, :, FT:2 * FT], wf_raw, wf[:, :, 0:FT].bitcast(F32),
                              ALU.subtract).then_inc(wf_lo, 1)

            def root(step, first):
                z = lambda ap: ap[:, 0:TT]
                dve.reciprocal(z(rs_b), z(rs_a)).then_inc(step, 1)
                dve.wait_ge(step, first + 1)
                dve.tensor_tensor(z(rs_a), z(rs_b), z(rs_b), ALU.mult).then_inc(step, 1)
                dve.wait_ge(step, first + 2)
                dve.tensor_tensor(z(rs_a), z(rs_a), z(ms), ALU.mult).then_inc(step, 1)
                dve.wait_ge(step, first + 3)
                dve.tensor_scalar(z(rs_a), z(rs_a), -0.5, 1.5, ALU.mult, ALU.add).then_inc(step, 1)
                dve.wait_ge(step, first + 4)
                dve.tensor_tensor(z(rstd), z(rs_a), z(rs_b), ALU.mult).then_inc(step, 1)
                dve.wait_ge(step, first + 5)

            dve.wait_ge(squared, 4)
            ss = sumsq.rearrange("p (a h) -> p a h", a=TT)
            dve.tensor_tensor(ms[:, 0:TT], ss[:, :, 0], ss[:, :, 1], ALU.add).then_inc(rms_dve, 1)
            dve.wait_ge(rms_dve, 1)
            dve.tensor_scalar(ms[:, 0:TT], ms[:, 0:TT], 1.0 / D, EPS, ALU.mult, ALU.add).then_inc(rms_dve, 1)
            dve.wait_ge(rms_act, 1)
            root(rms_dve, 2)
            for a, h in halves:
                part = x_rows[:, a, h * HW:(h + 1) * HW]
                dve.tensor_scalar(part, part, rstd[:, a:a + 1], None, ALU.mult).then_inc(bank_free, 1)
            for k in range(NK):
                dve.wait_ge(u_hi, k + 1)
                dve.scalar_tensor_tensor(acts[:, k, T:2 * T],
                                         xt_bank(k), col("g_pre", k), acts[:, k, 0:T].bitcast(F32),
                                         ALU.mult, ALU.subtract).then_inc(u_lo, 1)
                if k < LEAD:
                    low(0, k)

            with dve.Fori(0, B_QK - B_SRC) as i:
                for c in range(CH):
                    if c == CH - 1:
                        for j in range(JB):
                            dve.wait_ge(bank_cross, i * JB + j + 1)
                            dve.tensor_tensor(br[:, i * JB + j, :], main[:, j, 0:T], cross[:, j, :],
                                              ALU.add).then_inc(bank_free, 1)
                    low(i, c + LEAD)

            dve.wait_ge(fl_act, 2)
            dve.tensor_tensor(fl_z, fl[:, :, 0:FT], fl[:, :, FT:2 * FT], ALU.add).then_inc(fl_dve, 1)
            dve.wait_ge(fl_dve, 1)
            dve.tensor_tensor(fl_z, fl_z, fl[:, :, 2 * FT:3 * FT], ALU.add).then_inc(fl_dve, 1)
            dve.wait_ge(fl_dve, 2)
            dve.tensor_tensor(fl_z, fl_z, col("b_forget").rearrange("p (a h) -> p a h", a=TT),
                              ALU.add).then_inc(fl_dve, 1)
            dve.wait_ge(fl_act, 5)
            dve.wait_ge(fl_dve, 3)
            dve.scalar_tensor_tensor(logf[:, :, :].rearrange("p h a -> p a h"), fl_z, 0.0, fl_e,
                                     ALU.min, ALU.subtract).then_inc(fl_dve, 1)

            wide = lambda ap: ap.rearrange("p (r t) -> p r t", r=2)
            both = lambda ap: ap.unsqueeze(1).to_broadcast([P, 2, T])
            with dve.Fori(0, B_V - B_QK) as i:
                for c in range(CH):
                    if c == 0:
                        dve.wait_ge(s5_frac, i * SJ)
                        dve.wait_ge(s5_cprime, i)
                        dve.wait_ge(s5_done, i * SJ)
                        dve.wait_ge(pd, n_pd)
                        dve.tensor_scalar(s5_now, s5par[:, i, :], 1.0, None, ALU.mult).then_inc(p5_ready, 1)
                        dve.wait_ge(s5_bmm, i * SJ)
                        dve.wait_ge(s5_y, i)
                        dve.tensor_scalar(s5_u, br[:, SSM0 + i, :], 1.0, None, ALU.mult).then_inc(su_ready, 1)
                    if c >= 2 and (c - 2) // 3 < SJ:
                        j, part = (c - 2) // 3, (c - 2) % 3
                        g, done = i * SJ + j, i * (7 * SJ) + 7 * j
                        sin, cos, hs = s5_sin[j % 2], s5_cos[j % 2], s5_h[j % 2]
                        bu = side[:, j % 2, :]
                        if part == 0:
                            dve.wait_ge(s5_bmm, g + 1)
                            dve.wait_ge(s5_cosd, g + 1)
                            dve.wait_ge(s5_done, g)
                            dve.tensor_tensor(wide(s5_m1), wide(bu), both(cos), ALU.mult).then_inc(s5_dve, 1)
                            dve.tensor_tensor(wide(s5_m2), wide(bu)[:, ::-1, :], wide(sin),
                                              ALU.mult).then_inc(s5_dve, 1)
                            dve.wait_ge(s5_dve, done + 2)
                            dve.tensor_tensor(s5_m1, s5_m1, s5_m2, ALU.add).then_inc(s5_dve, 1)
                        if part == 1:
                            radius = s5_now[:, SJ + j:SJ + j + 1].to_broadcast([P, T])
                            dve.wait_ge(p5_ready, i + 1)
                            dve.wait_ge(s5_dve, done + 3)
                            for r in range(2):
                                dve.tensor_tensor_scan(s5_g[:, r * T:(r + 1) * T], radius,
                                                       s5_m1[:, r * T:(r + 1) * T], 0.0,
                                                       ALU.mult, ALU.add).then_inc(s5_dve, 1)
                        if part == 2:
                            dve.wait_ge(s5_dve, done + 5)
                            dve.tensor_tensor(wide(s5_m1), wide(s5_g), both(cos), ALU.mult).then_inc(s5_dve, 1)
                            dve.tensor_tensor(wide(s5_m2), wide(s5_g)[:, ::-1, :], wide(sin),
                                              ALU.mult).then_inc(s5_dve, 1)
                            dve.wait_ge(s5_dve, done + 7)
                            dve.wait_ge(s5_cmm, i * SJ + max(j - 1, 0))
                            dve.tensor_tensor(hs, s5_m1, s5_m2, ALU.subtract).then_inc(s5_done, 1)
                    if c == CH - 1:
                        dve.wait_ge(s5_cmm, i * SJ + SJ)
                        dve.scalar_tensor_tensor(br[:, SSM0 + i, :], s5_u,
                                                 pars[:, bass.ds(i + PC["ssm_d"][0], 1)],
                                                 side[:, 2, 0:T], ALU.mult, ALU.add).then_inc(s5_y, 1)
                        for j in range(JB):
                            dve.wait_ge(bank_cross, i * JB + (B_QK * JB + j + 1))
                            dve.scalar_tensor_tensor(br[:, i * JB + (FOX0 + j), :], main[:, j, 0:T], QK_SCALE,
                                                     cross[:, j, :], ALU.mult, ALU.add).then_inc(bank_free, 1)
                    low(i + B_QK, c + LEAD)

            dve.wait_ge(gelu_done, FT)
            with dve.Fori(0, B_G1 - B_V) as i:
                for c in range(CH):
                    for a, at in ((0, 0), (1, 7)):
                        f, done = i * 2 + a, i * 18 + 9 * a
                        now = lambda n: lru_now[:, n:n + 1]
                        if c == at:
                            dve.wait_ge(glu_sig, f)
                            dve.wait_ge(lru_done, f)
                            dve.tensor_scalar(lru_now, lru_par[:, f, :], 1.0, None, ALU.mult).then_inc(lru_v, 1)
                            dve.tensor_scalar(lru_x, br[:, LRU0 + f, :], 1.0, None, ALU.mult).then_inc(lru_v, 1)
                            dve.wait_ge(lru_v, done + 2)
                            dve.tensor_scalar(lru_xc, lru_x, now(TAP0 + 3), now(CONV_B), ALU.mult,
                                              ALU.add).then_inc(lru_v, 1)
                            for s in range(1, 4):
                                dve.wait_ge(lru_v, done + 2 + s)
                                dve.scalar_tensor_tensor(lru_xc[:, s:T], lru_x[:, 0:T - s], now(TAP0 + 3 - s),
                                                         lru_xc[:, s:T], ALU.mult, ALU.add).then_inc(lru_v, 1)
                        if c == at + 4:
                            dve.wait_ge(lru_act, i * 12 + 6 * a + 5)
                            dve.scalar_tensor_tensor(lru_s, lru_s, 1.0, lru_th, ALU.add,
                                                     ALU.mult).then_inc(lru_v, 1)
                        if c == at + 6:
                            dve.wait_ge(lru_act, i * 12 + 6 * a + 6)
                            dve.tensor_tensor(lru_x, lru_ri[:, T:2 * T], lru_xc, ALU.mult).then_inc(lru_v, 1)
                            dve.wait_ge(lru_v, done + 8)
                            dve.tensor_tensor(lru_x, lru_x, lru_s, ALU.mult).then_inc(lru_v, 1)
                            dve.wait_ge(lru_v, done + 9)
                            dve.tensor_tensor_scan(br[:, LRU0 + f, :], lru_a, lru_x, 0.0, ALU.mult,
                                                   ALU.add).then_inc(lru_done, 1)
                    low(i + B_V, c + LEAD)
            dve.wait_ge(glu_sig, FT)
            dve.tensor_tensor(br[:, SSM0:SSM0 + FT, :], br[:, SSM0:SSM0 + FT, :], glu_z,
                              ALU.mult).then_inc(glu_applied, 1)

            def gates(i, g, m, tile0):
                for j in range(JB):
                    dve.wait_ge(bank_cross, m * JB + j + 1)
                    dve.tensor_tensor(cross[:, j, :], main[:, j, 0:T], cross[:, j, :],
                                      ALU.add).then_inc(bank_free, 1)
                for j in range(JB):
                    dve.wait_ge(glu_applied, 1)
                    dve.wait_ge(gate_silu, g * JB + j + 1)
                    tile = br[:, i * JB + (tile0 + j), :]
                    dve.tensor_tensor(tile, tile, cross[:, j, :], ALU.mult).then_inc(gate_used, 1)

            def head_out(h):
                dve.wait_ge(at_out, h + 1)
                dve.tensor_scalar(br[:, FOX0 + h, :], side[:, 2, 0:T], 1.0, None, ALU.mult).then_inc(at_o, 1)

            with dve.Fori(0, B_G2 - B_G1) as i:
                for c in range(CH):
                    if c == 0:
                        dve.wait_ge(dec_ready, i * 2)
                        dve.wait_ge(fl_dve, 4)
                        dve.tensor_scalar(lf_now.rearrange("p (h a) -> p h a", h=2),
                                          logf[:, bass.ds(i * 2, 2), :], 1.0, None,
                                          ALU.mult).then_inc(lf_ready, 1)
                    for a in range(2):
                        h = i * 2 + a
                        if c == 2 + 7 * a:
                            dve.wait_ge(at_scores, h + 1)
                            dve.tensor_reduce(row_max[:, 0:1], side[:, 0, 0:P], AX.X, ALU.max, negate=True)
                            dve.tensor_reduce(row_max[:, 1:2], side[:, 0, P:3 * P], AX.X, ALU.max,
                                              negate=True).then_inc(at_max, 1)
                        if c == 3 + 7 * a:
                            dve.wait_ge(at_exp, i * 4 + 2 * a + 2)
                            dve.wait_ge(at_norm, i * 4 + 2 * a)
                            dve.reciprocal(row_inv, row_sum).then_inc(at_inv, 1)
                            dve.wait_ge(at_inv, h + 1)
                            dve.tensor_scalar(at_p[:, 0:P], at_p[:, 0:P], row_inv[:, 0:1], None,
                                              ALU.mult).then_inc(at_norm, 1)
                            dve.tensor_scalar(at_p[:, P:3 * P], at_p[:, P:3 * P], row_inv[:, 1:2], None,
                                              ALU.mult).then_inc(at_norm, 1)
                        if c == 7 + 7 * a:
                            head_out(h)
                    if c == CH - 1:
                        gates(i, i, i + B_V, SSM0)
                    low(i + B_G1, c + LEAD)

            with dve.Fori(0, B_OUT - B_G2) as i:
                for c in range(CH):
                    for a in range(2):
                        h, done = i * 2 + (FT + a), i * 8 + 4 * a
                        if c == 3 + 7 * a:
                            dve.wait_ge(sb_act, i * 6 + 3 * a + 3)
                            dve.wait_ge(sb_dve, done)
                            dve.scalar_tensor_tensor(at_sp, side[:, 0, 0:3 * P], 0.0, at_e, ALU.max,
                                                     ALU.add).then_inc(sb_dve, 1)
                            dve.wait_ge(sb_dve, done + 1)
                            dve.tensor_tensor_scan(at_r[:, 0:P][:, ::-1], ones[:, 0:P],
                                                   at_sp[:, 0:P][:, ::-1], 0.0, ALU.mult,
                                                   ALU.add).then_inc(sb_dve, 1)
                            dve.tensor_tensor_scan(at_r[:, P:3 * P][:, ::-1], ones,
                                                   at_sp[:, P:3 * P][:, ::-1], 0.0, ALU.mult,
                                                   ALU.add).then_inc(sb_dve, 1)
                            dve.wait_ge(sb_dve, done + 3)
                            dve.tensor_tensor(at_e, side[:, 0, 0:3 * P], at_r, ALU.subtract).then_inc(sb_dve, 1)
                        if c == 8 + 7 * a:
                            head_out(h)
                    if c == CH - 1:
                        gates(i, i + (B_G2 - B_G1), i + (B_V + B_G2 - B_G1), FOX0)
                    low(i + B_G2, c + LEAD)

            def weigh(n, b):
                for a in range(TT):
                    dve.wait_ge(o_sq, n * TT + a + 1)
                    dve.wait_ge(g_in, 16)
                    dve.tensor_tensor(mixed[:, a, bass.ds(n * BLK, BLK)], main[:, a, :],
                                      g_rows[:, bass.ds(n * BLK, BLK)], ALU.mult).then_inc(o_mg, 1)
                dve.wait_ge(o_ss, n)
                if b:
                    dve.tensor_tensor(ss_all, ss_all, ss_new, ALU.add).then_inc(o_ss, 1)
                else:
                    dve.tensor_copy(ss_all, ss_new).then_inc(o_ss, 1)

            for c in range(CH):
                for k in range(KC * c, KC * (c + 1)):
                    dve.wait_ge(mix_hi, k + 1)
                    dve.tensor_tensor(acts[:, k, T:2 * T], br[:, k, :], acts[:, k, 0:T].bitcast(F32),
                                      ALU.subtract).then_inc(mix_lo, 1)
                if c == CH - 1:
                    weigh(0, False)
                low(B_OUT, c + LEAD)
            with dve.Fori(1, N_OUT_BLOCKS - 1) as i:
                for c in range(CH):
                    if c == CH - 1:
                        weigh(i, True)
                    low(i + B_OUT, c + LEAD)
            for c in range(CH - LEAD):
                low(N_BLOCKS - 1, c + LEAD)
            weigh(N_OUT_BLOCKS - 1, True)
            dve.wait_ge(o_ss, N_OUT_BLOCKS)
            dve.tensor_scalar(ms[:, 0:TT], ss_all, 1.0 / D, EPS, ALU.mult, ALU.add).then_inc(fin_dve, 1)
            dve.wait_ge(fin_act, 1)
            dve.wait_ge(fin_dve, 1)
            root(fin_dve, 1)
            dve.wait_ge(o_mg, N_OUT_BLOCKS * TT)
            for a, h in halves:
                part = mixed[:, a, h * HW:(h + 1) * HW]
                dve.wait_ge(xl_in[a], 16)
                dve.scalar_tensor_tensor(part, part, rstd[:, a:a + 1], x_late[a][:, h * HW:(h + 1) * HW],
                                         ALU.mult, ALU.add).then_inc(fin_sum, 1)

        @block.gpsimd
        def _(pool):
            pool.iota(steps_t, pattern=[[1, T]], base=0, channel_multiplier=0,
                      allow_small_or_imprecise_dtypes=True).then_inc(consts, 1)
            pool.memset(small[:, 176:177], ROUND).then_inc(consts, 1)
            pool.memset(later[:, :], 1.0).then_inc(const_steps, 1)
            pool.memset(upto[:, :], 1.0).then_inc(const_steps, 1)
            pool.memset(ident[:, :], 0.0).then_inc(const_steps, 1)
            pool.memset(ident_b[:, :], 0.0).then_inc(const_steps, 1)
            pool.memset(causal_b[:, :], 0.0).then_inc(const_steps, 1)
            pool.memset(strict_b[:, :], 0.0).then_inc(const_steps, 1)
            pool.wait_ge(const_steps, 6)

            def choose(t, op, fill, sign):
                pool.affine_select(out=t, in_=t, compare_op=op, fill=fill, base=0,
                                   pattern=[[-sign, P]], channel_multiplier=sign).then_inc(consts, 1)

            choose(later[:, P:2 * P], ALU.is_gt, 0.0, 1)
            choose(upto[:, :], ALU.is_ge, 0.0, -1)
            choose(ident[:, :], ALU.not_equal, 1.0, 1)
            choose(ident_b[:, :], ALU.not_equal, 1.0, 1)
            choose(causal_b[:, :], ALU.is_ge, NEG, 1)
            choose(strict_b[:, :], ALU.is_gt, NEG, 1)

            pool.wait_ge(consts, N_CONST)
            rounder = small[:, 176:177].to_broadcast([P, T])
            with pool.Fori(0, B_V - B_QK) as i:
                def fraction(j):
                    g, tab = i * SJ + j, i * (3 * SJ) + 3 * j
                    pool.wait_ge(p5_ready, i + 1)
                    pool.wait_ge(s5_frac, g)
                    pool.tensor_tensor(s5_a, steps_t, s5_now[:, j:j + 1].to_broadcast([P, T]),
                                       ALU.mult).then_inc(s5_tab, 1)
                    pool.wait_ge(s5_tab, tab + 1)
                    pool.tensor_tensor(s5_k, s5_a, rounder, ALU.add).then_inc(s5_tab, 1)
                    pool.wait_ge(s5_tab, tab + 2)
                    pool.tensor_tensor(s5_k, s5_k, rounder, ALU.subtract).then_inc(s5_tab, 1)
                    pool.wait_ge(s5_tab, tab + 3)
                    pool.wait_ge(s5_trig, i * (4 * SJ) + 4 * j)
                    pool.tensor_tensor(s5_f, s5_a, s5_k, ALU.subtract).then_inc(s5_frac, 1)

                def cosine(j):
                    pool.wait_ge(s5_trig, i * (4 * SJ) + 4 * j + 4)
                    pool.wait_ge(s5_done, i * SJ + max(j - 1, 0))
                    pool.tensor_tensor(s5_cos[j % 2], ones, s5_q, ALU.subtract).then_inc(s5_cosd, 1)

                fraction(0)
                now = lambda n: s5_now[:, n * SJ:(n + 1) * SJ].unsqueeze(2).to_broadcast([P, SJ, 2 * HG])
                pool.wait_ge(ct_in, i * 16 + 16)
                pool.wait_ge(s5_cprime, i)
                c_re, c_im = s5_ct[:, :, 0, :], s5_ct[:, :, 1, :]
                for n, (part, factor) in enumerate(((c_re, 2), (c_im, 4), (c_re, 4), (c_im, 3))):
                    pool.tensor_tensor(s5_c[n], part, now(factor), ALU.mult).then_inc(s5_cq, 1)
                pool.wait_ge(s5_cmm, i * SJ)
                pool.wait_ge(s5_cq, i * 5 + 4)
                pool.tensor_tensor(s5_cp[:, :, 0, :], s5_c[0], s5_c[1], ALU.add).then_inc(s5_cq, 1)
                pool.wait_ge(s5_cq, i * 5 + 5)
                pool.tensor_tensor(s5_cp[:, :, 1, :], s5_c[2], s5_c[3], ALU.add).then_inc(s5_cprime, 1)
                for j in range(SJ):
                    cosine(j)
                    if j + 1 < SJ:
                        fraction(j + 1)

            def fetch(h):
                pool.wait_ge(at_scores, h)
                pool.wait_ge(glu_applied, 1)
                pool.tensor_copy(at_q, br[:, FOX0 + h, :]).then_inc(qs_ready, 1)
                pool.wait_ge(at_out, h)
                pool.wait_ge(v_free, (B_G1 - B_V) * TT)
                pool.tensor_copy(at_v, vals[:, :, bass.ds(h * P, P)]).then_inc(vs_ready, 1)

            with pool.Fori(0, B_G2 - B_G1) as i:
                for a in range(2):
                    h = i * 2 + a
                    fetch(h)
                    for n, (mask, tile) in enumerate(((upto[:, :], 0), (later[:, 0:P], 0), (upto[:, :], 1))):
                        pool.wait_ge(lf_ready, i + 1)
                        pool.wait_ge(at_scores, h)
                        log_f = lf_now[:, 2 * a + tile:2 * a + tile + 1].to_broadcast([P, P])
                        dec = pool.tensor_tensor(at_dec[:, n, :], mask, log_f, ALU.mult)
                    dec.then_inc(dec_ready, 1)
            with pool.Fori(0, B_OUT - B_G2) as i:
                for a in range(2):
                    fetch(i * 2 + (FT + a))


def _lay_out(v):
    import numpy as np

    f32 = np.float32
    sizes = [BW] * 4 + [FT] + [BW] * 8
    at = np.cumsum([0] + sizes)
    names = ["fq", "fk", "fv", "fg", "fl", "sq", "sk", "sv", "sg", "su", "ug", "lx", "lg"]
    where = {n: int(a) for n, a in zip(names, at)}
    w_in, w_out = v["w_in"][0], v["w_out"][0]

    wall = np.empty((N_BLOCKS, P, NK, BLK), f32)
    order = ["su", "lx", "fq", "sq", "fk", "sk", "fv", "sv", "ug", "lg", "fg", "sg"]
    for n, name in enumerate(order):
        for half in range(BW // BLK):
            a = where[name] + half * BLK
            wall[n * (BW // BLK) + half] = w_in[:, a:a + BLK].reshape(NK, P, BLK).transpose(1, 0, 2)
    rows = np.concatenate([w_out[2 * BW:4 * BW], w_out[0:2 * BW]], axis=0)
    for n in range(N_OUT_BLOCKS):
        wall[N_IN_BLOCKS + n] = rows[:, n * BLK:(n + 1) * BLK].reshape(NK, P, BLK).transpose(1, 0, 2)
    wfg = w_in[:, where["fl"]:where["fl"] + FT].reshape(NK, P, FT).transpose(1, 0, 2)

    by_state = lambda a: a.reshape(BW // HG // 2, 2, STATE).transpose(1, 2, 0).reshape(P, -1)
    by_feature = lambda a: a.reshape(-1, P).T
    par = np.zeros((P, NPAR), f32)

    def put(name, a):
        par[:, PC[name][0]:PC[name][1]] = a

    put("g_pre", by_feature(v["g_pre"][0]))
    put("a_re", by_state(v["ssm_a_re"][0]))
    put("a_im", by_state(v["ssm_a_im"][0]))
    put("log_dt", by_state(np.repeat(v["ssm_log_dt"][0][:, None], STATE, axis=1)))
    put("b_forget", np.broadcast_to(np.tile(v["b_forget"][0], TT), (P, TT * FT)))
    put("ssm_d", by_feature(v["ssm_d"][0]))
    put("lam", by_feature(v["lru_lambda"][0]))
    lru = np.zeros((P, FT, 9), f32)
    for n in range(4):
        lru[:, :, TAP0 + n] = by_feature(v["conv_w"][0][n])
    for n, name in ((CONV_B, "conv_b"), (B_R, "b_rgate"), (B_I, "b_igate"), (B_GLU, "b_glu")):
        lru[:, :, n] = by_feature(v[name][0])
    put("lru", lru.reshape(P, FT * 9))

    bt = np.zeros((FT, P, SJ, 2, P), f32)
    ct = np.zeros((FT, P, SJ, 2, 2 * HG), f32)
    for r, (b, c) in enumerate((("ssm_b_re", "ssm_c_re"), ("ssm_b_im", "ssm_c_im"))):
        for f in range(FT):
            for j in range(SJ):
                for a in range(2):
                    g = f * 2 * SJ + 2 * j + a
                    row = 2 * HG * j + HG * a
                    bt[f, row:row + HG, j, r, a * STATE:(a + 1) * STATE] = v[b][0][g].T
                    ct[f, a * STATE:(a + 1) * STATE, j, r, a * HG:(a + 1) * HG] = v[c][0][g].T
    wglu = v["w_glu"][0].reshape(FT, P, FT, P).transpose(2, 1, 0, 3)
    wri = np.zeros((FT, P, 2, P), f32)
    half = P // 2
    for r, name in enumerate(("w_rgate", "w_igate")):
        for n in range(2 * FT):
            a = (n % 2) * half
            wri[n // 2, a:a + half, r, a:a + half] = v[name][0][n]
    whole = np.ascontiguousarray
    return {"x": whole(v["x"][0]), "par": par, "bt": bt.reshape(FT, P, -1), "ct": ct.reshape(FT, P, -1),
            "wfg": whole(wfg), "wglu": whole(wglu).reshape(FT, P, -1), "wri": wri.reshape(FT, P, -1),
            "gpost": whole(v["g_post"][0]), "wall": wall.reshape(N_BLOCKS, P, NK * BLK)}


def kernel(**inputs):
    import numpy as np
    import concourse.bacc as bacc
    from concourse.bass_utils import run_bass_kernel_spmd

    arrays = _lay_out({n: np.asarray(a) for n, a in inputs.items()})
    nc = bacc.Bacc("TRN2", target_bir_lowering=False, num_devices=1)
    args = [nc.dram_tensor(f"in_{n}", a.shape, mybir.dt.from_np(a.dtype), kind="ExternalInput").ap()
            for n, a in arrays.items()]
    out = nc.dram_tensor("out_0", (T, D), F32, kind="ExternalOutput").ap()
    hybrid_trunk(nc, *args, out)
    r = run_bass_kernel_spmd(nc, [{f"in_{n}": a for n, a in arrays.items()}], core_ids=[0])
    return r.results[0]["out_0"].reshape(1, T, D)
```

```python
import math
from contextlib import ExitStack

import concourse.bass as bass
from concourse import mybir

F32 = mybir.dt.float32
F32R = mybir.dt.float32r
BF16 = mybir.dt.bfloat16
ACT = mybir.ActivationFunctionType
ALU = mybir.AluOpType
AX = mybir.AxisListType

P = 128
D = 4096
T = 256
TT = T // P
NK = D // P
BW = D // 4
FT = BW // P
BLK = 512
JB = BLK // P
KC = 2
CH = NK // KC
CW = KC * BLK
RING = 4
LEAD = RING - 1
STATE, HG = 64, 16
SJ = 4
N_IN_BLOCKS = 24
N_OUT_BLOCKS = D // BLK
N_BLOCKS = N_IN_BLOCKS + N_OUT_BLOCKS
B_SRC, B_QK, B_V, B_G1, B_G2, B_OUT = 0, 4, 12, 16, 20, 24
EPS = 1e-6
QK_SCALE = float(P) ** -0.25
LRU_C = 8.0
ROUND = 1.5 * 2.0 ** 23
TWO_PI = 6.283185
PI_1 = 6.28125
PI_2 = 0.0019350051879882812
PI_3 = 2.0 * math.pi - 6.28125 - 0.0019350051879882812
NEG = -1.0e30
SSM0, LRU0, FOX0, SB0, KEY0 = 0, FT, 2 * FT, 3 * FT, 4 * FT
PC = {}
_at = 0
for _name, _n in (("g_pre", NK), ("a_re", 32), ("a_im", 32), ("log_dt", 32), ("b_forget", TT * FT),
                  ("ssm_d", FT), ("lam", FT), ("lru", FT * 9)):
    PC[_name] = (_at, _at + _n)
    _at += _n
NPAR = _at
TAP0, CONV_B, B_R, B_I, LOG_A, B_GLU = 0, 4, 5, 6, 7, 8


def hybrid_trunk(nc, x, par, bt, ct, wfg, wglu, wri, gpost, wall, out):
    ctx = ExitStack()
    with ctx:
        def sb(name, shape, dt=F32):
            return ctx.enter_context(nc.sbuf_tensor(name, shape, dt))

        def sem(name):
            return ctx.enter_context(nc.semaphore(name))

        acts = sb("acts", [P, NK, 2 * T], F32R)
        w_raw = sb("w_raw", [P, RING, CW])
        w_hi = sb("w_hi", [P, RING, CW], F32R)
        w_lo = sb("w_lo", [P, RING, CW], F32R)
        br = sb("br", [P, 6 * FT, T])
        vals = sb("vals", [P, TT, 2 * BW])
        cross = sb("cross", [P, JB, T])
        scr = sb("scr", [P, 5120])
        pars = sb("pars", [P, NPAR])
        s5par = sb("s5par", [P, FT, 5 * SJ])
        small = sb("small", [P, 178])
        wf = sb("wf", [P, 2 * NK * FT + P], F32R)
        logf = sb("logf", [P, FT, TT])
        later = sb("later", [P, 2 * P])
        upto = sb("upto", [P, P])
        ident = sb("ident", [P, P])
        ident_b = sb("ident_b", [P, P], BF16)
        causal_b = sb("causal_b", [P, P], BF16)
        strict_b = sb("strict_b", [P, P], BF16)

        main = ctx.enter_context(nc.psum_tensor("main", [P, 4, BLK], F32))
        side = ctx.enter_context(nc.psum_tensor("side", [P, 4, BLK], F32))

        x_rows = br[:, 0:32, :].rearrange("p (a k) t -> p a (k t)", a=TT)
        mixed = br[:, 0:32, :].rearrange("p (a k) t -> p a (k t)", a=TT)
        g_rows = br[:, 32:48, :].rearrange("p k t -> p (k t)")
        x_late = [vals[:, :, :].rearrange("p a n -> p (a n)"), scr[:, 0:D]]
        wf_raw = scr[:, 0:256].rearrange("p (k n) -> p k n", k=NK)
        s5tmp = scr[:, 256:800].rearrange("p (n f) -> p n f", n=17)
        vflat = vals[:, :, :].rearrange("p a n -> p (a n)")
        s5_m1, s5_m2, s5_g = vflat[:, 0:512], vflat[:, 512:1024], vflat[:, 1024:1536]
        s5_h = [vflat[:, 1536:2048], vflat[:, 2048:2560]]
        s5_sin = [vflat[:, 2560:3072], vflat[:, 3072:3584]]
        s5_cos = [vflat[:, 3584:3840], vflat[:, 3840:4096]]
        steps_t = scr[:, 3328:3328 + T]
        s5_bt = scr[:, 0:1024].rearrange("p (j r s) -> p j r s", j=SJ, r=2)
        s5_ct = scr[:, 1024:1280].rearrange("p (j r h) -> p j r h", j=SJ, r=2)
        s5_cp = scr[:, 1280:1536].rearrange("p (j r h) -> p j r h", j=SJ, r=2)
        s5_u = scr[:, 1536:1792]
        s5_a, s5_k, s5_f, s5_q = (scr[:, 1792 + T * n:1792 + T * (n + 1)] for n in range(4))
        s5_c = [scr[:, 2816 + 128 * n:2816 + 128 * (n + 1)].rearrange("p (j h) -> p j h", j=SJ)
                for n in range(4)]
        glu_w = scr[:, 0:1024].rearrange("p (k n) -> p k n", k=FT)
        lru_w = scr[:, 1024:1280].rearrange("p (r n) -> p r n", r=2)
        lru_x, lru_xc = scr[:, 1280:1536], scr[:, 1536:1792]
        lru_ri = scr[:, 1792:2304]
        lru_a, lru_th, lru_s = scr[:, 2304:2560], scr[:, 2560:2816], scr[:, 2816:3072]
        glu_z = scr[:, 3072:5120].rearrange("p (n t) -> p n t", n=FT)
        at_q = scr[:, 0:256]
        at_v = scr[:, 256:512].rearrange("p (a d) -> p a d", a=TT)
        at_dec = scr[:, 512:896].rearrange("p (n t) -> p n t", n=3)
        at_p, at_pt = scr[:, 896:1280], scr[:, 1280:1664]
        at_e, at_sp, at_r = scr[:, 1664:2048], scr[:, 2048:2432], scr[:, 2432:2816]
        sumsq, ms, rs_a, rs_b, rstd = (small[:, 4 * n:4 * n + 4] for n in range(5))
        s5_now = small[:, 20:40]
        lru_now = small[:, 40:49]
        lf_now = small[:, 50:54]
        ones = later[:, 0:1].to_broadcast([P, T])
        row_max, row_sum, row_inv = small[:, 54:56], small[:, 56:58], small[:, 58:60]
        ss_new, ss_all = small[:, 60:62], small[:, 62:64]
        fl_cross, fl_rows = scr[:, 3584:3840], scr[:, 3840:4096]
        fl_z, fl_e = (small[:, 112 + 16 * n:128 + 16 * n].rearrange("p (a n) -> p a n", a=TT)
                      for n in range(2))
        log_a = [small[:, 144 + 8 * n:152 + 8 * n] for n in range(4)]

        def col(name, n=None):
            a, b = PC[name]
            return pars[:, a:b] if n is None else pars[:, a + n:a + n + 1]

        lru_par = col("lru").rearrange("p (f n) -> p f n", f=FT)
        halves = [(a, h) for a in range(TT) for h in range(2)]
        HW = D // 2

        x_in = [sem(f"x_in{n}") for n in range(4)]
        par_in, wf_in = sem("par_in"), sem("wf_in")
        raw_in = [sem(f"raw_in{n}") for n in range(RING)]
        hi_ready, lo_ready = sem("hi_ready"), sem("lo_ready")
        w_used = sem("w_used")
        fm_done, tm_done = sem("fm_done"), sem("tm_done")
        bank_cross = sem("bank_cross")
        bank_free = sem("bank_free")
        squared, rms_act, rms_dve = sem("squared"), sem("rms_act"), sem("rms_dve")
        x_scaled = sem("x_scaled")
        xt_done, u_hi, u_lo = sem("xt_done"), sem("u_hi"), sem("u_lo")
        consts, const_steps = sem("consts"), sem("const_steps")
        pa, pd = sem("pa"), sem("pd")
        wf_hi, wf_lo0, wf_lo = sem("wf_hi"), sem("wf_lo0"), sem("wf_lo")
        fl_mm, fl_act, fl_dve = sem("fl_mm"), sem("fl_act"), sem("fl_dve")
        bt_in, ct_in, p5_ready, su_ready = sem("bt_in"), sem("ct_in"), sem("p5_ready"), sem("su_ready")
        s5_tab, s5_frac, s5_trig, s5_cosd = sem("s5_tab"), sem("s5_frac"), sem("s5_trig"), sem("s5_cosd")
        s5_cq, s5_cprime = sem("s5_cq"), sem("s5_cprime")
        s5_bmm, s5_cmm, s5_dve, s5_done, s5_y = (sem(n) for n in
                                                 ("s5_bmm", "s5_cmm", "s5_dve", "s5_done", "s5_y"))
        gelu_done, wg_in, wr_in = sem("gelu_done"), sem("wg_in"), sem("wr_in")
        lru_v, lru_mm, lru_act, lru_done = sem("lru_v"), sem("lru_mm"), sem("lru_act"), sem("lru_done")
        glu_mm, glu_sig, glu_applied = sem("glu_mm"), sem("glu_sig"), sem("glu_applied")
        lf_ready, dec_ready, qs_ready, vs_ready = (sem(n) for n in
                                                   ("lf_ready", "dec_ready", "qs_ready", "vs_ready"))
        at_scores, at_max, at_exp, at_inv, at_norm = (sem(n) for n in
                                                      ("at_scores", "at_max", "at_exp", "at_inv", "at_norm"))
        at_tr, at_ptd, at_out, at_o = sem("at_tr"), sem("at_ptd"), sem("at_out"), sem("at_o")
        sb_act, sb_dve = sem("sb_act"), sem("sb_dve")
        gate_silu, gate_used = sem("gate_silu"), sem("gate_used")
        mix_hi, mix_lo = sem("mix_hi"), sem("mix_lo")
        g_in, xl_in = sem("g_in"), [sem("xl_in0"), sem("xl_in1")]
        o_sq, o_ss = sem("o_sq"), sem("o_ss")
        fin_act, fin_dve, fin_sum, stored = (sem(n) for n in ("fin_act", "fin_dve", "fin_sum", "stored"))

        N_CONST = 8
        FOX_AT, SB_AT = (3, 8), (0, 7)
        N_FM = B_V + B_OUT - B_G1
        V_READ = B_V * JB + (B_G1 - B_V) * TT
        block = ctx.enter_context(nc.Block())

        @block.sync
        def _(sp):
            for n, (a, h) in enumerate(halves):
                sp.dma_start(x_rows[:, a, h * HW:(h + 1) * HW],
                             x[a * P:(a + 1) * P, h * HW:(h + 1) * HW]).then_inc(x_in[n], 16)

            def load(b, c):
                sp.dma_start(w_raw[:, c % RING, :],
                             wall[bass.ds(b, 1), :, c * CW:(c + 1) * CW].rearrange("b p n -> (b p) n")
                             ).then_inc(raw_in[c % RING], 16)

            for c in range(RING):
                load(0, c)
            with sp.Fori(0, N_BLOCKS - 1) as b:
                for c in range(CH):
                    sp.wait_ge(lo_ready, b * CH + c + 1)
                    load(b + (c + RING) // CH, (c + RING) % CH)
            for c in range(CH - RING):
                sp.wait_ge(lo_ready, (N_BLOCKS - 1) * CH + c + 1)
                load(N_BLOCKS - 1, c + RING)
            for n, (a, h) in enumerate(halves):
                sp.wait_ge(fin_sum, n + 1)
                sp.dma_start(out[a * P:(a + 1) * P, h * HW:(h + 1) * HW],
                             mixed[:, a, h * HW:(h + 1) * HW]).then_inc(stored, 16)
            sp.wait_ge(stored, 16 * len(halves))

        @block.tensor
        def _(pe):
            def chunk_fm(b, m, c):
                pe.wait_ge(lo_ready, b * CH + c + 1)
                s = c % RING
                for j in range(JB):
                    if c == 0 and not isinstance(m, int):
                        pe.wait_ge(bank_free, m * JB + (j + 1 - JB))
                    for kk in range(KC):
                        k, at = KC * c + kk, kk * BLK + j * P
                        pe.matmul(main[:, j, :], w_hi[:, s, at:at + P], acts[:, k, :],
                                  start=(k == 0), stop=False)
                        mm = pe.matmul(main[:, j, T:2 * T], w_lo[:, s, at:at + P], acts[:, k, 0:T],
                                       start=False, stop=(k == NK - 1))
                    if c == CH - 1 and j < JB - 1:
                        mm.then_inc(fm_done, 1)
                mm.then_inc(w_used, 1)

            def chunk_tm(b, c, bank0, free, mixed_parts=False):
                pe.wait_ge(lo_ready, b * CH + c + 1)
                if mixed_parts:
                    pe.wait_ge(mix_lo, KC * (c + 1))
                s = c % RING
                for a in range(TT):
                    if c == 0:
                        free(a)
                    for kk in range(KC):
                        k = KC * c + kk
                        u_h, u_l = acts[:, k, a * P:(a + 1) * P], acts[:, k, T + a * P:T + (a + 1) * P]
                        wh, wl = w_hi[:, s, kk * BLK:(kk + 1) * BLK], w_lo[:, s, kk * BLK:(kk + 1) * BLK]
                        pe.matmul(main[:, bank0 + a, :], u_h, wh, start=(k == 0), stop=False)
                        pe.matmul(main[:, bank0 + a, :], u_h, wl, start=False, stop=False)
                        mm = pe.matmul(main[:, bank0 + a, :], u_l, wh, start=False, stop=(k == NK - 1))
                    if c == CH - 1 and a < TT - 1:
                        mm.then_inc(tm_done, 1)
                mm.then_inc(w_used, 1)

            def turn(k):
                if k == 0:
                    pe.wait_ge(x_scaled, 3)
                if k == NK // 2:
                    pe.wait_ge(x_scaled, 4)
                if k >= 4:
                    pe.wait_ge(u_lo, k - 3)
                for a in range(TT):
                    tr = pe.transpose(side[:, k % 4, a * P:(a + 1) * P], x_rows[:, a, k * P:(k + 1) * P],
                                      ident[:, :])
                tr.then_inc(xt_done, 1)

            pe.wait_ge(consts, N_CONST)
            for k in range(4):
                turn(k)
            for c in range(CH):
                for k in range(KC * c + 4, min(KC * (c + 1) + 4, NK)):
                    turn(k)
                pe.wait_ge(u_lo, KC * (c + 1))
                chunk_fm(0, 0, c)

            with pe.Fori(1, B_QK - B_SRC) as i:
                for c in range(CH):
                    chunk_fm(i, i, c)

            pe.wait_ge(wf_lo, 1)
            for k in range(NK):
                pe.matmul(side[:, 3, :], wf[:, k * FT:k * FT + P], acts[:, k, :], start=(k == 0), stop=False)
                mm = pe.matmul(side[:, 3, T:2 * T], wf[:, NK * FT + k * FT:NK * FT + k * FT + P],
                               acts[:, k, 0:T], start=False, stop=(k == NK - 1))
            mm.then_inc(fl_mm, 1)

            with pe.Fori(0, B_V - B_QK) as i:
                def s5_inputs(j):
                    if j == 0:
                        pe.wait_ge(su_ready, i + 1)
                        pe.wait_ge(bt_in, i * 16 + 16)
                    if j >= 2:
                        pe.wait_ge(s5_done, i * SJ + j - 1)
                    for r in range(2):
                        mm = pe.matmul(side[:, j % 2, r * T:(r + 1) * T], s5_bt[:, j, r, :], s5_u[:, :],
                                       start=True, stop=True)
                    mm.then_inc(s5_bmm, 1)

                for c in range(CH):
                    if c == 2:
                        s5_inputs(0)
                    if c in (4, 7, 10):
                        s5_inputs(c // 3)
                    if c % 3 == 0 and 2 <= c // 3:
                        j = c // 3 - 2
                        if j == 0:
                            pe.wait_ge(s5_cprime, i + 1)
                        pe.wait_ge(s5_done, i * SJ + j + 1)
                        for r in range(2):
                            mm = pe.matmul(side[32 * j:32 * j + 32, 2, 0:T], s5_cp[:, j, r, :],
                                           s5_h[j % 2][:, r * T:(r + 1) * T], start=(r == 0), stop=(r == 1))
                        mm.then_inc(s5_cmm, 1)
                    chunk_fm(i + B_QK, i + B_QK, c)

            pe.wait_ge(fl_dve, 1)
            for a in range(TT):
                mm = pe.transpose(side[:, 3, a * FT:(a + 1) * FT], fl_rows[0:FT, a * P:(a + 1) * P],
                                  ident[0:FT, 0:FT])
            mm.then_inc(fl_mm, 1)

            with pe.Fori(0, (B_G1 - B_V) // 2) as ii:
                for u in range(2):
                    i = ii * 2 + u

                    def v_bank(a):
                        pe.wait_ge(bank_free, (B_V - 1) * JB + 2 * u + a + 1)
                        pe.wait_ge(bank_cross, ii * (2 * TT) + ((B_V - 1) * JB + 2 * u + a + 1))

                    for c in range(CH):
                        for a, at in ((0, 0), (1, 7)):
                            if c == at + 3:
                                pe.wait_ge(wr_in, ii * 64 + (32 * u + 16 * (a + 1)))
                                pe.wait_ge(lru_v, ii * 36 + (18 * u + 9 * a + 6))
                                for r in range(2):
                                    mm = pe.matmul(side[:, 0, r * T:(r + 1) * T], lru_w[:, r, :], lru_xc[:, :],
                                                   start=True, stop=True)
                                mm.then_inc(lru_mm, 1)
                                pe.wait_ge(wg_in, ii * 64 + (32 * u + 16 * (a + 1)))
                                pe.wait_ge(gelu_done, FT)
                                for k in range(FT):
                                    mm = pe.matmul(side[:, 1, 0:T], glu_w[:, k, :], br[:, SSM0 + k, :],
                                                   start=(k == 0), stop=(k == FT - 1))
                                mm.then_inc(glu_mm, 1)
                        chunk_tm(i + B_V, c, 2 * u, v_bank)

            def transposes(h):
                pe.transpose(side[:, 1, 0:P], at_p[:, 0:P], ident[:, :])
                pe.transpose(side[:, 1, P:2 * P], at_p[:, P:2 * P], ident[:, :])
                pe.transpose(side[:, 1, 2 * P:3 * P], at_p[:, 2 * P:3 * P], ident[:, :]).then_inc(at_tr, 1)

            def weighted_values(h):
                pe.wait_ge(at_ptd, h + 1)
                pe.wait_ge(vs_ready, h + 1)
                pe.matmul(side[:, 2, 0:T], at_v[:, 0, :], at_pt[:, 0:T], start=True, stop=False)
                pe.matmul(side[:, 2, P:T], at_v[:, 1, :], at_pt[:, T:3 * P], start=False,
                          stop=True).then_inc(at_out, 1)

            pe.wait_ge(bank_cross, V_READ)
            with pe.Fori(0, B_G2 - B_G1) as i:
                for c in range(CH):
                    for a in range(2):
                        h = i * 2 + a
                        if c == FOX_AT[a]:
                            pe.wait_ge(qs_ready, h + 1)
                            pe.wait_ge(dec_ready, h + 1)
                            key = br[:, KEY0 + h, :]
                            q0, q1 = side[:, 0, 0:P], side[:, 0, P:3 * P]
                            pe.matmul(q0, at_q[:, 0:P], key[:, 0:P], start=True, stop=False)
                            pe.matmul(q0, at_dec[:, 0, :], later[:, P:2 * P], start=False, stop=False)
                            pe.matmul(q0, ident_b[:, :], causal_b[:, :], start=False, stop=True)
                            pe.matmul(q1, at_q[:, P:T], key[:, :], start=True, stop=False)
                            pe.matmul(side[:, 0, P:2 * P], at_dec[:, 1, :], later[:, P:2 * P],
                                      start=False, stop=False)
                            pe.matmul(q1, at_dec[:, 2, :], later[:, :], start=False, stop=False)
                            pe.matmul(side[:, 0, 2 * P:3 * P], ident_b[:, :], causal_b[:, :],
                                      start=False, stop=True).then_inc(at_scores, 1)
                        if c == FOX_AT[a] + 3:
                            pe.wait_ge(at_norm, i * 4 + 2 * a + 2)
                            transposes(h)
                        if c == FOX_AT[a] + 5:
                            weighted_values(h)
                    chunk_fm(i + B_G1, i + B_V, c)

            with pe.Fori(0, B_OUT - B_G2) as i:
                for c in range(CH):
                    for a in range(2):
                        h = i * 2 + (FT + a)
                        if c == SB_AT[a]:
                            pe.wait_ge(qs_ready, h + 1)
                            key = br[:, KEY0 + h, :]
                            q0, q1 = side[:, 0, 0:P], side[:, 0, P:3 * P]
                            pe.matmul(q0, at_q[:, 0:P], key[:, 0:P], start=True, stop=False)
                            pe.matmul(q0, ident_b[:, :], strict_b[:, :], start=False, stop=True)
                            pe.matmul(q1, at_q[:, P:T], key[:, :], start=True, stop=False)
                            pe.matmul(side[:, 0, 2 * P:3 * P], ident_b[:, :], strict_b[:, :],
                                      start=False, stop=True).then_inc(at_scores, 1)
                        if c == SB_AT[a] + 5:
                            pe.wait_ge(at_exp, i * 2 + (2 * FT + a + 1))
                            transposes(h)
                        if c == SB_AT[a] + 7:
                            weighted_values(h)
                    chunk_fm(i + B_G2, i + (B_V + B_G2 - B_G1), c)

            def out_block(n, u):
                for c in range(CH):
                    chunk_tm(n + B_OUT, c, 2 * u,
                             lambda a: pe.wait_ge(bank_free, n * TT + (N_FM * JB - 2 * TT + a + 1)),
                             mixed_parts=isinstance(n, int) and n == 0)

            out_block(0, 0)
            with pe.Fori(0, (N_OUT_BLOCKS - 2) // 2) as ii:
                out_block(ii * 2 + 1, 1)
                out_block(ii * 2 + 2, 0)
            out_block(N_OUT_BLOCKS - 1, 1)

        @block.scalar
        def _(act):
            def high(b, c):
                act.wait_ge(raw_in[c % RING], b * (16 * CH // RING) + 16 * (c // RING + 1))
                if not (isinstance(b, int) and b * CH + c < RING):
                    act.wait_ge(w_used, b * CH + (c - RING + 1))
                act.activation(w_hi[:, c % RING, :], w_raw[:, c % RING, :], ACT.Copy).then_inc(hi_ready, 1)

            def fm_wait(b, m, j):
                if j < JB - 1:
                    act.wait_ge(fm_done, m * (JB - 1) + j + 1)
                else:
                    act.wait_ge(w_used, b * CH + CH)

            def copy_cross(b, m, scale):
                for j in range(JB):
                    fm_wait(b, m, j)
                    act.activation(cross[:, j, :], main[:, j, T:2 * T], ACT.Copy,
                                   scale=scale).then_inc(bank_cross, 1)

            act.dma_start(wf_raw, wfg).then_inc(wf_in, 16)
            act.dma_start(pars[:, :], par).then_inc(par_in, 16)
            act.wait_ge(wf_in, 16)
            act.activation(wf[:, 0:NK * FT], wf_raw.rearrange("p k n -> p (k n)"), ACT.Copy).then_inc(wf_hi, 1)
            for n, (a, h) in enumerate(halves):
                act.wait_ge(x_in[n], 16)
                if n:
                    act.wait_ge(squared, n)
                act.activation(scr[:, 1024:1024 + HW], x_rows[:, a, h * HW:(h + 1) * HW],
                               ACT.Square, accum_out=sumsq[:, n:n + 1]).then_inc(squared, 1)
                if h == 1:
                    act.wait_ge(rms_dve, 7 * a + 2)
                    act.activation(rs_a[:, a:a + 1], ms[:, a:a + 1], ACT.Sqrt).then_inc(rms_act, 1)

            def take_high(k):
                act.wait_ge(xt_done, k + 1)
                act.activation(acts[:, k, 0:T], side[:, k % 4, 0:T], ACT.Copy,
                               scale=col("g_pre", k)).then_inc(u_hi, 1)

            tmp = lambda n: s5tmp[:, n, :]
            act.wait_ge(par_in, 16)
            for k in range(4):
                take_high(k)
                if k < LEAD:
                    high(0, k)
            for c in range(CH):
                for k in range(KC * c + 4, min(KC * (c + 1) + 4, NK)):
                    take_high(k)
                high(0, c + LEAD)
                if c == 2:
                    act.activation(tmp(0), col("log_dt"), ACT.Exp).then_inc(pa, 1)
                    act.activation(log_a[0], col("lam"), ACT.Abs).then_inc(pa, 1)
                    act.wait_ge(pa, 2)
                    act.activation(log_a[0], log_a[0], ACT.Exp, scale=-1.0).then_inc(pa, 1)
                if c == 6:
                    act.wait_ge(pd, 9)
                    act.activation(tmp(4), tmp(1), ACT.Exp).then_inc(pa, 1)
                    act.activation(tmp(5), tmp(1), ACT.Tanh, scale=0.5).then_inc(pa, 1)
                if c == 8:
                    act.activation(tmp(6), tmp(3), ACT.Sin, scale=TWO_PI).then_inc(pa, 1)
                    act.activation(tmp(7), tmp(3), ACT.Sin, scale=TWO_PI / 2).then_inc(pa, 1)
                if c == CH - 1:
                    copy_cross(0, 0, 1.0)

            with act.Fori(1, B_QK - B_SRC) as i:
                for c in range(CH):
                    high(i, c + LEAD)
                    if c == CH - 1:
                        copy_cross(i, i, 1.0)

            act.wait_ge(fl_mm, 1)
            act.activation(fl_cross[0:FT, :], side[0:FT, 3, T:2 * T], ACT.Copy).then_inc(fl_act, 1)

            with act.Fori(0, B_V - B_QK) as i:
                for c in range(CH):
                    high(i + B_QK, c + LEAD)
                    if c == 0:
                        act.dma_start(s5_bt, bt[bass.ds(i, 1), :, :].rearrange("f p n -> (f p) n")
                                      .rearrange("p (j r s) -> p j r s", j=SJ, r=2)).then_inc(bt_in, 16)
                        act.dma_start(s5_ct, ct[bass.ds(i, 1), :, :].rearrange("f p n -> (f p) n")
                                      .rearrange("p (j r h) -> p j r h", j=SJ, r=2)).then_inc(ct_in, 16)
                    if c % 3 == 0 and c // 3 < SJ:
                        j = c // 3
                        act.wait_ge(s5_frac, i * SJ + j + 1)
                        if j >= 2:
                            act.wait_ge(s5_done, i * SJ + j - 1)
                        act.activation(s5_sin[j % 2][:, 0:T], s5_f, ACT.Sin, scale=TWO_PI).then_inc(s5_trig, 1)
                        act.activation(s5_sin[j % 2][:, T:2 * T], s5_f, ACT.Sin, scale=-TWO_PI
                                       ).then_inc(s5_trig, 1)
                        act.activation(s5_q, s5_f, ACT.Sin, scale=TWO_PI / 2).then_inc(s5_trig, 1)
                        act.wait_ge(s5_trig, i * 4 * SJ + 4 * j + 3)
                        act.activation(s5_q, s5_q, ACT.Square, scale=math.sqrt(2.0)).then_inc(s5_trig, 1)
                    if c == CH - 1:
                        copy_cross(i + B_QK, i + B_QK, QK_SCALE)

            act.wait_ge(s5_y, FT)
            for f in range(FT):
                act.activation(br[:, SSM0 + f, :], br[:, SSM0 + f, :], ACT.Gelu_apprx_tanh).then_inc(gelu_done, 1)

            with act.Fori(0, (B_G1 - B_V) // 2) as ii:
                for u in range(2):
                    i = ii * 2 + u
                    for c in range(CH):
                        high(i + B_V, c + LEAD)
                        for a, at in ((0, 0), (1, 7)):
                            f = i * 2 + a
                            if c == at:
                                act.dma_start(glu_w, wglu[bass.ds(f, 1), :, :].rearrange("f p n -> (f p) n")
                                              .rearrange("p (k n) -> p k n", k=FT)).then_inc(wg_in, 16)
                                act.dma_start(lru_w, wri[bass.ds(f, 1), :, :].rearrange("f p n -> (f p) n")
                                              .rearrange("p (r n) -> p r n", r=2)).then_inc(wr_in, 16)
                            if c == at + 3:
                                act.wait_ge(lru_mm, f + 1)
                                act.activation(lru_ri[:, 0:T], side[:, 0, 0:T], ACT.Sigmoid,
                                               bias=lru_now[:, B_R:B_R + 1]).then_inc(lru_act, 1)
                                act.activation(lru_ri[:, T:2 * T], side[:, 0, T:2 * T], ACT.Sigmoid,
                                               bias=lru_now[:, B_I:B_I + 1]).then_inc(lru_act, 1)
                                act.wait_ge(lru_act, i * 12 + 6 * a + 1)
                                act.activation(lru_a, lru_ri[:, 0:T], ACT.Exp,
                                               scale=lru_now[:, LOG_A:LOG_A + 1]).then_inc(lru_act, 1)
                                act.activation(lru_th, lru_ri[:, 0:T], ACT.Tanh,
                                               scale=lru_now[:, LOG_A:LOG_A + 1]).then_inc(lru_act, 1)
                                act.wait_ge(lru_act, i * 12 + 6 * a + 3)
                                act.activation(lru_s, lru_a, ACT.Square).then_inc(lru_act, 1)
                            if c == at + 5:
                                act.wait_ge(lru_v, i * 18 + 9 * a + 7)
                                act.activation(lru_s, lru_s, ACT.Sqrt, scale=-1.0).then_inc(lru_act, 1)
                                act.wait_ge(glu_mm, f + 1)
                                act.wait_ge(par_in, 16)
                                act.activation(glu_z[:, f, :], side[:, 1, 0:T], ACT.Sigmoid,
                                               bias=lru_now[:, B_GLU:B_GLU + 1]).then_inc(glu_sig, 1)
                        if c == CH - 1:
                            for a in range(TT):
                                if a < TT - 1:
                                    act.wait_ge(tm_done, i * (TT - 1) + a + 1)
                                else:
                                    act.wait_ge(w_used, (i + B_V) * CH + CH)
                                act.wait_ge(gelu_done, FT)
                                act.activation(vals[:, a, bass.ds(i * BLK, BLK)], main[:, 2 * u + a, :],
                                               ACT.Copy).then_inc(bank_cross, 1)

            def silus(m):
                for j in range(JB):
                    act.wait_ge(bank_free, m * JB + j + 1)
                    act.activation(cross[:, j, :], cross[:, j, :], ACT.Silu).then_inc(gate_silu, 1)

            def copy_weights(h):
                act.wait_ge(at_tr, h + 1)
                act.activation(at_pt, side[:, 1, 0:3 * P], ACT.Copy).then_inc(at_ptd, 1)

            act.wait_ge(fl_dve, 2)
            act.activation(fl_e, fl_z, ACT.Abs).then_inc(fl_act, 1)
            act.wait_ge(fl_act, 2)
            act.activation(fl_e, fl_e, ACT.Exp, scale=-1.0).then_inc(fl_act, 1)
            act.wait_ge(fl_act, 3)
            act.activation(fl_e, fl_e, ACT.Ln, bias=1.0).then_inc(fl_act, 1)

            with act.Fori(0, B_G2 - B_G1) as i:
                for c in range(CH):
                    high(i + B_G1, c + LEAD)
                    for a in range(2):
                        h = i * 2 + a
                        if c == FOX_AT[a] + 1:
                            act.wait_ge(at_max, h + 1)
                            act.activation(at_p[:, 0:P], side[:, 0, 0:P], ACT.Exp, bias=row_max[:, 0:1],
                                           accum_out=row_sum[:, 0:1]).then_inc(at_exp, 1)
                            act.activation(at_p[:, P:3 * P], side[:, 0, P:3 * P], ACT.Exp, bias=row_max[:, 1:2],
                                           accum_out=row_sum[:, 1:2]).then_inc(at_exp, 1)
                        if c == FOX_AT[a] + 4:
                            copy_weights(h)
                    if c == CH - 1:
                        copy_cross(i + B_G1, i + B_V, 1.0)
                        silus(i + B_V)

            def mix_high(c):
                for k in range(KC * c, KC * (c + 1)):
                    act.wait_ge(gate_used, k + 1)
                    act.activation(acts[:, k, 0:T], br[:, k, :], ACT.Copy).then_inc(mix_hi, 1)

            def sb_block(i):
                for c in range(CH):
                    high(i + B_G2, c + LEAD)
                    if isinstance(i, int) and 0 < c < CH - 1:
                        act.wait_ge(w_used, (B_OUT - 1) * CH + c)
                        mix_high(c - 1)
                    for a in range(2):
                        h = i * 2 + (FT + a)
                        if c == SB_AT[a] + 1:
                            act.wait_ge(at_scores, h + 1)
                            act.activation(at_e, side[:, 0, 0:3 * P], ACT.Abs).then_inc(sb_act, 1)
                            act.wait_ge(sb_act, i * 6 + 3 * a + 1)
                            act.activation(at_e, at_e, ACT.Exp, scale=-1.0).then_inc(sb_act, 1)
                            act.wait_ge(sb_act, i * 6 + 3 * a + 2)
                            act.activation(at_e, at_e, ACT.Ln, bias=1.0).then_inc(sb_act, 1)
                        if c == SB_AT[a] + 3:
                            act.wait_ge(sb_dve, i * 8 + 4 * a + 4)
                            act.activation(at_p, at_e, ACT.Exp).then_inc(at_exp, 1)
                        if c == SB_AT[a] + 5:
                            copy_weights(h)
                    if c == CH - 1:
                        copy_cross(i + B_G2, i + (B_V + B_G2 - B_G1), 1.0)
                        silus(i + (B_V + B_G2 - B_G1))

            with act.Fori(0, B_OUT - B_G2 - 1) as i:
                sb_block(i)
            sb_block(B_OUT - B_G2 - 1)

            def squares(n, u):
                for a in range(TT):
                    if a < TT - 1:
                        act.wait_ge(tm_done, n * (TT - 1) + (B_G1 - B_V) * (TT - 1) + a + 1)
                    else:
                        act.wait_ge(w_used, (n + B_OUT) * CH + CH)
                    if not (isinstance(n, int) and n == 0):
                        act.wait_ge(o_ss, n)
                    act.activation(side[:, a, :], main[:, 2 * u + a, :], ACT.Square,
                                   accum_out=ss_new[:, a:a + 1]).then_inc(o_sq, 1)

            act.wait_ge(at_o, 2 * FT)
            act.wait_ge(w_used, B_OUT * CH)
            act.dma_start(g_rows, gpost.partition_broadcast(P)).then_inc(g_in, 16)
            for a in range(TT):
                act.dma_start(x_late[a], x[a * P:(a + 1) * P, :]).then_inc(xl_in[a], 16)
            def out_block(n, u):
                for c in range(CH):
                    if not (isinstance(n, int) and n == N_OUT_BLOCKS - 1 and c + LEAD >= CH):
                        high(n + B_OUT, c + LEAD)
                    if isinstance(n, int) and n == 0 and c < 2:
                        mix_high(c + CH - 2)
                    if c == CH - 1:
                        squares(n, u)

            out_block(0, 0)
            with act.Fori(0, (N_OUT_BLOCKS - 2) // 2) as ii:
                out_block(ii * 2 + 1, 1)
                out_block(ii * 2 + 2, 0)
            out_block(N_OUT_BLOCKS - 1, 1)
            act.wait_ge(fin_dve, 1)
            act.activation(rs_a[:, 0:TT], ms[:, 0:TT], ACT.Sqrt).then_inc(fin_act, 1)

        @block.vector
        def _(dve):
            def low(b, c):
                dve.wait_ge(hi_ready, b * CH + c + 1)
                if not (isinstance(b, int) and b * CH + c < RING):
                    dve.wait_ge(w_used, b * CH + (c - RING + 1))
                dve.tensor_tensor(w_lo[:, c % RING, :], w_raw[:, c % RING, :],
                                  w_hi[:, c % RING, :].bitcast(F32), ALU.subtract).then_inc(lo_ready, 1)

            tmp = lambda n: s5tmp[:, n, :]
            kind = lambda n: s5par[:, :, n * SJ:(n + 1) * SJ]
            by_tile = lambda ap: ap.rearrange("p (f j) -> p f j", f=FT)
            are, aim = col("a_re"), col("a_im")
            n_pd = 0

            def stepped(instruction):
                nonlocal n_pd
                instruction.then_inc(pd, 1)
                n_pd += 1
                return n_pd

            def s5_angles():
                dve.wait_ge(pa, 1)
                dve.wait_ge(par_in, 16)
                stepped(dve.tensor_tensor(tmp(1), are, tmp(0), ALU.mult))
                y = stepped(dve.tensor_tensor(tmp(2), aim, tmp(0), ALU.mult))
                dve.wait_ge(pd, y)
                y = stepped(dve.tensor_scalar(tmp(8), tmp(2), 1.0 / (2 * math.pi), ROUND, ALU.mult, ALU.add))
                dve.wait_ge(pd, y)
                y = stepped(dve.tensor_scalar(tmp(9), tmp(8), -ROUND, None, ALU.add))
                dve.wait_ge(pd, y)
                y = stepped(dve.scalar_tensor_tensor(tmp(10), tmp(9), -PI_1, tmp(2), ALU.mult, ALU.add))
                dve.wait_ge(pd, y)
                y = stepped(dve.scalar_tensor_tensor(tmp(11), tmp(9), -PI_2, tmp(10), ALU.mult, ALU.add))
                dve.wait_ge(pd, y)
                y = stepped(dve.scalar_tensor_tensor(tmp(12), tmp(9), -PI_3, tmp(11), ALU.mult, ALU.add))
                dve.wait_ge(pd, y)
                y = stepped(dve.tensor_scalar(tmp(13), tmp(12), 1.0 / (2 * math.pi), 0.5, ALU.mult, ALU.min))
                dve.wait_ge(pd, y)
                y = stepped(dve.tensor_scalar(tmp(3), tmp(13), -0.5, None, ALU.max))
                dve.wait_ge(pd, y)
                stepped(dve.tensor_scalar(kind(0), by_tile(tmp(3)), 1.0, None, ALU.mult))

            def s5_factors():
                dve.wait_ge(pa, 7)
                stepped(dve.tensor_scalar(kind(1), by_tile(tmp(4)), 1.0, None, ALU.mult))
                em = stepped(dve.scalar_tensor_tensor(tmp(8), tmp(4), 1.0, tmp(5), ALU.add, ALU.mult))
                sh = stepped(dve.tensor_tensor(tmp(9), tmp(7), tmp(7), ALU.mult))
                stepped(dve.tensor_tensor(tmp(10), tmp(4), tmp(6), ALU.mult))
                stepped(dve.tensor_tensor(tmp(11), are, are, ALU.mult))
                a2 = stepped(dve.tensor_tensor(tmp(12), aim, aim, ALU.mult))
                dve.wait_ge(pd, a2)
                y = stepped(dve.tensor_scalar(tmp(9), tmp(9), -2.0, None, ALU.mult))
                stepped(dve.tensor_tensor(tmp(13), tmp(11), tmp(12), ALU.add))
                dve.wait_ge(pd, y)
                y = stepped(dve.tensor_tensor(tmp(14), tmp(8), tmp(9), ALU.mult))
                dve.wait_ge(pd, y)
                y = stepped(dve.tensor_tensor(tmp(15), tmp(14), tmp(8), ALU.add))
                stepped(dve.reciprocal(tmp(16), tmp(13)))
                dve.wait_ge(pd, y)
                y = stepped(dve.tensor_tensor(tmp(14), tmp(15), tmp(9), ALU.add))
                dve.wait_ge(pd, y)
                stepped(dve.tensor_tensor(tmp(11), tmp(14), are, ALU.mult))
                stepped(dve.tensor_tensor(tmp(12), tmp(10), aim, ALU.mult))
                stepped(dve.tensor_tensor(tmp(13), tmp(10), are, ALU.mult))
                y = stepped(dve.tensor_tensor(tmp(15), tmp(14), aim, ALU.mult))
                dve.wait_ge(pd, y)
                stepped(dve.tensor_tensor(tmp(11), tmp(11), tmp(12), ALU.add))
                y = stepped(dve.tensor_tensor(tmp(13), tmp(15), tmp(13), ALU.subtract))
                dve.wait_ge(pd, y)
                y = stepped(dve.tensor_tensor(kind(2), by_tile(tmp(11)), by_tile(tmp(16)), ALU.mult))
                stepped(dve.tensor_tensor(kind(4), by_tile(tmp(13)), by_tile(tmp(16)), ALU.mult))
                dve.wait_ge(pd, y)
                stepped(dve.tensor_scalar(kind(3), kind(2), -1.0, None, ALU.mult))

            def lru_decays():
                e, s, s2, q = log_a
                dve.wait_ge(pa, 3)
                y = stepped(dve.tensor_scalar(s, e, 2.0, None, ALU.add))
                dve.wait_ge(pd, y)
                y = stepped(dve.reciprocal(s2, s))
                dve.wait_ge(pd, y)
                y = stepped(dve.tensor_tensor(s, e, s2, ALU.mult))
                dve.wait_ge(pd, y)
                y = stepped(dve.tensor_tensor(s2, s, s, ALU.mult))
                dve.wait_ge(pd, y)
                y = stepped(dve.tensor_scalar(q, s2, 1.0 / 17, None, ALU.mult))
                for n in range(15, 1, -2):
                    dve.wait_ge(pd, y)
                    y = stepped(dve.scalar_tensor_tensor(q, q, 1.0 / n, s2, ALU.add, ALU.mult))
                dve.wait_ge(pd, y)
                y = stepped(dve.scalar_tensor_tensor(q, q, 1.0, s, ALU.add, ALU.mult))
                y = stepped(dve.tensor_scalar(e, col("lam"), 0.0, LRU_C, ALU.min, ALU.mult))
                dve.wait_ge(pd, y)
                y = stepped(dve.scalar_tensor_tensor(lru_par[:, :, LOG_A:LOG_A + 1].rearrange("p f n -> p (f n)"),
                                                     q, -2.0 * LRU_C, e, ALU.mult, ALU.add))

            dve.memset(wf[:, 2 * NK * FT:2 * NK * FT + P].bitcast(F32), 0.0).then_inc(wf_lo0, 1)
            dve.wait_ge(wf_hi, 1)
            dve.tensor_tensor(wf[:, NK * FT:2 * NK * FT], wf_raw.rearrange("p k n -> p (k n)"),
                              wf[:, 0:NK * FT].bitcast(F32), ALU.subtract).then_inc(wf_lo, 1)

            def root(step, first, cols):
                z = lambda ap: ap[:, cols]
                dve.reciprocal(z(rs_b), z(rs_a)).then_inc(step, 1)
                dve.wait_ge(step, first + 1)
                dve.tensor_tensor(z(rs_a), z(rs_b), z(rs_b), ALU.mult).then_inc(step, 1)
                dve.wait_ge(step, first + 2)
                dve.tensor_tensor(z(rs_a), z(rs_a), z(ms), ALU.mult).then_inc(step, 1)
                dve.wait_ge(step, first + 3)
                dve.tensor_scalar(z(rs_a), z(rs_a), -0.5, 1.5, ALU.mult, ALU.add).then_inc(step, 1)
                dve.wait_ge(step, first + 4)
                dve.tensor_tensor(z(rstd), z(rs_a), z(rs_b), ALU.mult).then_inc(step, 1)
                dve.wait_ge(step, first + 5)

            for a in range(TT):
                one, first = slice(a, a + 1), 7 * a
                dve.wait_ge(squared, 2 * a + 2)
                dve.tensor_tensor(ms[:, one], sumsq[:, 2 * a:2 * a + 1], sumsq[:, 2 * a + 1:2 * a + 2],
                                  ALU.add).then_inc(rms_dve, 1)
                dve.wait_ge(rms_dve, first + 1)
                dve.tensor_scalar(ms[:, one], ms[:, one], 1.0 / D, EPS, ALU.mult, ALU.add).then_inc(rms_dve, 1)
                dve.wait_ge(rms_act, a + 1)
                root(rms_dve, first + 2, one)
                for h in range(2):
                    part = x_rows[:, a, h * HW:(h + 1) * HW]
                    dve.tensor_scalar(part, part, rstd[:, one], None, ALU.mult).then_inc(x_scaled, 1)

            def take_low(k):
                dve.wait_ge(u_hi, k + 1)
                dve.scalar_tensor_tensor(acts[:, k, T:2 * T], side[:, k % 4, 0:T], col("g_pre", k),
                                         acts[:, k, 0:T].bitcast(F32), ALU.mult, ALU.subtract).then_inc(u_lo, 1)

            def sum_bank(i, j):
                dve.wait_ge(bank_cross, i * JB + j + 1)
                dve.tensor_tensor(br[:, i * JB + j, :], main[:, j, 0:T], cross[:, j, :],
                                  ALU.add).then_inc(bank_free, 1)

            dve.wait_ge(par_in, 16)
            for k in range(4):
                take_low(k)
                if k < LEAD:
                    low(0, k)
            for c in range(CH):
                for k in range(KC * c + 4, min(KC * (c + 1) + 4, NK)):
                    take_low(k)
                low(0, c + LEAD)
                if c == 4:
                    s5_angles()
                if c == 10:
                    s5_factors()
                if c == 13:
                    lru_decays()
                if c == CH - 1:
                    for j in range(JB):
                        sum_bank(0, j)
            with dve.Fori(1, B_QK - B_SRC) as i:
                for c in range(CH):
                    low(i, c + LEAD)
                    if c == CH - 1:
                        for j in range(JB):
                            sum_bank(i, j)

            dve.wait_ge(fl_act, 1)
            dve.tensor_tensor(fl_rows[0:FT, :], side[0:FT, 3, 0:T], fl_cross[0:FT, :], ALU.add).then_inc(fl_dve, 1)

            wide = lambda ap: ap.rearrange("p (r t) -> p r t", r=2)
            both = lambda ap: ap.unsqueeze(1).to_broadcast([P, 2, T])
            with dve.Fori(0, B_V - B_QK) as i:
                for c in range(CH):
                    low(i + B_QK, c + LEAD)
                    if c == 0:
                        dve.wait_ge(lo_ready, (i + B_QK) * CH + (LEAD + 1))
                        dve.tensor_scalar(s5_now, s5par[:, i, :], 1.0, None, ALU.mult).then_inc(p5_ready, 1)
                        dve.tensor_scalar(s5_u, br[:, SSM0 + i, :], 1.0, None, ALU.mult).then_inc(su_ready, 1)
                    if c >= 2 and (c - 2) // 3 < SJ:
                        j, part = (c - 2) // 3, (c - 2) % 3
                        g, done = i * SJ + j, i * (7 * SJ) + 7 * j
                        sin, cos, hs = s5_sin[j % 2], s5_cos[j % 2], s5_h[j % 2]
                        bu = side[:, j % 2, :]
                        if part == 0:
                            dve.wait_ge(s5_bmm, g + 1)
                            dve.wait_ge(s5_cosd, g + 1)
                            if j:
                                dve.wait_ge(s5_done, g)
                            dve.tensor_tensor(wide(s5_m1), wide(bu), both(cos), ALU.mult).then_inc(s5_dve, 1)
                            dve.tensor_tensor(wide(s5_m2), wide(bu)[:, ::-1, :], wide(sin),
                                              ALU.mult).then_inc(s5_dve, 1)
                            dve.wait_ge(s5_dve, done + 2)
                            dve.tensor_tensor(s5_m1, s5_m1, s5_m2, ALU.add).then_inc(s5_dve, 1)
                        if part == 1:
                            radius = s5_now[:, SJ + j:SJ + j + 1].to_broadcast([P, T])
                            dve.wait_ge(p5_ready, i + 1)
                            dve.wait_ge(s5_dve, done + 3)
                            for r in range(2):
                                dve.tensor_tensor_scan(s5_g[:, r * T:(r + 1) * T], radius,
                                                       s5_m1[:, r * T:(r + 1) * T], 0.0,
                                                       ALU.mult, ALU.add).then_inc(s5_dve, 1)
                        if part == 2:
                            dve.wait_ge(s5_dve, done + 5)
                            dve.tensor_tensor(wide(s5_m1), wide(s5_g), both(cos), ALU.mult).then_inc(s5_dve, 1)
                            dve.tensor_tensor(wide(s5_m2), wide(s5_g)[:, ::-1, :], wide(sin),
                                              ALU.mult).then_inc(s5_dve, 1)
                            dve.wait_ge(s5_dve, done + 7)
                            if j >= 2:
                                dve.wait_ge(s5_cmm, i * SJ + j - 1)
                            dve.tensor_tensor(hs, s5_m1, s5_m2, ALU.subtract).then_inc(s5_done, 1)
                    if c == CH - 1:
                        dve.wait_ge(s5_cmm, i * SJ + SJ)
                        dve.scalar_tensor_tensor(br[:, SSM0 + i, :], s5_u,
                                                 pars[:, bass.ds(i + PC["ssm_d"][0], 1)],
                                                 side[:, 2, 0:T], ALU.mult, ALU.add).then_inc(s5_y, 1)
                        for j in range(JB):
                            dve.wait_ge(bank_cross, i * JB + (B_QK * JB + j + 1))
                            dve.scalar_tensor_tensor(br[:, i * JB + (FOX0 + j), :], main[:, j, 0:T], QK_SCALE,
                                                     cross[:, j, :], ALU.mult, ALU.add).then_inc(bank_free, 1)

            dve.wait_ge(gelu_done, FT)
            dve.wait_ge(fl_mm, 2)
            dve.tensor_tensor(fl_z, side[:, 3, 0:TT * FT].rearrange("p (a h) -> p a h", a=TT),
                              col("b_forget").rearrange("p (a h) -> p a h", a=TT), ALU.add).then_inc(fl_dve, 1)
            with dve.Fori(0, B_G1 - B_V) as i:
                for c in range(CH):
                    low(i + B_V, c + LEAD)
                    for a, at in ((0, 0), (1, 7)):
                        f, done = i * 2 + a, i * 18 + 9 * a
                        now = lambda n: lru_now[:, n:n + 1]
                        if c == at:
                            dve.wait_ge(lo_ready, (i + B_V) * CH + (at + LEAD + 1))
                            dve.tensor_scalar(lru_now, lru_par[:, f, :], 1.0, None, ALU.mult).then_inc(lru_v, 1)
                            dve.tensor_scalar(lru_x, br[:, LRU0 + f, :], 1.0, None, ALU.mult).then_inc(lru_v, 1)
                            dve.wait_ge(lru_v, done + 2)
                            dve.tensor_scalar(lru_xc, lru_x, now(TAP0 + 3), now(CONV_B), ALU.mult,
                                              ALU.add).then_inc(lru_v, 1)
                            for s in range(1, 4):
                                dve.wait_ge(lru_v, done + 2 + s)
                                dve.scalar_tensor_tensor(lru_xc[:, s:T], lru_x[:, 0:T - s], now(TAP0 + 3 - s),
                                                         lru_xc[:, s:T], ALU.mult, ALU.add).then_inc(lru_v, 1)
                        if c == at + 4:
                            dve.wait_ge(lru_act, i * 12 + 6 * a + 5)
                            dve.scalar_tensor_tensor(lru_s, lru_s, 1.0, lru_th, ALU.add,
                                                     ALU.mult).then_inc(lru_v, 1)
                        if c == at + 6:
                            dve.wait_ge(lru_act, i * 12 + 6 * a + 6)
                            dve.tensor_tensor(lru_x, lru_ri[:, T:2 * T], lru_xc, ALU.mult).then_inc(lru_v, 1)
                            dve.wait_ge(lru_v, done + 8)
                            dve.tensor_tensor(lru_x, lru_x, lru_s, ALU.mult).then_inc(lru_v, 1)
                            dve.wait_ge(lru_v, done + 9)
                            dve.tensor_tensor_scan(br[:, LRU0 + f, :], lru_a, lru_x, 0.0, ALU.mult,
                                                   ALU.add).then_inc(lru_done, 1)
            dve.wait_ge(glu_sig, FT)
            dve.tensor_tensor(br[:, SSM0:SSM0 + FT, :], br[:, SSM0:SSM0 + FT, :], glu_z,
                              ALU.mult).then_inc(glu_applied, 1)

            def gates(i, g, tile0):
                for j in range(JB):
                    dve.wait_ge(bank_cross, g * JB + (V_READ + j + 1))
                    dve.tensor_tensor(cross[:, j, :], main[:, j, 0:T], cross[:, j, :],
                                      ALU.add).then_inc(bank_free, 1)
                for j in range(JB):
                    dve.wait_ge(glu_applied, 1)
                    dve.wait_ge(gate_silu, g * JB + j + 1)
                    tile = br[:, i * JB + (tile0 + j), :]
                    dve.tensor_tensor(tile, tile, cross[:, j, :], ALU.mult).then_inc(gate_used, 1)

            def head_out(h):
                dve.wait_ge(at_out, h + 1)
                dve.tensor_scalar(br[:, FOX0 + h, :], side[:, 2, 0:T], 1.0, None, ALU.mult).then_inc(at_o, 1)

            dve.wait_ge(fl_act, 4)
            dve.wait_ge(fl_dve, 2)
            dve.scalar_tensor_tensor(logf[:, :, :].rearrange("p h a -> p a h"), fl_z, 0.0, fl_e,
                                     ALU.min, ALU.subtract).then_inc(fl_dve, 1)
            with dve.Fori(0, B_G2 - B_G1) as i:
                for c in range(CH):
                    low(i + B_G1, c + LEAD)
                    if c == 0:
                        dve.wait_ge(fl_dve, 3)
                        dve.tensor_scalar(lf_now.rearrange("p (h a) -> p h a", h=2),
                                          logf[:, bass.ds(i * 2, 2), :], 1.0, None,
                                          ALU.mult).then_inc(lf_ready, 1)
                    for a in range(2):
                        h = i * 2 + a
                        if c == FOX_AT[a] + 1:
                            dve.wait_ge(at_scores, h + 1)
                            dve.tensor_reduce(row_max[:, 0:1], side[:, 0, 0:P], AX.X, ALU.max, negate=True)
                            dve.tensor_reduce(row_max[:, 1:2], side[:, 0, P:3 * P], AX.X, ALU.max,
                                              negate=True).then_inc(at_max, 1)
                        if c == FOX_AT[a] + 2:
                            dve.wait_ge(at_exp, i * 4 + 2 * a + 2)
                            dve.reciprocal(row_inv, row_sum).then_inc(at_inv, 1)
                            dve.wait_ge(at_inv, h + 1)
                            dve.tensor_scalar(at_p[:, 0:P], at_p[:, 0:P], row_inv[:, 0:1], None,
                                              ALU.mult).then_inc(at_norm, 1)
                            dve.tensor_scalar(at_p[:, P:3 * P], at_p[:, P:3 * P], row_inv[:, 1:2], None,
                                              ALU.mult).then_inc(at_norm, 1)
                        if c == FOX_AT[a] + 6:
                            head_out(h)
                    if c == CH - 1:
                        gates(i, i, SSM0)

            def mix_low(c):
                for k in range(KC * c, KC * (c + 1)):
                    dve.wait_ge(mix_hi, k + 1)
                    dve.tensor_tensor(acts[:, k, T:2 * T], br[:, k, :], acts[:, k, 0:T].bitcast(F32),
                                      ALU.subtract).then_inc(mix_lo, 1)

            def sb_block(i):
                for c in range(CH):
                    low(i + B_G2, c + LEAD)
                    if isinstance(i, int) and 0 < c < CH - 1:
                        mix_low(c - 1)
                    for a in range(2):
                        h, done = i * 2 + (FT + a), i * 8 + 4 * a
                        if c == SB_AT[a] + 2:
                            dve.wait_ge(sb_act, i * 6 + 3 * a + 3)
                            dve.scalar_tensor_tensor(at_sp, side[:, 0, 0:3 * P], 0.0, at_e, ALU.max,
                                                     ALU.add).then_inc(sb_dve, 1)
                            dve.wait_ge(sb_dve, done + 1)
                            dve.tensor_tensor_scan(at_r[:, 0:P][:, ::-1], ones[:, 0:P],
                                                   at_sp[:, 0:P][:, ::-1], 0.0, ALU.mult,
                                                   ALU.add).then_inc(sb_dve, 1)
                            dve.tensor_tensor_scan(at_r[:, P:3 * P][:, ::-1], ones,
                                                   at_sp[:, P:3 * P][:, ::-1], 0.0, ALU.mult,
                                                   ALU.add).then_inc(sb_dve, 1)
                            dve.wait_ge(sb_dve, done + 3)
                            dve.tensor_tensor(at_e, side[:, 0, 0:3 * P], at_r, ALU.subtract).then_inc(sb_dve, 1)
                        if c == SB_AT[a] + 8:
                            head_out(h)
                    if c == CH - 1:
                        gates(i, i + (B_G2 - B_G1), FOX0)

            with dve.Fori(0, B_OUT - B_G2 - 1) as i:
                sb_block(i)
            sb_block(B_OUT - B_G2 - 1)

            def weigh(n, u):
                for a in range(TT):
                    dve.wait_ge(o_sq, n * TT + a + 1)
                    dve.wait_ge(g_in, 16)
                    dve.tensor_tensor(mixed[:, a, bass.ds(n * BLK, BLK)], main[:, 2 * u + a, :],
                                      g_rows[:, bass.ds(n * BLK, BLK)], ALU.mult).then_inc(bank_free, 1)
                if not (isinstance(n, int) and n == 0):
                    dve.wait_ge(o_ss, n)
                    dve.tensor_tensor(ss_all, ss_all, ss_new, ALU.add).then_inc(o_ss, 1)
                else:
                    dve.tensor_copy(ss_all, ss_new).then_inc(o_ss, 1)

            def out_block(n, u):
                for c in range(CH):
                    if not (isinstance(n, int) and n == N_OUT_BLOCKS - 1 and c + LEAD >= CH):
                        low(n + B_OUT, c + LEAD)
                    if isinstance(n, int) and n == 0 and c < 2:
                        mix_low(c + CH - 2)
                    if c == CH - 1:
                        weigh(n, u)

            out_block(0, 0)
            with dve.Fori(0, (N_OUT_BLOCKS - 2) // 2) as ii:
                out_block(ii * 2 + 1, 1)
                out_block(ii * 2 + 2, 0)
            out_block(N_OUT_BLOCKS - 1, 1)
            dve.wait_ge(o_ss, N_OUT_BLOCKS)
            dve.tensor_scalar(ms[:, 0:TT], ss_all, 1.0 / D, EPS, ALU.mult, ALU.add).then_inc(fin_dve, 1)
            dve.wait_ge(fin_act, 1)
            dve.wait_ge(fin_dve, 1)
            root(fin_dve, 1, slice(0, TT))
            dve.wait_ge(bank_free, N_FM * JB + N_OUT_BLOCKS * TT)
            for a, h in halves:
                part = mixed[:, a, h * HW:(h + 1) * HW]
                dve.wait_ge(xl_in[a], 16)
                dve.scalar_tensor_tensor(part, part, rstd[:, a:a + 1], x_late[a][:, h * HW:(h + 1) * HW],
                                         ALU.mult, ALU.add).then_inc(fin_sum, 1)

        @block.gpsimd
        def _(pool):
            pool.iota(steps_t, pattern=[[1, T]], base=0, channel_multiplier=0,
                      allow_small_or_imprecise_dtypes=True).then_inc(consts, 1)
            pool.memset(small[:, 176:177], ROUND).then_inc(consts, 1)
            pool.memset(later[:, :], 1.0).then_inc(const_steps, 1)
            pool.memset(upto[:, :], 1.0).then_inc(const_steps, 1)
            pool.memset(ident[:, :], 0.0).then_inc(const_steps, 1)
            pool.memset(ident_b[:, :], 0.0).then_inc(const_steps, 1)
            pool.memset(causal_b[:, :], 0.0).then_inc(const_steps, 1)
            pool.memset(strict_b[:, :], 0.0).then_inc(const_steps, 1)
            pool.wait_ge(const_steps, 6)

            def choose(t, op, fill, sign):
                pool.affine_select(out=t, in_=t, compare_op=op, fill=fill, base=0,
                                   pattern=[[-sign, P]], channel_multiplier=sign).then_inc(consts, 1)

            choose(later[:, P:2 * P], ALU.is_gt, 0.0, 1)
            choose(upto[:, :], ALU.is_ge, 0.0, -1)
            choose(ident[:, :], ALU.not_equal, 1.0, 1)
            choose(ident_b[:, :], ALU.not_equal, 1.0, 1)
            choose(causal_b[:, :], ALU.is_ge, NEG, 1)
            choose(strict_b[:, :], ALU.is_gt, NEG, 1)

            pool.wait_ge(consts, N_CONST)
            rounder = small[:, 176:177].to_broadcast([P, T])
            with pool.Fori(0, B_V - B_QK) as i:
                def fraction(j):
                    g, tab = i * SJ + j, i * (3 * SJ) + 3 * j
                    pool.wait_ge(p5_ready, i + 1)
                    pool.tensor_tensor(s5_a, steps_t, s5_now[:, j:j + 1].to_broadcast([P, T]),
                                       ALU.mult).then_inc(s5_tab, 1)
                    pool.wait_ge(s5_tab, tab + 1)
                    pool.tensor_tensor(s5_k, s5_a, rounder, ALU.add).then_inc(s5_tab, 1)
                    pool.wait_ge(s5_tab, tab + 2)
                    pool.tensor_tensor(s5_k, s5_k, rounder, ALU.subtract).then_inc(s5_tab, 1)
                    pool.wait_ge(s5_tab, tab + 3)
                    pool.tensor_tensor(s5_f, s5_a, s5_k, ALU.subtract).then_inc(s5_frac, 1)

                def cosine(j):
                    pool.wait_ge(s5_trig, i * (4 * SJ) + 4 * j + 4)
                    if j >= 2:
                        pool.wait_ge(s5_done, i * SJ + j - 1)
                    pool.tensor_tensor(s5_cos[j % 2], ones, s5_q, ALU.subtract).then_inc(s5_cosd, 1)

                fraction(0)
                now = lambda n: s5_now[:, n * SJ:(n + 1) * SJ].unsqueeze(2).to_broadcast([P, SJ, 2 * HG])
                pool.wait_ge(ct_in, i * 16 + 16)
                c_re, c_im = s5_ct[:, :, 0, :], s5_ct[:, :, 1, :]
                for n, (part, factor) in enumerate(((c_re, 2), (c_im, 4), (c_re, 4), (c_im, 3))):
                    pool.tensor_tensor(s5_c[n], part, now(factor), ALU.mult).then_inc(s5_cq, 1)
                pool.wait_ge(s5_cq, i * 5 + 4)
                pool.tensor_tensor(s5_cp[:, :, 0, :], s5_c[0], s5_c[1], ALU.add).then_inc(s5_cq, 1)
                pool.wait_ge(s5_cq, i * 5 + 5)
                pool.tensor_tensor(s5_cp[:, :, 1, :], s5_c[2], s5_c[3], ALU.add).then_inc(s5_cprime, 1)
                for j in range(SJ):
                    cosine(j)
                    if j + 1 < SJ:
                        fraction(j + 1)

            def fetch(h, free):
                if free is None:
                    pool.wait_ge(at_scores, h)
                else:
                    free()
                pool.wait_ge(glu_applied, 1)
                pool.tensor_copy(at_q, br[:, FOX0 + h, :]).then_inc(qs_ready, 1)
                if free is None:
                    pool.wait_ge(at_out, h)
                pool.wait_ge(bank_cross, V_READ)
                pool.tensor_copy(at_v, vals[:, :, bass.ds(h * P, P)]).then_inc(vs_ready, 1)

            with pool.Fori(0, B_G2 - B_G1) as i:
                for a in range(2):
                    h = i * 2 + a
                    fetch(h, None if a else lambda: pool.wait_ge(lf_ready, i + 1))
                    for n, (mask, tile) in enumerate(((upto[:, :], 0), (later[:, 0:P], 0), (upto[:, :], 1))):
                        pool.wait_ge(lf_ready, i + 1)
                        if a:
                            pool.wait_ge(at_scores, h)
                        log_f = lf_now[:, 2 * a + tile:2 * a + tile + 1].to_broadcast([P, P])
                        dec = pool.tensor_tensor(at_dec[:, n, :], mask, log_f, ALU.mult)
                    dec.then_inc(dec_ready, 1)
            with pool.Fori(0, B_OUT - B_G2) as i:
                for a in range(2):
                    fetch(i * 2 + (FT + a), None)


def _lay_out(v):
    import numpy as np

    f32 = np.float32
    sizes = [BW] * 4 + [FT] + [BW] * 8
    at = np.cumsum([0] + sizes)
    names = ["fq", "fk", "fv", "fg", "fl", "sq", "sk", "sv", "sg", "su", "ug", "lx", "lg"]
    where = {n: int(a) for n, a in zip(names, at)}
    w_in, w_out = v["w_in"][0], v["w_out"][0]

    wall = np.empty((N_BLOCKS, P, NK, BLK), f32)
    order = ["su", "lx", "fq", "sq", "fk", "sk", "fv", "sv", "ug", "lg", "fg", "sg"]
    for n, name in enumerate(order):
        for half in range(BW // BLK):
            a = where[name] + half * BLK
            wall[n * (BW // BLK) + half] = w_in[:, a:a + BLK].reshape(NK, P, BLK).transpose(1, 0, 2)
    rows = np.concatenate([w_out[2 * BW:4 * BW], w_out[0:2 * BW]], axis=0)
    for n in range(N_OUT_BLOCKS):
        wall[N_IN_BLOCKS + n] = rows[:, n * BLK:(n + 1) * BLK].reshape(NK, P, BLK).transpose(1, 0, 2)
    wfg = w_in[:, where["fl"]:where["fl"] + FT].reshape(NK, P, FT).transpose(1, 0, 2)

    by_state = lambda a: a.reshape(BW // HG // 2, 2, STATE).transpose(1, 2, 0).reshape(P, -1)
    by_feature = lambda a: a.reshape(-1, P).T
    par = np.zeros((P, NPAR), f32)

    def put(name, a):
        par[:, PC[name][0]:PC[name][1]] = a

    put("g_pre", by_feature(v["g_pre"][0]))
    put("a_re", by_state(v["ssm_a_re"][0]))
    put("a_im", by_state(v["ssm_a_im"][0]))
    put("log_dt", by_state(np.repeat(v["ssm_log_dt"][0][:, None], STATE, axis=1)))
    put("b_forget", np.broadcast_to(np.tile(v["b_forget"][0], TT), (P, TT * FT)))
    put("ssm_d", by_feature(v["ssm_d"][0]))
    put("lam", by_feature(v["lru_lambda"][0]))
    lru = np.zeros((P, FT, 9), f32)
    for n in range(4):
        lru[:, :, TAP0 + n] = by_feature(v["conv_w"][0][n])
    for n, name in ((CONV_B, "conv_b"), (B_R, "b_rgate"), (B_I, "b_igate"), (B_GLU, "b_glu")):
        lru[:, :, n] = by_feature(v[name][0])
    put("lru", lru.reshape(P, FT * 9))

    bt = np.zeros((FT, P, SJ, 2, P), f32)
    ct = np.zeros((FT, P, SJ, 2, 2 * HG), f32)
    for r, (b, c) in enumerate((("ssm_b_re", "ssm_c_re"), ("ssm_b_im", "ssm_c_im"))):
        for f in range(FT):
            for j in range(SJ):
                for a in range(2):
                    g = f * 2 * SJ + 2 * j + a
                    row = 2 * HG * j + HG * a
                    bt[f, row:row + HG, j, r, a * STATE:(a + 1) * STATE] = v[b][0][g].T
                    ct[f, a * STATE:(a + 1) * STATE, j, r, a * HG:(a + 1) * HG] = v[c][0][g].T
    wglu = v["w_glu"][0].reshape(FT, P, FT, P).transpose(2, 1, 0, 3)
    wri = np.zeros((FT, P, 2, P), f32)
    half = P // 2
    for r, name in enumerate(("w_rgate", "w_igate")):
        for n in range(2 * FT):
            a = (n % 2) * half
            wri[n // 2, a:a + half, r, a:a + half] = v[name][0][n]
    whole = np.ascontiguousarray
    return {"x": whole(v["x"][0]), "par": par, "bt": bt.reshape(FT, P, -1), "ct": ct.reshape(FT, P, -1),
            "wfg": whole(wfg), "wglu": whole(wglu).reshape(FT, P, -1), "wri": wri.reshape(FT, P, -1),
            "gpost": whole(v["g_post"][0]), "wall": wall.reshape(N_BLOCKS, P, NK * BLK)}


def kernel(**inputs):
    import numpy as np
    import concourse.bacc as bacc
    from concourse.bass_utils import run_bass_kernel_spmd

    arrays = _lay_out({n: np.asarray(a) for n, a in inputs.items()})
    nc = bacc.Bacc("TRN2", target_bir_lowering=False, num_devices=1)
    args = [nc.dram_tensor(f"in_{n}", a.shape, mybir.dt.from_np(a.dtype), kind="ExternalInput").ap()
            for n, a in arrays.items()]
    out = nc.dram_tensor("out_0", (T, D), F32, kind="ExternalOutput").ap()
    hybrid_trunk(nc, *args, out)
    r = run_bass_kernel_spmd(nc, [{f"in_{n}": a for n, a in arrays.items()}], core_ids=[0])
    return r.results[0]["out_0"].reshape(1, T, D)
```

```python
import math
from contextlib import ExitStack

import concourse.bass as bass
from concourse import mybir

F32 = mybir.dt.float32
F32R = mybir.dt.float32r
BF16 = mybir.dt.bfloat16
ACT = mybir.ActivationFunctionType
ALU = mybir.AluOpType
AX = mybir.AxisListType

P = 128
D = 4096
T = 256
TT = T // P
NK = D // P
BW = D // 4
FT = BW // P
BLK = 512
JB = BLK // P
KC = 2
CH = NK // KC
CW = KC * BLK
RING = 4
LEAD = RING - 1
STATE, HG = 64, 16
SJ = 4
N_IN_BLOCKS = 24
N_OUT_BLOCKS = D // BLK
N_BLOCKS = N_IN_BLOCKS + N_OUT_BLOCKS
B_SRC, B_QK, B_V, B_G1, B_G2, B_OUT = 0, 4, 12, 16, 20, 24
EPS = 1e-6
QK_SCALE = float(P) ** -0.25
LRU_C = 8.0
ROUND = 1.5 * 2.0 ** 23
TWO_PI = 6.283185
PI_1 = 6.28125
PI_2 = 0.0019350051879882812
PI_3 = 2.0 * math.pi - 6.28125 - 0.0019350051879882812
NEG = -1.0e30
SSM0, LRU0, FOX0, SB0, KEY0 = 0, FT, 2 * FT, 3 * FT, 4 * FT
PC = {}
_at = 0
for _name, _n in (("g_pre", NK), ("a_re", 32), ("a_im", 32), ("log_dt", 32), ("b_forget", TT * FT),
                  ("ssm_d", FT), ("lam", FT), ("lru", FT * 9)):
    PC[_name] = (_at, _at + _n)
    _at += _n
NPAR = _at
TAP0, CONV_B, B_R, B_I, LOG_A, B_GLU = 0, 4, 5, 6, 7, 8


def hybrid_trunk(nc, x, par, bt, ct, wfg, wglu, wri, gpost, wall, out):
    ctx = ExitStack()
    with ctx:
        def sb(name, shape, dt=F32):
            return ctx.enter_context(nc.sbuf_tensor(name, shape, dt))

        def sem(name):
            return ctx.enter_context(nc.semaphore(name))

        acts = sb("acts", [P, NK, 2 * T], F32R)
        w_raw = sb("w_raw", [P, RING, CW])
        w_hi = sb("w_hi", [P, RING, CW], F32R)
        w_lo = sb("w_lo", [P, RING, CW], F32R)
        br = sb("br", [P, 6 * FT, T])
        vals = sb("vals", [P, TT, 2 * BW])
        cross = sb("cross", [P, JB, T])
        scr = sb("scr", [P, 5120])
        rs_row = sb("rs_row", [P, T])[:, :]
        pars = sb("pars", [P, NPAR])
        small = sb("small", [P, 147])
        wf = sb("wf", [P, 2 * NK * FT + P], F32R)
        later = sb("later", [P, 2 * P])
        upto = sb("upto", [P, P])
        ident = sb("ident", [P, P])
        ident_b = sb("ident_b", [P, P], BF16)
        causal_b = sb("causal_b", [P, P], BF16)
        strict_b = sb("strict_b", [P, P], BF16)

        main = ctx.enter_context(nc.psum_tensor("main", [P, 4, BLK], F32))
        side = ctx.enter_context(nc.psum_tensor("side", [P, 4, BLK], F32))

        x_rows = br[:, 0:32, :].rearrange("p (a k) t -> p a (k t)", a=TT)
        mixed = br[:, 0:32, :].rearrange("p (a k) t -> p a (k t)", a=TT)
        g_rows = br[:, 32:48, :].rearrange("p k t -> p (k t)")
        x_late = [vals[:, :, :].rearrange("p a n -> p (a n)"), scr[:, 0:D]]
        wf_raw = scr[:, 0:256].rearrange("p (k n) -> p k n", k=NK)
        s5tmp = scr[:, 256:800].rearrange("p (n f) -> p n f", n=17)
        vflat = vals[:, :, :].rearrange("p a n -> p (a n)")
        s5_m1, s5_m2, s5_g = vflat[:, 0:512], vflat[:, 512:1024], vflat[:, 1024:1536]
        s5_h = [vflat[:, 1536:2048], vflat[:, 2048:2560]]
        s5_sin = [vflat[:, 2560:3072], vflat[:, 3072:3584]]
        s5_cos = [vflat[:, 3584:3840], vflat[:, 3840:4096]]
        rs_banks = rs_row.unsqueeze(1).to_broadcast([P, JB, T])
        rs_diag = scr[:, 3072:3328]
        s5par = scr[:, D:D + FT * 5 * SJ].rearrange("p (f n) -> p f n", f=FT)
        logf = scr[:, D:D + FT * TT].rearrange("p (h a) -> p h a", h=FT)
        steps_t = scr[:, 3328:3328 + T]
        s5_bt = scr[:, 0:1024].rearrange("p (j r s) -> p j r s", j=SJ, r=2)
        s5_ct = scr[:, 1024:1280].rearrange("p (j r h) -> p j r h", j=SJ, r=2)
        s5_cp = scr[:, 1280:1536].rearrange("p (j r h) -> p j r h", j=SJ, r=2)
        s5_u = scr[:, 1536:1792]
        s5_a, s5_k, s5_f, s5_q = (scr[:, 1792 + T * n:1792 + T * (n + 1)] for n in range(4))
        s5_c = [scr[:, 2816 + 128 * n:2816 + 128 * (n + 1)].rearrange("p (j h) -> p j h", j=SJ)
                for n in range(4)]
        glu_w = scr[:, 0:1024].rearrange("p (k n) -> p k n", k=FT)
        lru_w = scr[:, 1024:1280].rearrange("p (r n) -> p r n", r=2)
        lru_x, lru_xc = scr[:, 1280:1536], scr[:, 1536:1792]
        lru_ri = scr[:, 1792:2304]
        lru_a, lru_th, lru_s = scr[:, 2304:2560], scr[:, 2560:2816], scr[:, 2816:3072]
        glu_z = scr[:, 3072:5120].rearrange("p (n t) -> p n t", n=FT)
        at_q = scr[:, 0:256]
        at_v = scr[:, 256:512].rearrange("p (a d) -> p a d", a=TT)
        at_dec = scr[:, 512:896].rearrange("p (n t) -> p n t", n=3)
        at_p, at_pt = scr[:, 896:1280], scr[:, 1280:1664]
        at_e, at_sp, at_r = scr[:, 1664:2048], scr[:, 2048:2432], scr[:, 2432:2816]
        sumsq, ms, rs_a, rs_b, rstd = (small[:, 4 * n:4 * n + 4] for n in range(5))
        s5_now = small[:, 20:40]
        lru_now = small[:, 40:49]
        lf_now = small[:, 50:54]
        ones = later[:, 0:1].to_broadcast([P, T])
        row_max, row_sum, row_inv = small[:, 54:56], small[:, 56:58], small[:, 58:60]
        ss_new, ss_all = small[:, 60:62], small[:, 62:64]
        fl_cross, fl_rows = scr[:, 3584:3840], scr[:, 3840:4096]
        fl_z, fl_e = (small[:, 112 + 16 * n:128 + 16 * n].rearrange("p (a n) -> p a n", a=TT)
                      for n in range(2))
        log_a = [scr[:, 4352 + 8 * n:4360 + 8 * n] for n in range(4)]

        def col(name, n=None):
            a, b = PC[name]
            return pars[:, a:b] if n is None else pars[:, a + n:a + n + 1]

        lru_par = col("lru").rearrange("p (f n) -> p f n", f=FT)
        halves = [(a, h) for a in range(TT) for h in range(2)]
        HW, QW = D // 2, D // 4
        quarters = [(a, q) for a in range(TT) for q in range(4)]

        x_in = [sem(f"x_in{n}") for n in range(D // BLK)]
        par_in, wf_in = sem("par_in"), sem("wf_in")
        raw_in = [sem(f"raw_in{n}") for n in range(RING)]
        hi_ready, lo_ready = sem("hi_ready"), sem("lo_ready")
        w_used = sem("w_used")
        fm_done, tm_done = sem("fm_done"), sem("tm_done")
        bank_cross = sem("bank_cross")
        bank_free = sem("bank_free")
        squared, rms_act, rms_dve = sem("squared"), sem("rms_act"), sem("rms_dve")
        rs_mm, rs_ready = sem("rs_mm"), sem("rs_ready")
        br_ready = sem("br_ready")
        xt_done, u_hi, u_lo = sem("xt_done"), sem("u_hi"), sem("u_lo")
        consts, const_steps = sem("consts"), sem("const_steps")
        pa, pd = sem("pa"), sem("pd")
        wf_hi, wf_lo0, wf_lo = sem("wf_hi"), sem("wf_lo0"), sem("wf_lo")
        fl_mm, fl_act, fl_dve = sem("fl_mm"), sem("fl_act"), sem("fl_dve")
        bt_in, ct_in, p5_ready, su_ready = sem("bt_in"), sem("ct_in"), sem("p5_ready"), sem("su_ready")
        s5_tab, s5_frac, s5_trig, s5_cosd = sem("s5_tab"), sem("s5_frac"), sem("s5_trig"), sem("s5_cosd")
        s5_cq, s5_cprime = sem("s5_cq"), sem("s5_cprime")
        s5_bmm, s5_cmm, s5_dve, s5_done, s5_y = (sem(n) for n in
                                                 ("s5_bmm", "s5_cmm", "s5_dve", "s5_done", "s5_y"))
        gelu_done, wg_in, wr_in = sem("gelu_done"), sem("wg_in"), sem("wr_in")
        lru_v, lru_mm, lru_act, lru_done = sem("lru_v"), sem("lru_mm"), sem("lru_act"), sem("lru_done")
        glu_mm, glu_sig, glu_applied = sem("glu_mm"), sem("glu_sig"), sem("glu_applied")
        lf_ready, dec_ready, qs_ready, vs_ready = (sem(n) for n in
                                                   ("lf_ready", "dec_ready", "qs_ready", "vs_ready"))
        at_scores, at_max, at_exp, at_inv, at_norm = (sem(n) for n in
                                                      ("at_scores", "at_max", "at_exp", "at_inv", "at_norm"))
        at_tr, at_ptd, at_out, at_o = sem("at_tr"), sem("at_ptd"), sem("at_out"), sem("at_o")
        sb_act, sb_dve = sem("sb_act"), sem("sb_dve")
        gate_normed, gate_silu, gate_used = sem("gate_normed"), sem("gate_silu"), sem("gate_used")
        mix_hi, mix_lo = sem("mix_hi"), sem("mix_lo")
        g_in, xl_in = sem("g_in"), [sem("xl_in0"), sem("xl_in1")]
        o_sq, o_ss = sem("o_sq"), sem("o_ss")
        fin_act, fin_dve, fin_sum, stored = (sem(n) for n in ("fin_act", "fin_dve", "fin_sum", "stored"))

        N_CONST = 8
        FOX_AT, SB_AT = (4, 9), (0, 7)
        LRU_AT = (1, 8)
        N_FM = B_V + B_OUT - B_G1
        V_READ = B_V * JB + (B_G1 - B_V) * TT
        block = ctx.enter_context(nc.Block())

        @block.sync
        def _(sp):
            def load_x(n):
                for a in range(TT):
                    sp.dma_start(x_rows[:, a, n * BLK:(n + 1) * BLK],
                                 x[a * P:(a + 1) * P, n * BLK:(n + 1) * BLK]).then_inc(x_in[n], 16)

            def load(b, c):
                sp.dma_start(w_raw[:, c % RING, :],
                             wall[bass.ds(b, 1), :, c * CW:(c + 1) * CW].rearrange("b p n -> (b p) n")
                             ).then_inc(raw_in[c % RING], 16)

            for n in range(RING // 2):
                load_x(n)
                load(0, 2 * n)
                load(0, 2 * n + 1)
            load_x(2)
            load_x(3)
            for c in range(CH):
                sp.wait_ge(lo_ready, c + 1)
                load((c + RING) // CH, (c + RING) % CH)
                if c + 4 < D // BLK:
                    load_x(c + 4)
            with sp.Fori(1, N_BLOCKS - 1) as b:
                for c in range(CH):
                    sp.wait_ge(lo_ready, b * CH + c + 1)
                    load(b + (c + RING) // CH, (c + RING) % CH)
            for c in range(CH - RING):
                sp.wait_ge(lo_ready, (N_BLOCKS - 1) * CH + c + 1)
                load(N_BLOCKS - 1, c + RING)
            for n, (a, q) in enumerate(quarters):
                sp.wait_ge(fin_sum, n + 1)
                sp.dma_start(out[a * P:(a + 1) * P, q * QW:(q + 1) * QW],
                             mixed[:, a, q * QW:(q + 1) * QW]).then_inc(stored, 16)
            sp.wait_ge(stored, 16 * len(quarters))

        @block.tensor
        def _(pe):
            def chunk_fm(b, m, c):
                pe.wait_ge(lo_ready, b * CH + c + 1)
                s = c % RING
                for j in range(JB):
                    if c == 0 and not isinstance(m, int):
                        pe.wait_ge(bank_free, m * JB + (j + 1 - JB))
                    for kk in range(KC):
                        k, at = KC * c + kk, kk * BLK + j * P
                        pe.matmul(main[:, j, :], w_hi[:, s, at:at + P], acts[:, k, :],
                                  start=(k == 0), stop=False)
                        mm = pe.matmul(main[:, j, T:2 * T], w_lo[:, s, at:at + P], acts[:, k, 0:T],
                                       start=False, stop=(k == NK - 1))
                    if c == CH - 1 and j < JB - 1:
                        mm.then_inc(fm_done, 1)
                mm.then_inc(w_used, 1)

            def chunk_tm(b, c, bank0, free, mixed_parts=False):
                pe.wait_ge(lo_ready, b * CH + c + 1)
                if mixed_parts:
                    pe.wait_ge(mix_lo, KC * (c + 1))
                s = c % RING
                for a in range(TT):
                    if c == 0:
                        free(a)
                    for kk in range(KC):
                        k = KC * c + kk
                        u_h, u_l = acts[:, k, a * P:(a + 1) * P], acts[:, k, T + a * P:T + (a + 1) * P]
                        wh, wl = w_hi[:, s, kk * BLK:(kk + 1) * BLK], w_lo[:, s, kk * BLK:(kk + 1) * BLK]
                        pe.matmul(main[:, bank0 + a, :], u_h, wh, start=(k == 0), stop=False)
                        pe.matmul(main[:, bank0 + a, :], u_h, wl, start=False, stop=False)
                        mm = pe.matmul(main[:, bank0 + a, :], u_l, wh, start=False, stop=(k == NK - 1))
                    if c == CH - 1 and a < TT - 1:
                        mm.then_inc(tm_done, 1)
                mm.then_inc(w_used, 1)

            def turn(k):
                if k % JB == 0:
                    pe.wait_ge(x_in[k // JB], 16 * TT)
                if k >= 4:
                    pe.wait_ge(u_lo, k - 3)
                for a in range(TT):
                    tr = pe.transpose(side[:, k % 4, a * P:(a + 1) * P], x_rows[:, a, k * P:(k + 1) * P],
                                      ident[:, :])
                tr.then_inc(xt_done, 1)

            pe.wait_ge(consts, N_CONST)
            for k in range(4):
                turn(k)
            for c in range(CH):
                for k in range(KC * c + 4, min(KC * (c + 1) + 4, NK)):
                    turn(k)
                pe.wait_ge(u_lo, KC * (c + 1))
                if c == CH - 2:
                    pe.wait_ge(u_lo, NK)
                    pe.wait_ge(rms_dve, 9)
                    pe.matmul(side[:, 0, 0:T], later[:, 0:1].to_broadcast([P, P]), rs_diag, start=True,
                              stop=True).then_inc(rs_mm, 1)
                chunk_fm(0, 0, c)

            with pe.Fori(1, B_QK - B_SRC) as i:
                for c in range(CH):
                    chunk_fm(i, i, c)

            pe.wait_ge(wf_lo, 1)
            for k in range(NK):
                pe.matmul(side[:, 3, :], wf[:, k * FT:k * FT + P], acts[:, k, :], start=(k == 0), stop=False)
                mm = pe.matmul(side[:, 3, T:2 * T], wf[:, NK * FT + k * FT:NK * FT + k * FT + P],
                               acts[:, k, 0:T], start=False, stop=(k == NK - 1))
            mm.then_inc(fl_mm, 1)

            with pe.Fori(0, B_V - B_QK) as i:
                def s5_inputs(j):
                    if j == 0:
                        pe.wait_ge(su_ready, i + 1)
                        pe.wait_ge(bt_in, i * 16 + 16)
                    if j >= 2:
                        pe.wait_ge(s5_done, i * SJ + j - 1)
                    for r in range(2):
                        mm = pe.matmul(side[:, j % 2, r * T:(r + 1) * T], s5_bt[:, j, r, :], s5_u[:, :],
                                       start=True, stop=True)
                    mm.then_inc(s5_bmm, 1)

                for c in range(CH):
                    if c == 2:
                        s5_inputs(0)
                    if c in (4, 7, 10):
                        s5_inputs(c // 3)
                    if c in (7, 10, 13, 15):
                        j = (7, 10, 13, 15).index(c)
                        if j == 0:
                            pe.wait_ge(s5_cprime, i + 1)
                        pe.wait_ge(s5_done, i * SJ + j + 1)
                        for r in range(2):
                            mm = pe.matmul(side[32 * j:32 * j + 32, 2, 0:T], s5_cp[:, j, r, :],
                                           s5_h[j % 2][:, r * T:(r + 1) * T], start=(r == 0), stop=(r == 1))
                        mm.then_inc(s5_cmm, 1)
                    chunk_fm(i + B_QK, i + B_QK, c)

            pe.wait_ge(fl_dve, 1)
            for a in range(TT):
                mm = pe.transpose(side[:, 3, a * FT:(a + 1) * FT], fl_rows[0:FT, a * P:(a + 1) * P],
                                  ident[0:FT, 0:FT])
            mm.then_inc(fl_mm, 1)

            with pe.Fori(0, (B_G1 - B_V) // 2) as ii:
                for u in range(2):
                    i = ii * 2 + u

                    def v_bank(a):
                        pe.wait_ge(bank_free, (B_V - 1) * JB + 2 * u + a + 1)
                        pe.wait_ge(bank_cross, ii * (2 * TT) + ((B_V - 1) * JB + 2 * u + a + 1))

                    for c in range(CH):
                        for a, at in enumerate(LRU_AT):
                            if c == at + 3:
                                pe.wait_ge(wr_in, ii * 64 + (32 * u + 16 * (a + 1)))
                                pe.wait_ge(lru_v, ii * 36 + (18 * u + 9 * a + 6))
                                for r in range(2):
                                    mm = pe.matmul(side[:, 0, r * T:(r + 1) * T], lru_w[:, r, :], lru_xc[:, :],
                                                   start=True, stop=True)
                                mm.then_inc(lru_mm, 1)
                                pe.wait_ge(wg_in, ii * 64 + (32 * u + 16 * (a + 1)))
                                pe.wait_ge(gelu_done, FT)
                                for k in range(FT):
                                    mm = pe.matmul(side[:, 1, 0:T], glu_w[:, k, :], br[:, SSM0 + k, :],
                                                   start=(k == 0), stop=(k == FT - 1))
                                mm.then_inc(glu_mm, 1)
                        chunk_tm(i + B_V, c, 2 * u, v_bank)

            def transposes(h):
                pe.transpose(side[:, 1, 0:P], at_p[:, 0:P], ident[:, :])
                pe.transpose(side[:, 1, P:2 * P], at_p[:, P:2 * P], ident[:, :])
                pe.transpose(side[:, 1, 2 * P:3 * P], at_p[:, 2 * P:3 * P], ident[:, :]).then_inc(at_tr, 1)

            def weighted_values(h):
                pe.wait_ge(at_ptd, h + 1)
                pe.wait_ge(vs_ready, h + 1)
                pe.matmul(side[:, 2, 0:T], at_v[:, 0, :], at_pt[:, 0:T], start=True, stop=False)
                pe.matmul(side[:, 2, P:T], at_v[:, 1, :], at_pt[:, T:3 * P], start=False,
                          stop=True).then_inc(at_out, 1)

            pe.wait_ge(bank_cross, V_READ)
            with pe.Fori(0, B_G2 - B_G1) as i:
                for c in range(CH):
                    for a in range(2):
                        h = i * 2 + a
                        if c == FOX_AT[a]:
                            pe.wait_ge(qs_ready, h + 1)
                            pe.wait_ge(dec_ready, h + 1)
                            key = br[:, KEY0 + h, :]
                            q0, q1 = side[:, 0, 0:P], side[:, 0, P:3 * P]
                            pe.matmul(q0, at_q[:, 0:P], key[:, 0:P], start=True, stop=False)
                            pe.matmul(q0, at_dec[:, 0, :], later[:, P:2 * P], start=False, stop=False)
                            pe.matmul(q0, ident_b[:, :], causal_b[:, :], start=False, stop=True)
                            pe.matmul(q1, at_q[:, P:T], key[:, :], start=True, stop=False)
                            pe.matmul(side[:, 0, P:2 * P], at_dec[:, 1, :], later[:, P:2 * P],
                                      start=False, stop=False)
                            pe.matmul(q1, at_dec[:, 2, :], later[:, :], start=False, stop=False)
                            pe.matmul(side[:, 0, 2 * P:3 * P], ident_b[:, :], causal_b[:, :],
                                      start=False, stop=True).then_inc(at_scores, 1)
                        if c == FOX_AT[a] + 4:
                            pe.wait_ge(at_norm, i * 4 + 2 * a + 2)
                            transposes(h)
                        if c == FOX_AT[a] + 5:
                            weighted_values(h)
                    chunk_fm(i + B_G1, i + B_V, c)

            with pe.Fori(0, B_OUT - B_G2) as i:
                for c in range(CH):
                    for a in range(2):
                        h = i * 2 + (FT + a)
                        if c == SB_AT[a]:
                            pe.wait_ge(qs_ready, h + 1)
                            key = br[:, KEY0 + h, :]
                            q0, q1 = side[:, 0, 0:P], side[:, 0, P:3 * P]
                            pe.matmul(q0, at_q[:, 0:P], key[:, 0:P], start=True, stop=False)
                            pe.matmul(q0, ident_b[:, :], strict_b[:, :], start=False, stop=True)
                            pe.matmul(q1, at_q[:, P:T], key[:, :], start=True, stop=False)
                            pe.matmul(side[:, 0, 2 * P:3 * P], ident_b[:, :], strict_b[:, :],
                                      start=False, stop=True).then_inc(at_scores, 1)
                        if c == SB_AT[a] + 5:
                            pe.wait_ge(at_exp, i * 2 + (2 * FT + a + 1))
                            transposes(h)
                        if c == SB_AT[a] + 7:
                            weighted_values(h)
                    chunk_fm(i + B_G2, i + (B_V + B_G2 - B_G1), c)

            def out_block(n, u):
                for c in range(CH):
                    chunk_tm(n + B_OUT, c, 2 * u,
                             lambda a: pe.wait_ge(bank_free, n * TT + (N_FM * JB - 2 * TT + a + 1)),
                             mixed_parts=isinstance(n, int) and n == 0)

            out_block(0, 0)
            with pe.Fori(0, (N_OUT_BLOCKS - 2) // 2) as ii:
                out_block(ii * 2 + 1, 1)
                out_block(ii * 2 + 2, 0)
            out_block(N_OUT_BLOCKS - 1, 1)

        @block.scalar
        def _(act):
            def high(b, c):
                act.wait_ge(raw_in[c % RING], b * (16 * CH // RING) + 16 * (c // RING + 1))
                if not (isinstance(b, int) and b * CH + c < RING):
                    act.wait_ge(w_used, b * CH + (c - RING + 1))
                act.activation(w_hi[:, c % RING, :], w_raw[:, c % RING, :], ACT.Copy).then_inc(hi_ready, 1)

            def fm_wait(b, m, j):
                if j < JB - 1:
                    act.wait_ge(fm_done, m * (JB - 1) + j + 1)
                else:
                    act.wait_ge(w_used, b * CH + CH)

            def copy_cross(b, m):
                for j in range(JB):
                    fm_wait(b, m, j)
                    act.activation(cross[:, j, :], main[:, j, T:2 * T], ACT.Copy).then_inc(bank_cross, 1)

            act.dma_start(pars[:, :], par).then_inc(par_in, 16)
            act.wait_ge(consts, 2)
            act.activation(small[:, 145:146], small[:, 144:145], ACT.Copy)

            def square_half(a, h):
                for n in range(h * JB, (h + 1) * JB):
                    act.wait_ge(x_in[n], 16 * TT)
                if (a, h) != (0, 0):
                    act.wait_ge(squared, 2 * a + h)
                act.activation(scr[:, 1024:1024 + HW], x_rows[:, a, h * HW:(h + 1) * HW], ACT.Square,
                               accum_out=sumsq[:, 2 * a + h:2 * a + h + 1]).then_inc(squared, 1)

            def take_high(k):
                act.wait_ge(xt_done, k + 1)
                act.activation(acts[:, k, 0:T], side[:, k % 4, 0:T], ACT.Copy,
                               scale=col("g_pre", k)).then_inc(u_hi, 1)

            tmp = lambda n: s5tmp[:, n, :]
            act.wait_ge(par_in, 16)
            for k in range(4):
                take_high(k)
                if k < LEAD:
                    high(0, k)
            act.dma_start(wf_raw, wfg).then_inc(wf_in, 16)
            for c in range(CH):
                for k in range(KC * c + 4, min(KC * (c + 1) + 4, NK)):
                    take_high(k)
                high(0, c + LEAD)
                if c == 2:
                    act.activation(tmp(0), col("log_dt"), ACT.Exp).then_inc(pa, 1)
                    act.activation(log_a[0], col("lam"), ACT.Abs).then_inc(pa, 1)
                    act.wait_ge(pa, 2)
                    act.activation(log_a[0], log_a[0], ACT.Exp, scale=-1.0).then_inc(pa, 1)
                if c == 3:
                    act.wait_ge(wf_in, 16)
                    act.activation(wf[:, 0:NK * FT], wf_raw.rearrange("p k n -> p (k n)"),
                                   ACT.Copy).then_inc(wf_hi, 1)
                if 4 <= c < 12 and c % 2:
                    square_half((c - 5) // 4, (c - 5) // 2 % 2)
                if c == 12:
                    act.wait_ge(rms_dve, 2)
                    act.activation(rs_a[:, 0:TT], ms[:, 0:TT], ACT.Sqrt).then_inc(rms_act, 1)
                if c == 6:
                    act.wait_ge(pd, 9)
                    act.activation(tmp(4), tmp(1), ACT.Exp).then_inc(pa, 1)
                    act.activation(tmp(5), tmp(1), ACT.Tanh, scale=0.5).then_inc(pa, 1)
                if c == 8:
                    act.activation(tmp(6), tmp(3), ACT.Sin, scale=TWO_PI).then_inc(pa, 1)
                    act.activation(tmp(7), tmp(3), ACT.Sin, scale=TWO_PI / 2).then_inc(pa, 1)
                if c == CH - 1:
                    copy_cross(0, 0)

            with act.Fori(1, B_QK - B_SRC) as i:
                for c in range(CH):
                    high(i, c + LEAD)
                    if c == CH - 1:
                        copy_cross(i, i)

            act.wait_ge(fl_mm, 1)
            act.activation(fl_cross[0:FT, :], side[0:FT, 3, T:2 * T], ACT.Copy).then_inc(fl_act, 1)

            with act.Fori(0, B_V - B_QK) as i:
                for c in range(CH):
                    high(i + B_QK, c + LEAD)
                    if c == 0:
                        act.dma_start(s5_bt, bt[bass.ds(i, 1), :, :].rearrange("f p n -> (f p) n")
                                      .rearrange("p (j r s) -> p j r s", j=SJ, r=2)).then_inc(bt_in, 16)
                        act.dma_start(s5_ct, ct[bass.ds(i, 1), :, :].rearrange("f p n -> (f p) n")
                                      .rearrange("p (j r h) -> p j r h", j=SJ, r=2)).then_inc(ct_in, 16)
                    if c % 3 == 0 and c // 3 < SJ:
                        j = c // 3
                        act.wait_ge(s5_frac, i * SJ + j + 1)
                        if j >= 2:
                            act.wait_ge(s5_done, i * SJ + j - 1)
                        act.activation(s5_sin[j % 2][:, 0:T], s5_f, ACT.Sin, scale=TWO_PI).then_inc(s5_trig, 1)
                        act.activation(s5_sin[j % 2][:, T:2 * T], s5_f, ACT.Sin, scale=-TWO_PI
                                       ).then_inc(s5_trig, 1)
                        act.activation(s5_q, s5_f, ACT.Sin, scale=TWO_PI / 2).then_inc(s5_trig, 1)
                        act.wait_ge(s5_trig, i * 4 * SJ + 4 * j + 3)
                        act.activation(s5_q, s5_q, ACT.Square, scale=math.sqrt(2.0)).then_inc(s5_trig, 1)
                    if c == CH - 1:
                        copy_cross(i + B_QK, i + B_QK)

            act.wait_ge(s5_y, FT)
            for f in range(FT):
                act.activation(br[:, SSM0 + f, :], br[:, SSM0 + f, :], ACT.Gelu_apprx_tanh).then_inc(gelu_done, 1)

            with act.Fori(0, (B_G1 - B_V) // 2) as ii:
                for u in range(2):
                    i = ii * 2 + u
                    for c in range(CH):
                        high(i + B_V, c + LEAD)
                        for a, at in enumerate(LRU_AT):
                            f = i * 2 + a
                            if c == at:
                                act.dma_start(glu_w, wglu[bass.ds(f, 1), :, :].rearrange("f p n -> (f p) n")
                                              .rearrange("p (k n) -> p k n", k=FT)).then_inc(wg_in, 16)
                                act.dma_start(lru_w, wri[bass.ds(f, 1), :, :].rearrange("f p n -> (f p) n")
                                              .rearrange("p (r n) -> p r n", r=2)).then_inc(wr_in, 16)
                            if c == at + 3:
                                act.wait_ge(lru_mm, f + 1)
                                act.activation(lru_ri[:, 0:T], side[:, 0, 0:T], ACT.Sigmoid,
                                               bias=lru_now[:, B_R:B_R + 1]).then_inc(lru_act, 1)
                                act.activation(lru_ri[:, T:2 * T], side[:, 0, T:2 * T], ACT.Sigmoid,
                                               bias=lru_now[:, B_I:B_I + 1]).then_inc(lru_act, 1)
                                act.wait_ge(lru_act, i * 12 + 6 * a + 1)
                                act.activation(lru_a, lru_ri[:, 0:T], ACT.Exp,
                                               scale=lru_now[:, LOG_A:LOG_A + 1]).then_inc(lru_act, 1)
                                act.activation(lru_th, lru_ri[:, 0:T], ACT.Tanh,
                                               scale=lru_now[:, LOG_A:LOG_A + 1]).then_inc(lru_act, 1)
                                act.wait_ge(lru_act, i * 12 + 6 * a + 3)
                                act.activation(lru_s, lru_a, ACT.Square).then_inc(lru_act, 1)
                            if c == at + 5:
                                act.wait_ge(lru_v, i * 18 + 9 * a + 7)
                                act.activation(lru_s, lru_s, ACT.Sqrt, scale=-1.0).then_inc(lru_act, 1)
                                act.wait_ge(glu_mm, f + 1)
                                act.wait_ge(par_in, 16)
                                act.activation(glu_z[:, f, :], side[:, 1, 0:T], ACT.Sigmoid,
                                               bias=lru_now[:, B_GLU:B_GLU + 1]).then_inc(glu_sig, 1)
                        if c == CH - 1:
                            for a in range(TT):
                                if a < TT - 1:
                                    act.wait_ge(tm_done, i * (TT - 1) + a + 1)
                                else:
                                    act.wait_ge(w_used, (i + B_V) * CH + CH)
                                act.wait_ge(gelu_done, FT)
                                act.activation(vals[:, a, bass.ds(i * BLK, BLK)], main[:, 2 * u + a, :], ACT.Copy,
                                               scale=rstd[:, a:a + 1]).then_inc(bank_cross, 1)

            def silus(g):
                act.wait_ge(gate_normed, g + 1)
                act.activation(cross[:, :, :], cross[:, :, :], ACT.Silu).then_inc(gate_silu, 1)

            def copy_weights(h):
                act.wait_ge(at_tr, h + 1)
                act.activation(at_pt, side[:, 1, 0:3 * P], ACT.Copy).then_inc(at_ptd, 1)

            act.wait_ge(fl_dve, 3)
            act.activation(fl_e, fl_z, ACT.Abs).then_inc(fl_act, 1)
            act.wait_ge(fl_act, 2)
            act.activation(fl_e, fl_e, ACT.Exp, scale=-1.0).then_inc(fl_act, 1)
            act.wait_ge(fl_act, 3)
            act.activation(fl_e, fl_e, ACT.Ln, bias=1.0).then_inc(fl_act, 1)

            with act.Fori(0, B_G2 - B_G1) as i:
                for c in range(CH):
                    high(i + B_G1, c + LEAD)
                    for a in range(2):
                        h = i * 2 + a
                        if c == FOX_AT[a] + 1:
                            act.wait_ge(at_max, h + 1)
                            act.activation(at_p[:, 0:P], side[:, 0, 0:P], ACT.Exp, bias=row_max[:, 0:1],
                                           accum_out=row_sum[:, 0:1]).then_inc(at_exp, 1)
                            act.activation(at_p[:, P:3 * P], side[:, 0, P:3 * P], ACT.Exp, bias=row_max[:, 1:2],
                                           accum_out=row_sum[:, 1:2]).then_inc(at_exp, 1)
                        if c == FOX_AT[a] + 4:
                            copy_weights(h)
                    if c == CH - 1:
                        copy_cross(i + B_G1, i + B_V)
                        silus(i)

            def mix_high(c):
                for k in range(KC * c, KC * (c + 1)):
                    act.wait_ge(gate_used, k // JB + 1)
                    act.activation(acts[:, k, 0:T], br[:, k, :], ACT.Copy).then_inc(mix_hi, 1)

            def sb_block(i):
                for c in range(CH):
                    high(i + B_G2, c + LEAD)
                    if isinstance(i, int) and 0 < c < CH - 1:
                        act.wait_ge(w_used, (B_OUT - 1) * CH + c)
                        mix_high(c - 1)
                    for a in range(2):
                        h = i * 2 + (FT + a)
                        if c == SB_AT[a] + 1:
                            act.wait_ge(at_scores, h + 1)
                            act.activation(at_e, side[:, 0, 0:3 * P], ACT.Abs).then_inc(sb_act, 1)
                            act.wait_ge(sb_act, i * 6 + 3 * a + 1)
                            act.activation(at_e, at_e, ACT.Exp, scale=-1.0).then_inc(sb_act, 1)
                            act.wait_ge(sb_act, i * 6 + 3 * a + 2)
                            act.activation(at_e, at_e, ACT.Ln, bias=1.0).then_inc(sb_act, 1)
                        if c == SB_AT[a] + 3:
                            act.wait_ge(sb_dve, i * 8 + 4 * a + 4)
                            act.activation(at_p, at_e, ACT.Exp).then_inc(at_exp, 1)
                        if c == SB_AT[a] + 5:
                            copy_weights(h)
                    if c == CH - 1:
                        copy_cross(i + B_G2, i + (B_V + B_G2 - B_G1))
                        silus(i + (B_G2 - B_G1))

            with act.Fori(0, B_OUT - B_G2 - 1) as i:
                sb_block(i)
            sb_block(B_OUT - B_G2 - 1)

            def squares(n, u):
                for a in range(TT):
                    if a < TT - 1:
                        act.wait_ge(tm_done, n * (TT - 1) + (B_G1 - B_V) * (TT - 1) + a + 1)
                    else:
                        act.wait_ge(w_used, (n + B_OUT) * CH + CH)
                    if not (isinstance(n, int) and n == 0):
                        act.wait_ge(o_ss, n)
                    act.activation(side[:, a, :], main[:, 2 * u + a, :], ACT.Square,
                                   accum_out=ss_new[:, a:a + 1]).then_inc(o_sq, 1)

            def late_load(n, c):
                at = slice(c % FT * BLK, (c % FT + 1) * BLK)
                if n == 0 and c < FT:
                    act.wait_ge(at_o, 2 * FT)
                    act.dma_start(g_rows[:, at], gpost[at].partition_broadcast(P)).then_inc(g_in, 16)
                elif n == 0 or c < FT:
                    a = 0 if n == 0 else 1
                    act.wait_ge(at_o, 2 * FT)
                    act.dma_start(x_late[a][:, at], x[a * P:(a + 1) * P, at]).then_inc(xl_in[a], 16)

            def out_block(n, u):
                for c in range(CH):
                    if not (isinstance(n, int) and n == N_OUT_BLOCKS - 1 and c + LEAD >= CH):
                        high(n + B_OUT, c + LEAD)
                    if isinstance(n, int) and n == 0 and c < 2:
                        mix_high(c + CH - 2)
                    if isinstance(n, int):
                        late_load(n, c)
                    if isinstance(n, int) and n == N_OUT_BLOCKS - 1 and c == CH - LEAD:
                        act.activation(small[:, 146:147], later[:, 0:1], ACT.Sqrt)
                    if c == CH - 1:
                        squares(n, u)

            out_block(0, 0)
            with act.Fori(0, (N_OUT_BLOCKS - 2) // 2) as ii:
                out_block(ii * 2 + 1, 1)
                out_block(ii * 2 + 2, 0)
            out_block(N_OUT_BLOCKS - 1, 1)
            act.wait_ge(fin_dve, 1)
            act.activation(rs_a[:, 0:TT], ms[:, 0:TT], ACT.Sqrt).then_inc(fin_act, 1)

        @block.vector
        def _(dve):
            def low(b, c):
                dve.wait_ge(hi_ready, b * CH + c + 1)
                if not (isinstance(b, int) and b * CH + c < RING):
                    dve.wait_ge(w_used, b * CH + (c - RING + 1))
                dve.tensor_tensor(w_lo[:, c % RING, :], w_raw[:, c % RING, :],
                                  w_hi[:, c % RING, :].bitcast(F32), ALU.subtract).then_inc(lo_ready, 1)

            tmp = lambda n: s5tmp[:, n, :]
            kind = lambda n: s5par[:, :, n * SJ:(n + 1) * SJ]
            by_tile = lambda ap: ap.rearrange("p (f j) -> p f j", f=FT)
            are, aim = col("a_re"), col("a_im")
            n_pd = 0

            def stepped(instruction):
                nonlocal n_pd
                instruction.then_inc(pd, 1)
                n_pd += 1
                return n_pd

            def s5_angles():
                dve.wait_ge(pa, 1)
                dve.wait_ge(par_in, 16)
                stepped(dve.tensor_tensor(tmp(1), are, tmp(0), ALU.mult))
                y = stepped(dve.tensor_tensor(tmp(2), aim, tmp(0), ALU.mult))
                dve.wait_ge(pd, y)
                y = stepped(dve.tensor_scalar(tmp(8), tmp(2), 1.0 / (2 * math.pi), ROUND, ALU.mult, ALU.add))
                dve.wait_ge(pd, y)
                y = stepped(dve.tensor_scalar(tmp(9), tmp(8), -ROUND, None, ALU.add))
                dve.wait_ge(pd, y)
                y = stepped(dve.scalar_tensor_tensor(tmp(10), tmp(9), -PI_1, tmp(2), ALU.mult, ALU.add))
                dve.wait_ge(pd, y)
                y = stepped(dve.scalar_tensor_tensor(tmp(11), tmp(9), -PI_2, tmp(10), ALU.mult, ALU.add))
                dve.wait_ge(pd, y)
                y = stepped(dve.scalar_tensor_tensor(tmp(12), tmp(9), -PI_3, tmp(11), ALU.mult, ALU.add))
                dve.wait_ge(pd, y)
                y = stepped(dve.tensor_scalar(tmp(13), tmp(12), 1.0 / (2 * math.pi), 0.5, ALU.mult, ALU.min))
                dve.wait_ge(pd, y)
                y = stepped(dve.tensor_scalar(tmp(3), tmp(13), -0.5, None, ALU.max))
                dve.wait_ge(pd, y)
                stepped(dve.tensor_scalar(kind(0), by_tile(tmp(3)), 1.0, None, ALU.mult))

            def s5_expm1():
                dve.wait_ge(pa, 7)
                stepped(dve.tensor_scalar(kind(1), by_tile(tmp(4)), 1.0, None, ALU.mult))
                em = stepped(dve.scalar_tensor_tensor(tmp(8), tmp(4), 1.0, tmp(5), ALU.add, ALU.mult))
                sh = stepped(dve.tensor_tensor(tmp(9), tmp(7), tmp(7), ALU.mult))
                stepped(dve.tensor_tensor(tmp(10), tmp(4), tmp(6), ALU.mult))
                stepped(dve.tensor_tensor(tmp(11), are, are, ALU.mult))
                a2 = stepped(dve.tensor_tensor(tmp(12), aim, aim, ALU.mult))
                dve.wait_ge(pd, a2)
                y = stepped(dve.tensor_scalar(tmp(9), tmp(9), -2.0, None, ALU.mult))
                stepped(dve.tensor_tensor(tmp(13), tmp(11), tmp(12), ALU.add))
                dve.wait_ge(pd, y)
                y = stepped(dve.tensor_tensor(tmp(14), tmp(8), tmp(9), ALU.mult))
                dve.wait_ge(pd, y)
                stepped(dve.tensor_tensor(tmp(15), tmp(14), tmp(8), ALU.add))
                stepped(dve.reciprocal(tmp(16), tmp(13)))

            def s5_factors():
                dve.wait_ge(pd, n_pd)
                y = stepped(dve.tensor_tensor(tmp(14), tmp(15), tmp(9), ALU.add))
                dve.wait_ge(pd, y)
                stepped(dve.tensor_tensor(tmp(11), tmp(14), are, ALU.mult))
                stepped(dve.tensor_tensor(tmp(12), tmp(10), aim, ALU.mult))
                stepped(dve.tensor_tensor(tmp(13), tmp(10), are, ALU.mult))
                y = stepped(dve.tensor_tensor(tmp(15), tmp(14), aim, ALU.mult))
                dve.wait_ge(pd, y)
                stepped(dve.tensor_tensor(tmp(11), tmp(11), tmp(12), ALU.add))
                y = stepped(dve.tensor_tensor(tmp(13), tmp(15), tmp(13), ALU.subtract))
                dve.wait_ge(pd, y)
                y = stepped(dve.tensor_tensor(kind(2), by_tile(tmp(11)), by_tile(tmp(16)), ALU.mult))
                stepped(dve.tensor_tensor(kind(4), by_tile(tmp(13)), by_tile(tmp(16)), ALU.mult))
                dve.wait_ge(pd, y)
                stepped(dve.tensor_scalar(kind(3), kind(2), -1.0, None, ALU.mult))

            def lru_series():
                e, s, s2, q = log_a
                dve.wait_ge(pa, 3)
                y = stepped(dve.tensor_scalar(s, e, 2.0, None, ALU.add))
                dve.wait_ge(pd, y)
                y = stepped(dve.reciprocal(s2, s))
                dve.wait_ge(pd, y)
                y = stepped(dve.tensor_tensor(s, e, s2, ALU.mult))
                dve.wait_ge(pd, y)
                y = stepped(dve.tensor_tensor(s2, s, s, ALU.mult))
                dve.wait_ge(pd, y)
                y = stepped(dve.tensor_scalar(q, s2, 1.0 / 17, None, ALU.mult))
                for n in range(15, 7, -2):
                    dve.wait_ge(pd, y)
                    y = stepped(dve.scalar_tensor_tensor(q, q, 1.0 / n, s2, ALU.add, ALU.mult))

            def lru_decays():
                e, s, s2, q = log_a
                for n in range(7, 1, -2):
                    dve.wait_ge(pd, n_pd)
                    stepped(dve.scalar_tensor_tensor(q, q, 1.0 / n, s2, ALU.add, ALU.mult))
                dve.wait_ge(pd, n_pd)
                y = stepped(dve.scalar_tensor_tensor(q, q, 1.0, s, ALU.add, ALU.mult))
                y = stepped(dve.tensor_scalar(e, col("lam"), 0.0, LRU_C, ALU.min, ALU.mult))
                dve.wait_ge(pd, y)
                y = stepped(dve.scalar_tensor_tensor(lru_par[:, :, LOG_A:LOG_A + 1].rearrange("p f n -> p (f n)"),
                                                     q, -2.0 * LRU_C, e, ALU.mult, ALU.add))

            def root(step, first, cols):
                z = lambda ap: ap[:, cols]
                dve.reciprocal(z(rs_b), z(rs_a)).then_inc(step, 1)
                dve.wait_ge(step, first + 1)
                dve.tensor_tensor(z(rs_a), z(rs_b), z(rs_b), ALU.mult).then_inc(step, 1)
                dve.wait_ge(step, first + 2)
                dve.tensor_tensor(z(rs_a), z(rs_a), z(ms), ALU.mult).then_inc(step, 1)
                dve.wait_ge(step, first + 3)
                dve.tensor_scalar(z(rs_a), z(rs_a), -0.5, 1.5, ALU.mult, ALU.add).then_inc(step, 1)
                dve.wait_ge(step, first + 4)
                dve.tensor_tensor(z(rstd), z(rs_a), z(rs_b), ALU.mult).then_inc(step, 1)
                dve.wait_ge(step, first + 5)

            def norm_sums():
                dve.wait_ge(squared, 2 * TT)
                sq = sumsq.rearrange("p (a h) -> p h a", h=2)
                dve.tensor_tensor(ms[:, 0:TT], sq[:, 0, :], sq[:, 1, :], ALU.add).then_inc(rms_dve, 1)
                dve.wait_ge(rms_dve, 1)
                dve.tensor_scalar(ms[:, 0:TT], ms[:, 0:TT], 1.0 / D, EPS, ALU.mult, ALU.add).then_inc(rms_dve, 1)

            def norm_root():
                dve.wait_ge(rms_act, 1)
                root(rms_dve, 2, slice(0, TT))
                for a in range(TT):
                    dve.tensor_scalar(rs_diag[:, a * P:(a + 1) * P], ident[:, :], rstd[:, a:a + 1], None,
                                      ALU.mult).then_inc(rms_dve, 1)

            def take_low(k):
                dve.wait_ge(u_hi, k + 1)
                dve.scalar_tensor_tensor(acts[:, k, T:2 * T], side[:, k % 4, 0:T], col("g_pre", k),
                                         acts[:, k, 0:T].bitcast(F32), ALU.mult, ALU.subtract).then_inc(u_lo, 1)

            def sum_banks(i):
                for j in range(JB):
                    dve.wait_ge(bank_cross, i * JB + (j + 1))
                    dve.tensor_tensor(cross[:, j, :], main[:, j, 0:T], cross[:, j, :],
                                      ALU.add).then_inc(bank_free, 1)

            def source_tiles(i):
                sum_banks(i)
                dve.wait_ge(bank_free, i * JB + JB)
                dve.tensor_tensor(br[:, bass.ds(i * JB, JB), :], cross[:, :, :], rs_banks,
                                  ALU.mult).then_inc(br_ready, 1)

            dve.wait_ge(par_in, 16)
            for k in range(4):
                take_low(k)
                if k < LEAD:
                    low(0, k)
            for c in range(CH):
                for k in range(KC * c + 4, min(KC * (c + 1) + 4, NK)):
                    take_low(k)
                low(0, c + LEAD)
                if c == 3:
                    dve.memset(wf[:, 2 * NK * FT:2 * NK * FT + P].bitcast(F32), 0.0).then_inc(wf_lo0, 1)
                    dve.wait_ge(wf_hi, 1)
                    dve.tensor_tensor(wf[:, NK * FT:2 * NK * FT], wf_raw.rearrange("p k n -> p (k n)"),
                                      wf[:, 0:NK * FT].bitcast(F32), ALU.subtract).then_inc(wf_lo, 1)
                if c == 4:
                    s5_angles()
                if c == 5:
                    lru_series()
                if c == 7:
                    lru_decays()
                if c == 9:
                    s5_expm1()
                if c == 10:
                    s5_factors()
                if c == 12:
                    norm_sums()
                if c == 13:
                    norm_root()
                if c == CH - 2:
                    dve.wait_ge(rs_mm, 1)
                    dve.tensor_scalar(rs_row, side[:, 0, 0:T], 1.0, None, ALU.mult).then_inc(rs_ready, 1)
                if c == CH - 1:
                    dve.wait_ge(rs_ready, 1)
                    source_tiles(0)
            with dve.Fori(1, B_QK - B_SRC) as i:
                for c in range(CH):
                    if c == CH - 1:
                        source_tiles(i)
                    low(i, c + LEAD)

            dve.wait_ge(fl_act, 1)
            dve.tensor_tensor(fl_rows[0:FT, :], side[0:FT, 3, 0:T], fl_cross[0:FT, :], ALU.add).then_inc(fl_dve, 1)

            wide = lambda ap: ap.rearrange("p (r t) -> p r t", r=2)
            both = lambda ap: ap.unsqueeze(1).to_broadcast([P, 2, T])
            with dve.Fori(0, B_V - B_QK) as i:
                for c in range(CH):
                    if c == CH - 1:
                        sum_banks(i + B_QK)
                    low(i + B_QK, c + LEAD)
                    if c == 0:
                        dve.wait_ge(lo_ready, (i + B_QK) * CH + (LEAD + 1))
                        dve.tensor_scalar(s5_now, s5par[:, i, :], 1.0, None, ALU.mult).then_inc(p5_ready, 1)
                        dve.tensor_scalar(s5_u, br[:, SSM0 + i, :], 1.0, None, ALU.mult).then_inc(su_ready, 1)
                    if c >= 2 and (c - 2) // 3 < SJ:
                        j, part = (c - 2) // 3, (c - 2) % 3
                        g, done = i * SJ + j, i * (7 * SJ) + 7 * j
                        sin, cos, hs = s5_sin[j % 2], s5_cos[j % 2], s5_h[j % 2]
                        bu = side[:, j % 2, :]
                        if part == 0:
                            dve.wait_ge(s5_bmm, g + 1)
                            dve.wait_ge(s5_cosd, g + 1)
                            if j:
                                dve.wait_ge(s5_done, g)
                            dve.tensor_tensor(wide(s5_m1), wide(bu), both(cos), ALU.mult).then_inc(s5_dve, 1)
                            dve.tensor_tensor(wide(s5_m2), wide(bu)[:, ::-1, :], wide(sin),
                                              ALU.mult).then_inc(s5_dve, 1)
                            dve.wait_ge(s5_dve, done + 2)
                            dve.tensor_tensor(s5_m1, s5_m1, s5_m2, ALU.add).then_inc(s5_dve, 1)
                        if part == 1:
                            radius = s5_now[:, SJ + j:SJ + j + 1].to_broadcast([P, T])
                            dve.wait_ge(p5_ready, i + 1)
                            dve.wait_ge(s5_dve, done + 3)
                            for r in range(2):
                                dve.tensor_tensor_scan(s5_g[:, r * T:(r + 1) * T], radius,
                                                       s5_m1[:, r * T:(r + 1) * T], 0.0,
                                                       ALU.mult, ALU.add).then_inc(s5_dve, 1)
                        if part == 2:
                            dve.wait_ge(s5_dve, done + 5)
                            dve.tensor_tensor(wide(s5_m1), wide(s5_g), both(cos), ALU.mult).then_inc(s5_dve, 1)
                            dve.tensor_tensor(wide(s5_m2), wide(s5_g)[:, ::-1, :], wide(sin),
                                              ALU.mult).then_inc(s5_dve, 1)
                            dve.wait_ge(s5_dve, done + 7)
                            if j >= 2:
                                dve.wait_ge(s5_cmm, i * SJ + j - 1)
                            dve.tensor_tensor(hs, s5_m1, s5_m2, ALU.subtract).then_inc(s5_done, 1)
                    if c == CH - 1:
                        dve.wait_ge(s5_cmm, i * SJ + SJ)
                        dve.scalar_tensor_tensor(br[:, SSM0 + i, :], s5_u,
                                                 pars[:, bass.ds(i + PC["ssm_d"][0], 1)],
                                                 side[:, 2, 0:T], ALU.mult, ALU.add).then_inc(s5_y, 1)
                        dve.wait_ge(bank_free, i * JB + (B_QK + 1) * JB)
                        dve.scalar_tensor_tensor(br[:, bass.ds(i * JB + FOX0, JB), :], cross[:, :, :], QK_SCALE,
                                                 rs_banks, ALU.mult, ALU.mult).then_inc(br_ready, 1)

            dve.wait_ge(gelu_done, FT)
            dve.wait_ge(fl_mm, 2)
            for a in range(TT):
                dve.scalar_tensor_tensor(fl_z[:, a, :], side[:, 3, a * FT:(a + 1) * FT], rstd[:, a:a + 1],
                                         col("b_forget")[:, a * FT:(a + 1) * FT], ALU.mult,
                                         ALU.add).then_inc(fl_dve, 1)
            with dve.Fori(0, B_G1 - B_V) as i:
                for c in range(CH):
                    low(i + B_V, c + LEAD)
                    for a, at in enumerate(LRU_AT):
                        f, done = i * 2 + a, i * 18 + 9 * a
                        now = lambda n: lru_now[:, n:n + 1]
                        if c == at:
                            dve.wait_ge(lo_ready, (i + B_V) * CH + (at + LEAD + 1))
                            dve.tensor_scalar(lru_now, lru_par[:, f, :], 1.0, None, ALU.mult).then_inc(lru_v, 1)
                            dve.tensor_scalar(lru_x, br[:, LRU0 + f, :], 1.0, None, ALU.mult).then_inc(lru_v, 1)
                            dve.wait_ge(lru_v, done + 2)
                            dve.tensor_scalar(lru_xc, lru_x, now(TAP0 + 3), now(CONV_B), ALU.mult,
                                              ALU.add).then_inc(lru_v, 1)
                            for s in range(1, 4):
                                dve.wait_ge(lru_v, done + 2 + s)
                                dve.scalar_tensor_tensor(lru_xc[:, s:T], lru_x[:, 0:T - s], now(TAP0 + 3 - s),
                                                         lru_xc[:, s:T], ALU.mult, ALU.add).then_inc(lru_v, 1)
                        if c == at + 4:
                            dve.wait_ge(lru_act, i * 12 + 6 * a + 5)
                            dve.scalar_tensor_tensor(lru_s, lru_s, 1.0, lru_th, ALU.add,
                                                     ALU.mult).then_inc(lru_v, 1)
                        if c == at + 6:
                            dve.wait_ge(lru_act, i * 12 + 6 * a + 6)
                            dve.tensor_tensor(lru_x, lru_ri[:, T:2 * T], lru_xc, ALU.mult).then_inc(lru_v, 1)
                            dve.wait_ge(lru_v, done + 8)
                            dve.tensor_tensor(lru_x, lru_x, lru_s, ALU.mult).then_inc(lru_v, 1)
                            dve.wait_ge(lru_v, done + 9)
                            dve.tensor_tensor_scan(br[:, LRU0 + f, :], lru_a, lru_x, 0.0, ALU.mult,
                                                   ALU.add).then_inc(lru_done, 1)
            dve.wait_ge(glu_sig, FT)
            dve.tensor_tensor(br[:, SSM0:SSM0 + FT, :], br[:, SSM0:SSM0 + FT, :], glu_z,
                              ALU.mult).then_inc(glu_applied, 1)

            def gates(i, g, b, tile0):
                for j in range(JB):
                    dve.wait_ge(bank_cross, g * JB + (V_READ + j + 1))
                    dve.tensor_tensor(cross[:, j, :], main[:, j, 0:T], cross[:, j, :],
                                      ALU.add).then_inc(bank_free, 1)
                dve.wait_ge(bank_free, g * JB + (B_V + 1) * JB)
                dve.tensor_tensor(cross[:, :, :], cross[:, :, :], rs_banks, ALU.mult).then_inc(gate_normed, 1)
                low(b, CH - 1 + LEAD)
                dve.wait_ge(glu_applied, 1)
                dve.wait_ge(gate_silu, g + 1)
                tiles = br[:, bass.ds(i * JB + tile0, JB), :]
                dve.tensor_tensor(tiles, tiles, cross[:, :, :], ALU.mult).then_inc(gate_used, 1)

            def head_out(h):
                dve.wait_ge(at_out, h + 1)
                dve.tensor_scalar(br[:, FOX0 + h, :], side[:, 2, 0:T], 1.0, None, ALU.mult).then_inc(at_o, 1)

            dve.wait_ge(fl_act, 4)
            dve.wait_ge(fl_dve, 3)
            dve.wait_ge(glu_applied, 1)
            dve.scalar_tensor_tensor(logf[:, :, :].rearrange("p h a -> p a h"), fl_z, 0.0, fl_e,
                                     ALU.min, ALU.subtract).then_inc(fl_dve, 1)
            with dve.Fori(0, B_G2 - B_G1) as i:
                for c in range(CH):
                    if c < CH - 1:
                        low(i + B_G1, c + LEAD)
                    if c == 0:
                        dve.wait_ge(fl_dve, 4)
                        dve.tensor_scalar(lf_now.rearrange("p (h a) -> p h a", h=2),
                                          logf[:, bass.ds(i * 2, 2), :], 1.0, None,
                                          ALU.mult).then_inc(lf_ready, 1)
                    for a in range(2):
                        h = i * 2 + a
                        if c == FOX_AT[a] + 1:
                            dve.wait_ge(at_scores, h + 1)
                            dve.tensor_reduce(row_max[:, 0:1], side[:, 0, 0:P], AX.X, ALU.max, negate=True)
                            dve.tensor_reduce(row_max[:, 1:2], side[:, 0, P:3 * P], AX.X, ALU.max,
                                              negate=True).then_inc(at_max, 1)
                        if c == FOX_AT[a] + 2:
                            dve.wait_ge(at_exp, i * 4 + 2 * a + 2)
                            dve.reciprocal(row_inv, row_sum).then_inc(at_inv, 1)
                            dve.wait_ge(at_inv, h + 1)
                            dve.tensor_scalar(at_p[:, 0:P], at_p[:, 0:P], row_inv[:, 0:1], None,
                                              ALU.mult).then_inc(at_norm, 1)
                            dve.tensor_scalar(at_p[:, P:3 * P], at_p[:, P:3 * P], row_inv[:, 1:2], None,
                                              ALU.mult).then_inc(at_norm, 1)
                        if c == FOX_AT[a] + 6:
                            head_out(h)
                    if c == CH - 1:
                        gates(i, i, i + B_G1, SSM0)

            def mix_low(c):
                for k in range(KC * c, KC * (c + 1)):
                    dve.wait_ge(mix_hi, k + 1)
                    dve.tensor_tensor(acts[:, k, T:2 * T], br[:, k, :], acts[:, k, 0:T].bitcast(F32),
                                      ALU.subtract).then_inc(mix_lo, 1)

            def sb_block(i):
                for c in range(CH):
                    if c < CH - 1:
                        low(i + B_G2, c + LEAD)
                    if isinstance(i, int) and 0 < c < CH - 1:
                        mix_low(c - 1)
                    for a in range(2):
                        h, done = i * 2 + (FT + a), i * 8 + 4 * a
                        if c == SB_AT[a] + 2:
                            dve.wait_ge(sb_act, i * 6 + 3 * a + 3)
                            dve.scalar_tensor_tensor(at_sp, side[:, 0, 0:3 * P], 0.0, at_e, ALU.max,
                                                     ALU.add).then_inc(sb_dve, 1)
                            dve.wait_ge(sb_dve, done + 1)
                            dve.tensor_tensor_scan(at_r[:, 0:P][:, ::-1], ones[:, 0:P],
                                                   at_sp[:, 0:P][:, ::-1], 0.0, ALU.mult,
                                                   ALU.add).then_inc(sb_dve, 1)
                            dve.tensor_tensor_scan(at_r[:, P:3 * P][:, ::-1], ones,
                                                   at_sp[:, P:3 * P][:, ::-1], 0.0, ALU.mult,
                                                   ALU.add).then_inc(sb_dve, 1)
                            dve.wait_ge(sb_dve, done + 3)
                            dve.tensor_tensor(at_e, side[:, 0, 0:3 * P], at_r, ALU.subtract).then_inc(sb_dve, 1)
                        if c == SB_AT[a] + 8:
                            head_out(h)
                    if c == CH - 1:
                        gates(i, i + (B_G2 - B_G1), i + B_G2, FOX0)

            with dve.Fori(0, B_OUT - B_G2 - 1) as i:
                sb_block(i)
            sb_block(B_OUT - B_G2 - 1)

            def weigh(n, u):
                for a in range(TT):
                    dve.wait_ge(o_sq, n * TT + a + 1)
                    dve.wait_ge(g_in, 16 * FT)
                    dve.tensor_tensor(mixed[:, a, bass.ds(n * BLK, BLK)], main[:, 2 * u + a, :],
                                      g_rows[:, bass.ds(n * BLK, BLK)], ALU.mult).then_inc(bank_free, 1)
                if not (isinstance(n, int) and n == 0):
                    dve.wait_ge(o_ss, n)
                    dve.tensor_tensor(ss_all, ss_all, ss_new, ALU.add).then_inc(o_ss, 1)
                else:
                    dve.tensor_copy(ss_all, ss_new).then_inc(o_ss, 1)

            def out_block(n, u):
                for c in range(CH):
                    if not (isinstance(n, int) and n == N_OUT_BLOCKS - 1 and c + LEAD >= CH):
                        low(n + B_OUT, c + LEAD)
                    if isinstance(n, int) and n == 0 and c < 2:
                        mix_low(c + CH - 2)
                    if c == CH - 1:
                        weigh(n, u)

            out_block(0, 0)
            with dve.Fori(0, (N_OUT_BLOCKS - 2) // 2) as ii:
                out_block(ii * 2 + 1, 1)
                out_block(ii * 2 + 2, 0)
            out_block(N_OUT_BLOCKS - 1, 1)
            dve.wait_ge(o_ss, N_OUT_BLOCKS)
            dve.tensor_scalar(ms[:, 0:TT], ss_all, 1.0 / D, EPS, ALU.mult, ALU.add).then_inc(fin_dve, 1)
            dve.wait_ge(fin_act, 1)
            dve.wait_ge(fin_dve, 1)
            root(fin_dve, 1, slice(0, TT))
            dve.wait_ge(bank_free, N_FM * JB + N_OUT_BLOCKS * TT)
            for a, q in quarters:
                part = mixed[:, a, q * QW:(q + 1) * QW]
                dve.wait_ge(xl_in[a], 16 * FT)
                dve.scalar_tensor_tensor(part, part, rstd[:, a:a + 1], x_late[a][:, q * QW:(q + 1) * QW],
                                         ALU.mult, ALU.add).then_inc(fin_sum, 1)

        @block.gpsimd
        def _(pool):
            pool.iota(steps_t, pattern=[[1, T]], base=0, channel_multiplier=0,
                      allow_small_or_imprecise_dtypes=True).then_inc(consts, 1)
            pool.memset(small[:, 144:145], ROUND).then_inc(consts, 1)
            pool.memset(later[:, :], 1.0).then_inc(const_steps, 1)
            pool.memset(upto[:, :], 1.0).then_inc(const_steps, 1)
            pool.memset(ident[:, :], 0.0).then_inc(const_steps, 1)
            pool.memset(ident_b[:, :], 0.0).then_inc(const_steps, 1)
            pool.memset(causal_b[:, :], 0.0).then_inc(const_steps, 1)
            pool.memset(strict_b[:, :], 0.0).then_inc(const_steps, 1)
            pool.wait_ge(const_steps, 6)

            def choose(t, op, fill, sign):
                pool.affine_select(out=t, in_=t, compare_op=op, fill=fill, base=0,
                                   pattern=[[-sign, P]], channel_multiplier=sign).then_inc(consts, 1)

            choose(later[:, P:2 * P], ALU.is_gt, 0.0, 1)
            choose(upto[:, :], ALU.is_ge, 0.0, -1)
            choose(ident[:, :], ALU.not_equal, 1.0, 1)
            choose(ident_b[:, :], ALU.not_equal, 1.0, 1)
            choose(causal_b[:, :], ALU.is_ge, NEG, 1)
            choose(strict_b[:, :], ALU.is_gt, NEG, 1)

            pool.wait_ge(consts, N_CONST)
            rounder = small[:, 144:145].to_broadcast([P, T])
            with pool.Fori(0, B_V - B_QK) as i:
                def fraction(j):
                    g, tab = i * SJ + j, i * (3 * SJ) + 3 * j
                    pool.wait_ge(p5_ready, i + 1)
                    pool.tensor_tensor(s5_a, steps_t, s5_now[:, j:j + 1].to_broadcast([P, T]),
                                       ALU.mult).then_inc(s5_tab, 1)
                    pool.wait_ge(s5_tab, tab + 1)
                    pool.tensor_tensor(s5_k, s5_a, rounder, ALU.add).then_inc(s5_tab, 1)
                    pool.wait_ge(s5_tab, tab + 2)
                    pool.tensor_tensor(s5_k, s5_k, rounder, ALU.subtract).then_inc(s5_tab, 1)
                    pool.wait_ge(s5_tab, tab + 3)
                    pool.tensor_tensor(s5_f, s5_a, s5_k, ALU.subtract).then_inc(s5_frac, 1)

                def cosine(j):
                    pool.wait_ge(s5_trig, i * (4 * SJ) + 4 * j + 4)
                    if j >= 2:
                        pool.wait_ge(s5_done, i * SJ + j - 1)
                    pool.tensor_tensor(s5_cos[j % 2], ones, s5_q, ALU.subtract).then_inc(s5_cosd, 1)

                fraction(0)
                now = lambda n: s5_now[:, n * SJ:(n + 1) * SJ].unsqueeze(2).to_broadcast([P, SJ, 2 * HG])
                pool.wait_ge(ct_in, i * 16 + 16)
                c_re, c_im = s5_ct[:, :, 0, :], s5_ct[:, :, 1, :]
                for n, (part, factor) in enumerate(((c_re, 2), (c_im, 4), (c_re, 4), (c_im, 3))):
                    pool.tensor_tensor(s5_c[n], part, now(factor), ALU.mult).then_inc(s5_cq, 1)
                pool.wait_ge(s5_cq, i * 5 + 4)
                pool.tensor_tensor(s5_cp[:, :, 0, :], s5_c[0], s5_c[1], ALU.add).then_inc(s5_cq, 1)
                pool.wait_ge(s5_cq, i * 5 + 5)
                pool.tensor_tensor(s5_cp[:, :, 1, :], s5_c[2], s5_c[3], ALU.add).then_inc(s5_cprime, 1)
                for j in range(SJ):
                    cosine(j)
                    if j + 1 < SJ:
                        fraction(j + 1)

            def fetch_queries(h):
                pool.wait_ge(glu_applied, 1)
                pool.tensor_copy(at_q, br[:, FOX0 + h, :]).then_inc(qs_ready, 1)

            def fetch_values(h):
                pool.wait_ge(bank_cross, V_READ)
                pool.tensor_copy(at_v, vals[:, :, bass.ds(h * P, P)]).then_inc(vs_ready, 1)

            with pool.Fori(0, B_G2 - B_G1) as i:
                for a in range(2):
                    h = i * 2 + a
                    if a:
                        pool.wait_ge(at_scores, h)
                    else:
                        pool.wait_ge(lf_ready, i + 1)
                    fetch_queries(h)
                    for n, (mask, tile) in enumerate(((upto[:, :], 0), (later[:, 0:P], 0), (upto[:, :], 1))):
                        pool.wait_ge(lf_ready, i + 1)
                        if a:
                            pool.wait_ge(at_scores, h)
                        log_f = lf_now[:, 2 * a + tile:2 * a + tile + 1].to_broadcast([P, P])
                        dec = pool.tensor_tensor(at_dec[:, n, :], mask, log_f, ALU.mult)
                    dec.then_inc(dec_ready, 1)
                    if a:
                        pool.wait_ge(at_out, h)
                    fetch_values(h)
            with pool.Fori(0, B_OUT - B_G2) as i:
                for a in range(2):
                    h = i * 2 + (FT + a)
                    pool.wait_ge(at_scores, h)
                    fetch_queries(h)
                    pool.wait_ge(at_out, h)
                    fetch_values(h)


def _lay_out(v):
    import numpy as np

    f32 = np.float32
    sizes = [BW] * 4 + [FT] + [BW] * 8
    at = np.cumsum([0] + sizes)
    names = ["fq", "fk", "fv", "fg", "fl", "sq", "sk", "sv", "sg", "su", "ug", "lx", "lg"]
    where = {n: int(a) for n, a in zip(names, at)}
    w_in, w_out = v["w_in"][0], v["w_out"][0]

    wall = np.empty((N_BLOCKS, P, NK, BLK), f32)
    order = ["su", "lx", "fq", "sq", "fk", "sk", "fv", "sv", "ug", "lg", "fg", "sg"]
    for n, name in enumerate(order):
        for half in range(BW // BLK):
            a = where[name] + half * BLK
            wall[n * (BW // BLK) + half] = w_in[:, a:a + BLK].reshape(NK, P, BLK).transpose(1, 0, 2)
    rows = np.concatenate([w_out[2 * BW:4 * BW], w_out[0:2 * BW]], axis=0)
    for n in range(N_OUT_BLOCKS):
        wall[N_IN_BLOCKS + n] = rows[:, n * BLK:(n + 1) * BLK].reshape(NK, P, BLK).transpose(1, 0, 2)
    wfg = w_in[:, where["fl"]:where["fl"] + FT].reshape(NK, P, FT).transpose(1, 0, 2)

    by_state = lambda a: a.reshape(BW // HG // 2, 2, STATE).transpose(1, 2, 0).reshape(P, -1)
    by_feature = lambda a: a.reshape(-1, P).T
    par = np.zeros((P, NPAR), f32)

    def put(name, a):
        par[:, PC[name][0]:PC[name][1]] = a

    put("g_pre", by_feature(v["g_pre"][0]))
    put("a_re", by_state(v["ssm_a_re"][0]))
    put("a_im", by_state(v["ssm_a_im"][0]))
    put("log_dt", by_state(np.repeat(v["ssm_log_dt"][0][:, None], STATE, axis=1)))
    put("b_forget", np.broadcast_to(np.tile(v["b_forget"][0], TT), (P, TT * FT)))
    put("ssm_d", by_feature(v["ssm_d"][0]))
    put("lam", by_feature(v["lru_lambda"][0]))
    lru = np.zeros((P, FT, 9), f32)
    for n in range(4):
        lru[:, :, TAP0 + n] = by_feature(v["conv_w"][0][n])
    for n, name in ((CONV_B, "conv_b"), (B_R, "b_rgate"), (B_I, "b_igate"), (B_GLU, "b_glu")):
        lru[:, :, n] = by_feature(v[name][0])
    put("lru", lru.reshape(P, FT * 9))

    bt = np.zeros((FT, P, SJ, 2, P), f32)
    ct = np.zeros((FT, P, SJ, 2, 2 * HG), f32)
    for r, (b, c) in enumerate((("ssm_b_re", "ssm_c_re"), ("ssm_b_im", "ssm_c_im"))):
        for f in range(FT):
            for j in range(SJ):
                for a in range(2):
                    g = f * 2 * SJ + 2 * j + a
                    row = 2 * HG * j + HG * a
                    bt[f, row:row + HG, j, r, a * STATE:(a + 1) * STATE] = v[b][0][g].T
                    ct[f, a * STATE:(a + 1) * STATE, j, r, a * HG:(a + 1) * HG] = v[c][0][g].T
    wglu = v["w_glu"][0].reshape(FT, P, FT, P).transpose(2, 1, 0, 3)
    wri = np.zeros((FT, P, 2, P), f32)
    half = P // 2
    for r, name in enumerate(("w_rgate", "w_igate")):
        for n in range(2 * FT):
            a = (n % 2) * half
            wri[n // 2, a:a + half, r, a:a + half] = v[name][0][n]
    whole = np.ascontiguousarray
    return {"x": whole(v["x"][0]), "par": par, "bt": bt.reshape(FT, P, -1), "ct": ct.reshape(FT, P, -1),
            "wfg": whole(wfg), "wglu": whole(wglu).reshape(FT, P, -1), "wri": wri.reshape(FT, P, -1),
            "gpost": whole(v["g_post"][0]), "wall": wall.reshape(N_BLOCKS, P, NK * BLK)}


def kernel(**inputs):
    import numpy as np
    import concourse.bacc as bacc
    from concourse.bass_utils import run_bass_kernel_spmd

    arrays = _lay_out({n: np.asarray(a) for n, a in inputs.items()})
    nc = bacc.Bacc("TRN2", target_bir_lowering=False, num_devices=1)
    args = [nc.dram_tensor(f"in_{n}", a.shape, mybir.dt.from_np(a.dtype), kind="ExternalInput").ap()
            for n, a in arrays.items()]
    out = nc.dram_tensor("out_0", (T, D), F32, kind="ExternalOutput").ap()
    hybrid_trunk(nc, *args, out)
    r = run_bass_kernel_spmd(nc, [{f"in_{n}": a for n, a in arrays.items()}], core_ids=[0])
    return r.results[0]["out_0"].reshape(1, T, D)
```
